# Optimizing a Trainium2 kernel written in Bass

```python
import math
import jax, jax.numpy as jnp
from jax import lax
import numpy as np
import jax
import jax.numpy as jnp

D_MODEL = 1024
BATCH = 1
SEQ = 512
DEPTH = 2

ATT_HEADS = 8
ATT_HEAD_DIM = 64
ATT_WIDTH = ATT_HEADS * ATT_HEAD_DIM
DILATED_PATTERNS = ((128, 1), (512, 4), (2048, 16))
ATT_BLOCK = 128
ROPE_THETA = 500000.0
ROPE_DIM = ATT_HEAD_DIM // 4

MLSTM_HEADS = 4
MLSTM_HEAD_DIM = 128
MLSTM_WIDTH = MLSTM_HEADS * MLSTM_HEAD_DIM
MLSTM_CHUNK = 64
CONV_WIDTH = 4
FORGET_BIAS = 3.0

D_FF = 4 * D_MODEL
NORM_EPS = 1e-6

COL_AQ = 0
COL_AK = COL_AQ + ATT_WIDTH
COL_AV = COL_AK + ATT_WIDTH
COL_MQ = COL_AV + ATT_WIDTH
COL_MK = COL_MQ + MLSTM_WIDTH
COL_MV = COL_MK + MLSTM_WIDTH
COL_MO = COL_MV + MLSTM_WIDTH
COL_MI = COL_MO + MLSTM_WIDTH
COL_MF = COL_MI + MLSTM_HEADS
COL_GA = COL_MF + MLSTM_HEADS
COL_GB = COL_GA + D_MODEL
D_IN = COL_GB + D_MODEL


def rms_norm(x, w):
    xf = x.astype(jnp.float32)
    y = xf * lax.rsqrt(jnp.mean(xf * xf, axis=-1, keepdims=True) + NORM_EPS)
    return (y * w.astype(jnp.float32)).astype(x.dtype)

def rope_tables(positions):
    inv_freq = ROPE_THETA ** (-jnp.arange(0, ROPE_DIM, 2, dtype=jnp.float32) / ROPE_DIM)
    ang = positions.astype(jnp.float32)[..., None] * inv_freq
    return jnp.cos(ang)[:, :, None, :], jnp.sin(ang)[:, :, None, :]

def apply_partial_rope(t, cos, sin):
    half = ROPE_DIM // 2
    t1 = t[..., :half]
    t2 = t[..., half:ROPE_DIM]
    return jnp.concatenate([t1 * cos - t2 * sin, t2 * cos + t1 * sin, t[..., ROPE_DIM:]], axis=-1)

def dilated_window_attention(q, k, v, window, dilation):
    B, S, H, Dh = q.shape
    span = window // dilation
    L = S // dilation
    nb = -(-L // ATT_BLOCK)
    Lp = nb * ATT_BLOCK
    BD = B * dilation

    def to_sub(t):
        return t.reshape(B, L, dilation, H, Dh).transpose(0, 2, 1, 3, 4).reshape(BD, L, H, Dh)

    qs, ks, vs = to_sub(q), to_sub(k), to_sub(v)
    qb = jnp.pad(qs, ((0, 0), (0, Lp - L), (0, 0), (0, 0))).reshape(BD, nb, ATT_BLOCK, H, Dh)

    def key_blocks(t):
        tp = jnp.pad(t, ((0, 0), (ATT_BLOCK, Lp - L), (0, 0), (0, 0)))
        tp = tp.reshape(BD, nb + 1, ATT_BLOCK, H, Dh)
        return jnp.concatenate([tp[:, :-1], tp[:, 1:]], axis=2)

    kb, vb = key_blocks(ks), key_blocks(vs)
    blk = jnp.arange(nb)[:, None, None]
    qa = jnp.arange(ATT_BLOCK)[None, :, None]
    kc = jnp.arange(2 * ATT_BLOCK)[None, None, :]
    dist = qa + ATT_BLOCK - kc
    key_idx = blk * ATT_BLOCK - ATT_BLOCK + kc
    mask = (dist >= 0) & (dist <= span) & (key_idx >= 0)

    s = jnp.einsum('bnqhd,bnkhd->bnhqk', qb, kb) * (Dh ** -0.5)
    s = jnp.where(mask[None, :, None], s, -jnp.inf)
    m = jnp.max(s, axis=-1, keepdims=True)
    p = jnp.exp(s - m)
    l = jnp.sum(p, axis=-1)
    o = jnp.einsum('bnhqk,bnkhd->bnqhd', p, vb) / jnp.transpose(l, (0, 1, 3, 2))[..., None]
    lse = jnp.transpose(m[..., 0] + jnp.log(l), (0, 1, 3, 2))

    o = o.reshape(BD, Lp, H, Dh)[:, :L].reshape(B, dilation, L, H, Dh)
    o = o.transpose(0, 2, 1, 3, 4).reshape(B, S, H, Dh)
    lse = lse.reshape(BD, Lp, H)[:, :L].reshape(B, dilation, L, H)
    lse = lse.transpose(0, 2, 1, 3).reshape(B, S, H)
    return o, lse

def dilated_mixture_attention(q, k, v):
    outs, lses = [], []
    for window, dilation in DILATED_PATTERNS:
        o, lse = dilated_window_attention(q, k, v, window, dilation)
        outs.append(o)
        lses.append(lse)
    wts = jax.nn.softmax(jnp.stack(lses), axis=0)
    return jnp.einsum('gbsh,gbshd->bshd', wts, jnp.stack(outs))

def causal_short_conv(u, w, b):
    S = u.shape[1]
    up = jnp.pad(u, ((0, 0), (CONV_WIDTH - 1, 0), (0, 0)))
    out = b
    for j in range(CONV_WIDTH):
        out = out + w[j] * up[:, j:j + S]
    return out

def mlstm_chunkwise(q, k, v, ig, fg):
    B, S, H, D = q.shape
    L = MLSTM_CHUNK
    NC = S // L

    def chunks(t):
        return t.reshape(B, NC, L, H, D).transpose(0, 3, 1, 2, 4)

    def gchunks(t):
        return t.reshape(B, NC, L, H).transpose(0, 3, 1, 2)

    q = chunks(q) * (D ** -0.5)
    k = chunks(k)
    v = chunks(v)
    ig = gchunks(ig)
    lf = gchunks(jax.nn.log_sigmoid(fg))
    bcum = jnp.cumsum(lf, axis=-1)
    g = bcum[..., -1]

    a = g[..., None] - bcum + ig
    m_loc = jnp.max(a, axis=-1)
    wk = jnp.exp(a - m_loc[..., None])
    kv_c = jnp.einsum('bhcl,bhclk,bhclv->bhckv', wk, k, v)
    n_c = jnp.einsum('bhcl,bhclk->bhck', wk, k)

    def step(carry, xs):
        C, n, m = carry
        g_c, ml, kv, nn = xs
        m_new = jnp.maximum(g_c + m, ml)
        decay = jnp.exp(g_c + m - m_new)
        inj = jnp.exp(ml - m_new)
        C_new = decay[..., None, None] * C + inj[..., None, None] * kv
        n_new = decay[..., None] * n + inj[..., None] * nn
        return (C_new, n_new, m_new), (C, n, m)

    init = (jnp.zeros((B, H, D, D), jnp.float32), jnp.zeros((B, H, D), jnp.float32),
            jnp.zeros((B, H), jnp.float32))
    xs = (g.transpose(2, 0, 1), m_loc.transpose(2, 0, 1),
          kv_c.transpose(2, 0, 1, 3, 4), n_c.transpose(2, 0, 1, 3))
    _, (C_prev, n_prev, m_prev) = lax.scan(step, init, xs)
    C_prev = C_prev.transpose(1, 2, 0, 3, 4)
    n_prev = n_prev.transpose(1, 2, 0, 3)
    m_prev = m_prev.transpose(1, 2, 0)

    causal = jnp.tril(jnp.ones((L, L), dtype=bool))
    dmat = bcum[..., :, None] - bcum[..., None, :] + ig[..., None, :]
    dmat = jnp.where(causal, dmat, -jnp.inf)
    m_inter = bcum + m_prev[..., None]
    m_t = jnp.maximum(jnp.max(dmat, axis=-1), m_inter)
    p = jnp.exp(dmat - m_t[..., None]) * jnp.einsum('bhcld,bhcsd->bhcls', q, k)
    w_inter = jnp.exp(m_inter - m_t)
    num = (w_inter[..., None] * jnp.einsum('bhcld,bhcdv->bhclv', q, C_prev)
           + jnp.einsum('bhcls,bhcsv->bhclv', p, v))
    den = w_inter * jnp.einsum('bhcld,bhcd->bhcl', q, n_prev) + jnp.sum(p, axis=-1)
    h = num / jnp.maximum(jnp.abs(den), jnp.exp(-m_t))[..., None]
    return h.transpose(0, 2, 3, 1, 4).reshape(B, S, H, D)

def hybrid_layer(x, cos, sin, norm_mix_w, w_in, b_in, conv_w, conv_b, mlstm_norm_w,
                 w_proj_att, w_proj_mlstm, w_out, norm_mlp_w, w_ff1, w_ff2):
    B, S, _ = x.shape
    f32 = jnp.float32
    h = rms_norm(x, norm_mix_w)
    z = h @ w_in + b_in

    aq = z[..., COL_AQ:COL_AK].astype(f32).reshape(B, S, ATT_HEADS, ATT_HEAD_DIM)
    ak = z[..., COL_AK:COL_AV].astype(f32).reshape(B, S, ATT_HEADS, ATT_HEAD_DIM)
    av = z[..., COL_AV:COL_MQ].astype(f32).reshape(B, S, ATT_HEADS, ATT_HEAD_DIM)
    aq = apply_partial_rope(aq, cos, sin)
    ak = apply_partial_rope(ak, cos, sin)
    ya = dilated_mixture_attention(aq, ak, av).reshape(B, S, ATT_WIDTH).astype(x.dtype)

    qk = jax.nn.silu(causal_short_conv(z[..., COL_MQ:COL_MV].astype(f32),
                                       conv_w.astype(f32), conv_b.astype(f32)))
    mq = qk[..., :MLSTM_WIDTH].reshape(B, S, MLSTM_HEADS, MLSTM_HEAD_DIM)
    mk = qk[..., MLSTM_WIDTH:].reshape(B, S, MLSTM_HEADS, MLSTM_HEAD_DIM)
    mv = z[..., COL_MV:COL_MO].astype(f32).reshape(B, S, MLSTM_HEADS, MLSTM_HEAD_DIM)
    mi = z[..., COL_MI:COL_MF].astype(f32)
    mf = z[..., COL_MF:COL_GA].astype(f32)
    hm = mlstm_chunkwise(mq, mk, mv, mi, mf)
    hm = hm * lax.rsqrt(jnp.mean(hm * hm, axis=-1, keepdims=True) + NORM_EPS)
    hm = hm.reshape(B, S, MLSTM_WIDTH) * mlstm_norm_w.astype(f32)
    yb = (jax.nn.sigmoid(z[..., COL_MO:COL_MI].astype(f32)) * hm).astype(x.dtype)

    ga = jax.nn.sigmoid(z[..., COL_GA:COL_GB])
    gb = jax.nn.sigmoid(z[..., COL_GB:D_IN])
    mixed = ga * (ya @ w_proj_att) + gb * (yb @ w_proj_mlstm)
    x = x + mixed @ w_out

    h2 = rms_norm(x, norm_mlp_w)
    x = x + jnp.square(jax.nn.relu(h2 @ w_ff1)) @ w_ff2
    return x

def first_inputs(seed: int = 0) -> dict:
    key = jax.random.key(seed)
    ks = jax.random.split(key, 16)
    nrm = jax.random.normal
    x = nrm(ks[0], (BATCH, SEQ, D_MODEL), jnp.float32)
    offsets = jax.random.randint(ks[1], (BATCH, 1), 0, 1024, dtype=jnp.int32)
    positions = offsets + jnp.arange(SEQ, dtype=jnp.int32)[None, :]
    norm_mix_w = 1.0 + 0.05 * nrm(ks[2], (DEPTH, D_MODEL), jnp.float32)
    w_in = nrm(ks[3], (DEPTH, D_MODEL, D_IN), jnp.float32) * D_MODEL ** -0.5
    b_in = 0.02 * nrm(ks[4], (DEPTH, D_IN), jnp.float32)
    b_in = b_in.at[:, COL_MF:COL_GA].add(FORGET_BIAS)
    conv_w = nrm(ks[5], (DEPTH, CONV_WIDTH, 2 * MLSTM_WIDTH), jnp.float32) * CONV_WIDTH ** -0.5
    conv_b = 0.02 * nrm(ks[6], (DEPTH, 2 * MLSTM_WIDTH), jnp.float32)
    mlstm_norm_w = 1.0 + 0.05 * nrm(ks[7], (DEPTH, MLSTM_WIDTH), jnp.float32)
    w_proj_att = nrm(ks[8], (DEPTH, ATT_WIDTH, D_MODEL), jnp.float32) * ATT_WIDTH ** -0.5
    w_proj_mlstm = nrm(ks[9], (DEPTH, MLSTM_WIDTH, D_MODEL), jnp.float32) * MLSTM_WIDTH ** -0.5
    w_out = nrm(ks[10], (DEPTH, D_MODEL, D_MODEL), jnp.float32) * D_MODEL ** -0.5
    norm_mlp_w = 1.0 + 0.05 * nrm(ks[11], (DEPTH, D_MODEL), jnp.float32)
    w_ff1 = nrm(ks[12], (DEPTH, D_MODEL, D_FF), jnp.float32) * D_MODEL ** -0.5
    w_ff2 = nrm(ks[13], (DEPTH, D_FF, D_MODEL), jnp.float32) * (0.5 * D_FF ** -0.5)
    final_norm_w = 1.0 + 0.05 * nrm(ks[14], (D_MODEL,), jnp.float32)
    return {"x": x, "positions": positions, "norm_mix_w": norm_mix_w, "w_in": w_in,
            "b_in": b_in, "conv_w": conv_w, "conv_b": conv_b, "mlstm_norm_w": mlstm_norm_w,
            "w_proj_att": w_proj_att, "w_proj_mlstm": w_proj_mlstm, "w_out": w_out,
            "norm_mlp_w": norm_mlp_w, "w_ff1": w_ff1, "w_ff2": w_ff2,
            "final_norm_w": final_norm_w}

def first_block(x, positions, norm_mix_w, w_in, b_in, conv_w, conv_b, mlstm_norm_w,
              w_proj_att, w_proj_mlstm, w_out, norm_mlp_w, w_ff1, w_ff2, final_norm_w):
    cos, sin = rope_tables(positions)
    for l in range(DEPTH):
        x = hybrid_layer(x, cos, sin, norm_mix_w[l], w_in[l], b_in[l], conv_w[l], conv_b[l],
                         mlstm_norm_w[l], w_proj_att[l], w_proj_mlstm[l], w_out[l],
                         norm_mlp_w[l], w_ff1[l], w_ff2[l])
    return rms_norm(x, final_norm_w)


DEPTH_2 = 1

SSD_HEADS = 16
SSD_HEAD_DIM = 64
SSD_INNER = SSD_HEADS * SSD_HEAD_DIM
SSD_GROUPS = 2
SSD_STATE = 128
SSD_CONV_DIM = SSD_INNER + 2 * SSD_GROUPS * SSD_STATE
SSD_CHUNK = 128
ATT_KV_HEADS = 2
ATT_WIDTH_2 = ATT_HEADS * ATT_HEAD_DIM
IDX_HEADS = 4
IDX_HEAD_DIM = 64
TOPK_MAX = 256
Q_BLOCK = 128
POOL_WINDOWS = (2, 4, 8, 16)
POOL_GROUPS = 4
POOL_GROUP_DIM = 128
POOL_WIDTH = POOL_GROUPS * POOL_GROUP_DIM
N_BRANCH = 3
FFN_HIDDEN = ((8 * D_MODEL // 3 + 255) // 256) * 256
EPS = 1e-6
IN_SIZES = (SSD_INNER, SSD_CONV_DIM, SSD_HEADS, ATT_WIDTH_2, ATT_KV_HEADS * ATT_HEAD_DIM, ATT_KV_HEADS * ATT_HEAD_DIM, IDX_HEADS * IDX_HEAD_DIM, IDX_HEAD_DIM, IDX_HEADS, POOL_WIDTH, N_BRANCH * D_MODEL)
IN_WIDTH = SSD_INNER + SSD_CONV_DIM + SSD_HEADS + ATT_WIDTH_2 + 2 * ATT_KV_HEADS * ATT_HEAD_DIM + IDX_HEADS * IDX_HEAD_DIM + IDX_HEAD_DIM + IDX_HEADS + POOL_WIDTH + N_BRANCH * D_MODEL


def _rmsnorm(x, w):
    xf = x.astype(jnp.float32)
    y = xf * lax.rsqrt(jnp.mean(xf * xf, axis=-1, keepdims=True) + EPS)
    return (y * w.astype(jnp.float32)).astype(x.dtype)

def _split_proj(p):
    offs, acc = [], 0
    for s in IN_SIZES[:-1]:
        acc += s
        offs.append(acc)
    return jnp.split(p, offs, axis=-1)

def _causal_dwconv(u, w, b):
    out = lax.conv_general_dilated(u, w[:, None, :].astype(u.dtype), window_strides=(1,), padding=[(CONV_WIDTH - 1, 0)], dimension_numbers=('NWC', 'WIO', 'NWC'), feature_group_count=u.shape[-1])
    return out + b.astype(u.dtype)

def _ssd_scan(xh, dt, A, Bm, Cm):
    out_dtype = xh.dtype
    b, T, g, j, p = xh.shape
    n = Bm.shape[-1]
    c = T // SSD_CHUNK
    f32 = jnp.float32
    x = (xh.astype(f32) * dt.astype(f32)[..., None]).reshape(b, c, SSD_CHUNK, g, j, p)
    a = (dt.astype(f32) * A.astype(f32)).reshape(b, c, SSD_CHUNK, g, j)
    Bc = Bm.astype(f32).reshape(b, c, SSD_CHUNK, g, n)
    Cc = Cm.astype(f32).reshape(b, c, SSD_CHUNK, g, n)
    a_cs = jnp.cumsum(a, axis=2)
    causal = jnp.tril(jnp.ones((SSD_CHUNK, SSD_CHUNK), dtype=bool))[None, None, :, :, None, None]
    seg = a_cs[:, :, :, None] - a_cs[:, :, None, :]
    lmat = jnp.exp(jnp.where(causal, seg, -jnp.inf))
    cb = jnp.einsum('bclgn,bcsgn->bclsg', Cc, Bc)
    y_diag = jnp.einsum('bclsg,bclsgj,bcsgjp->bclgjp', cb, lmat, x)
    decay_states = jnp.exp(a_cs[:, :, -1:] - a_cs)
    states = jnp.einsum('bclgn,bclgj,bclgjp->bcgjpn', Bc, decay_states, x)
    chunk_decay = jnp.exp(a_cs[:, :, -1])

    def step(h, inp):
        s_c, d_c = inp
        return h * d_c[..., None, None] + s_c, h

    h0 = jnp.zeros((b, g, j, p, n), f32)
    _, prev = lax.scan(step, h0, (jnp.swapaxes(states, 0, 1), jnp.swapaxes(chunk_decay, 0, 1)))
    prev = jnp.swapaxes(prev, 0, 1)
    y_off = jnp.einsum('bclgn,bcgjpn,bclgj->bclgjp', Cc, prev, jnp.exp(a_cs))
    return (y_diag + y_off).reshape(b, T, g, j, p).astype(out_dtype)

def _dsa_attention(q, k, v, qi, ki, wi):
    b, T = q.shape[0], q.shape[1]
    topk = min(TOPK_MAX, T // 4)
    nb = T // Q_BLOCK
    att_scale = ATT_HEAD_DIM ** -0.5
    idx_scale = (IDX_HEADS ** -0.5) * (IDX_HEAD_DIM ** -0.5)
    key_pos = jnp.arange(T)
    ki32 = ki.astype(jnp.float32)

    def blockify(a):
        return jnp.swapaxes(a.reshape((b, nb, Q_BLOCK) + a.shape[2:]), 0, 1)

    def one_block(args):
        qb, qib, wib, pos = args
        s = jnp.einsum('bqhd,bsd->bqhs', qib.astype(jnp.float32), ki32)
        score = jnp.einsum('bqhs,bqh->bqs', jax.nn.relu(s), wib.astype(jnp.float32) * idx_scale)
        admissible = key_pos[None, None, :] <= pos[None, :, None]
        score = jnp.where(admissible, score, -jnp.inf)
        _, idx = lax.top_k(score, topk)
        valid = idx <= pos[None, :, None]
        ksel = jax.vmap(lambda kb, ib: kb[ib])(k, idx)
        vsel = jax.vmap(lambda vb, ib: vb[ib])(v, idx)
        logits = jnp.einsum('bqhgd,bqkhd->bqhgk', qb, ksel).astype(jnp.float32) * att_scale
        logits = jnp.where(valid[:, :, None, None, :], logits, -jnp.inf)
        prob = jax.nn.softmax(logits, axis=-1)
        return jnp.einsum('bqhgk,bqkhd->bqhgd', prob.astype(vsel.dtype), vsel)

    pos_blocks = jnp.arange(T).reshape(nb, Q_BLOCK)
    out = lax.map(one_block, (blockify(q), blockify(qi), blockify(wi), pos_blocks))
    return jnp.swapaxes(out, 0, 1).reshape(b, T, ATT_WIDTH_2)

def _pool_mixer(u, w, scale):
    b, T, _ = u.shape
    ug = u.reshape(b, T, POOL_GROUPS, POOL_GROUP_DIM).astype(jnp.float32)
    cs = jnp.cumsum(ug, axis=1)
    t1 = jnp.arange(1, T + 1, dtype=jnp.float32)
    outs = []
    for gi, win in enumerate(POOL_WINDOWS):
        c = cs[:, :, gi]
        lag = jnp.pad(c, ((0, 0), (win, 0), (0, 0)))[:, :T]
        cnt = jnp.minimum(t1, float(win))[None, :, None]
        outs.append((c - lag) / cnt - ug[:, :, gi])
    pooled = jnp.stack(outs, axis=2).astype(u.dtype)
    mixed = jnp.einsum('btgc,gcd->btgd', pooled, w)
    return mixed.reshape(b, T, POOL_WIDTH) * scale

def _layer(h, norm1_w, w_in, conv_w, conv_b, dt_bias, a_log, d_skip, ssd_norm_w, pool_w, pool_scale, w_up_ssd, w_up_attn, w_up_pool, w_out, norm2_w, w_ffn_in, w_ffn_out):
    b, T, _ = h.shape
    xn = _rmsnorm(h, norm1_w)
    proj = xn @ w_in
    z, xbc, dt_raw, q, k, v, qi, ki, wi, u, gates = _split_proj(proj)
    xbc = jax.nn.silu(_causal_dwconv(xbc, conv_w, conv_b))
    xs, Bm, Cm = jnp.split(xbc, [SSD_INNER, SSD_INNER + SSD_GROUPS * SSD_STATE], axis=-1)
    dt = jax.nn.softplus(dt_raw + dt_bias)
    A = -jnp.exp(a_log)
    hpg = SSD_HEADS // SSD_GROUPS
    xh = xs.reshape(b, T, SSD_GROUPS, hpg, SSD_HEAD_DIM)
    y = _ssd_scan(xh, dt.reshape(b, T, SSD_GROUPS, hpg), A.reshape(SSD_GROUPS, hpg), Bm.reshape(b, T, SSD_GROUPS, SSD_STATE), Cm.reshape(b, T, SSD_GROUPS, SSD_STATE))
    y = y + d_skip.reshape(SSD_GROUPS, hpg)[..., None] * xh
    y_ssd = _rmsnorm(y.reshape(b, T, SSD_INNER) * jax.nn.silu(z), ssd_norm_w)
    qh = q.reshape(b, T, ATT_KV_HEADS, ATT_HEADS // ATT_KV_HEADS, ATT_HEAD_DIM)
    kh = k.reshape(b, T, ATT_KV_HEADS, ATT_HEAD_DIM)
    vh = v.reshape(b, T, ATT_KV_HEADS, ATT_HEAD_DIM)
    y_att = _dsa_attention(qh, kh, vh, qi.reshape(b, T, IDX_HEADS, IDX_HEAD_DIM), ki, wi)
    y_pool = _pool_mixer(u, pool_w, pool_scale)
    g = jax.nn.sigmoid(gates.reshape(b, T, N_BRANCH, D_MODEL))
    merged = g[:, :, 0] * (y_ssd @ w_up_ssd) + g[:, :, 1] * (y_att @ w_up_attn) + g[:, :, 2] * (y_pool @ w_up_pool)
    h = h + merged @ w_out
    hn = _rmsnorm(h, norm2_w)
    a_part, b_part = jnp.split(hn @ w_ffn_in, 2, axis=-1)
    return h + (jax.nn.silu(a_part) * b_part) @ w_ffn_out

def second_inputs(seed: int = 0) -> dict:
    key = jax.random.key(seed)
    ks = jax.random.split(key, 20)
    f32 = jnp.float32
    L = DEPTH_2

    def nrm(k, shape, fan_in):
        return jax.random.normal(k, shape, f32) * (fan_in ** -0.5)

    def gain(k, shape):
        return 1.0 + 0.02 * jax.random.normal(k, shape, f32)

    u_dt = jax.random.uniform(ks[5], (L, SSD_HEADS), f32)
    dt0 = jnp.exp(u_dt * (math.log(0.1) - math.log(0.001)) + math.log(0.001))
    dt_bias = dt0 + jnp.log(-jnp.expm1(-dt0))
    return {
        "x": jax.random.normal(ks[0], (BATCH, SEQ, D_MODEL), f32),
        "norm1_w": gain(ks[1], (L, D_MODEL)),
        "w_in": nrm(ks[2], (L, D_MODEL, IN_WIDTH), D_MODEL),
        "conv_w": nrm(ks[3], (L, CONV_WIDTH, SSD_CONV_DIM), CONV_WIDTH),
        "conv_b": 0.02 * jax.random.normal(ks[4], (L, SSD_CONV_DIM), f32),
        "dt_bias": dt_bias,
        "a_log": jnp.log(jax.random.uniform(ks[6], (L, SSD_HEADS), f32, minval=1.0, maxval=16.0)),
        "d_skip": gain(ks[7], (L, SSD_HEADS)),
        "ssd_norm_w": gain(ks[8], (L, SSD_INNER)),
        "pool_w": nrm(ks[9], (L, POOL_GROUPS, POOL_GROUP_DIM, POOL_GROUP_DIM), POOL_GROUP_DIM),
        "pool_scale": gain(ks[10], (L, POOL_WIDTH)),
        "w_up_ssd": nrm(ks[11], (L, SSD_INNER, D_MODEL), SSD_INNER),
        "w_up_attn": nrm(ks[12], (L, ATT_WIDTH_2, D_MODEL), ATT_WIDTH_2),
        "w_up_pool": nrm(ks[13], (L, POOL_WIDTH, D_MODEL), POOL_WIDTH),
        "w_out": nrm(ks[14], (L, D_MODEL, D_MODEL), D_MODEL),
        "norm2_w": gain(ks[15], (L, D_MODEL)),
        "w_ffn_in": nrm(ks[16], (L, D_MODEL, 2 * FFN_HIDDEN), D_MODEL),
        "w_ffn_out": nrm(ks[17], (L, FFN_HIDDEN, D_MODEL), FFN_HIDDEN),
        "final_norm_w": gain(ks[18], (D_MODEL,)),
    }

def second_block(x, norm1_w, w_in, conv_w, conv_b, dt_bias, a_log, d_skip, ssd_norm_w, pool_w, pool_scale, w_up_ssd, w_up_attn, w_up_pool, w_out, norm2_w, w_ffn_in, w_ffn_out, final_norm_w):
    h = x
    for l in range(DEPTH_2):
        h = _layer(h, norm1_w[l], w_in[l], conv_w[l], conv_b[l], dt_bias[l], a_log[l], d_skip[l], ssd_norm_w[l], pool_w[l], pool_scale[l], w_up_ssd[l], w_up_attn[l], w_up_pool[l], w_out[l], norm2_w[l], w_ffn_in[l], w_ffn_out[l])
    return _rmsnorm(h, final_norm_w)


_first_inputs = second_inputs


def second_inputs(seed=0):
    import zlib

    import numpy as np

    out = dict(_first_inputs(seed))
    spreads = {}
    factors = {'conv_b': 4.469,
     'd_skip': 8.0,
     'ssd_norm_w': 6.328,
     'pool_scale': 6.437,
     'norm2_w': 4.565,
     'final_norm_w': 2.915}
    for name, (base, spread) in spreads.items():
        noise = np.random.default_rng([zlib.crc32(name.encode()), seed]).standard_normal(out[name].shape)
        drawn = base * np.exp(spread * noise) if base else spread * noise
        out[name] = jnp.asarray(drawn.astype(out[name].dtype))
    for name, factor in factors.items():
        out[name] = (out[name] * factor).astype(out[name].dtype)
    return out


_narrow_inputs = second_inputs


def second_inputs(seed=0):

    out = dict(_narrow_inputs(seed))
    wider = {'d_skip': 3.73, 'ssd_norm_w': 3.42, 'pool_scale': 3.37, 'final_norm_w': 3.28}
    for name, times in wider.items():
        mean = out[name].mean()
        out[name] = (mean + times * (out[name] - mean)).astype(out[name].dtype)
    return out


def setup_inputs(seed=0):
    out = dict(first_inputs(seed))
    for name, value in second_inputs(seed + 1).items():
        if name != "x":
            out[name + "_2"] = value
    return out


def reference(
    x, positions, norm_mix_w, w_in, b_in, conv_w, conv_b, mlstm_norm_w, w_proj_att,
    w_proj_mlstm, w_out, norm_mlp_w, w_ff1, w_ff2, final_norm_w, norm1_w_2, w_in_2, conv_w_2,
    conv_b_2, dt_bias_2, a_log_2, d_skip_2, ssd_norm_w_2, pool_w_2, pool_scale_2, w_up_ssd_2,
    w_up_attn_2, w_up_pool_2, w_out_2, norm2_w_2, w_ffn_in_2, w_ffn_out_2, final_norm_w_2,
):
    x = first_block(
        x, positions, norm_mix_w, w_in, b_in, conv_w, conv_b, mlstm_norm_w, w_proj_att,
        w_proj_mlstm, w_out, norm_mlp_w, w_ff1, w_ff2, final_norm_w,
    )
    return second_block(
        x, norm1_w_2, w_in_2, conv_w_2, conv_b_2, dt_bias_2, a_log_2, d_skip_2, ssd_norm_w_2,
        pool_w_2, pool_scale_2, w_up_ssd_2, w_up_attn_2, w_up_pool_2, w_out_2, norm2_w_2,
        w_ffn_in_2, w_ffn_out_2, final_norm_w_2,
    )


_drawn_inputs = setup_inputs


def setup_inputs(seed=0):
    import zlib

    import numpy as np

    out = dict(_drawn_inputs(seed))
    spreads = {}
    factors = {'conv_b': 3.061}
    for name, (base, spread) in spreads.items():
        noise = np.random.default_rng([zlib.crc32(name.encode()), seed]).standard_normal(out[name].shape)
        drawn = base * np.exp(spread * noise) if base else spread * noise
        out[name] = jnp.asarray(drawn.astype(out[name].dtype))
    for name, factor in factors.items():
        out[name] = (out[name] * factor).astype(out[name].dtype)
    return out
```

```python
import math
from contextlib import ExitStack

import numpy as np

import concourse.bass as bass
from concourse import mybir

F32 = mybir.dt.float32
F32R = mybir.dt.float32r
I32 = mybir.dt.int32
ACT = mybir.ActivationFunctionType
ALU = mybir.AluOpType
AX = mybir.AxisListType

P = 128
T = 512
TT = T // P
D = 1024
KD = D // P
DEPTH = 2
EPS = 1e-6
BIG = 1e30
SLOT = 2048
UC = SLOT // KD
UT = UC // P

HEADS, HD = 8, 64
MH, MD = 4, 128
CONV = 4
DFF = 4 * D
AQ, AK, AV, MQ, MK, MV, MO = (512 * i for i in range(7))
MI = 3584
GA = MI + 2 * MH
GB = GA + D
NPAT = 3
PATTERNS = ((128, 1), (512, 4), (2048, 16))
ROPE_THETA, ROPE_DIM = 500000.0, HD // 4

SH, SHD, SG = 16, 64, 2
SPG = SH // SG
XC = 1536
Z2, XBC2 = 0, D
DT2 = XBC2 + XC
Q2 = DT2 + SH
K2 = Q2 + 512
QI2 = K2 + 256
KI2 = QI2 + 256
IH = 4
U2 = KI2 + 64 + IH
G2 = U2 + 512
FF2 = 2816
TOPK = 128
TAKEN = -3e38
WINDOWS = (2, 4, 8, 16)

C_ID, C_ONE, C_ROT, C_QK, C_ST, C_KEEP, C_PAT = (P * i for i in range(7))
C_INV = C_PAT + TT * P
C_MSK, C_UNM = C_INV + 1, C_INV + 2
C_CNT = C_INV + 3
C_END = C_CNT + len(WINDOWS) * 16


def up8(n):
    return (n + 7) // 8 * 8


def constants():
    c = np.zeros((P, C_END), np.float32)
    i = np.arange(P)
    c[:, C_ID:C_ID + P] = np.eye(P)
    c[:, C_ONE:C_ONE + P] = 1.0
    half = ROPE_DIM // 2
    for p in range(P):
        d = p % HD
        if d < half:
            c[p + half, C_ROT + p] = -1.0
        elif d < ROPE_DIM:
            c[p - half, C_ROT + p] = 1.0
    c[:, C_QK:C_QK + P] = np.where(i[None, :] > i[:, None], BIG, 0.0)
    c[:, C_ST:C_ST + P] = np.where(i[:, None] > i[None, :], BIG, 0.0)
    c[:, C_KEEP:C_KEEP + P] = i[:, None] <= i[None, :]
    for b in range(TT):
        dist = i[:, None] - i[None, :] + (TT - 1 - b) * P
        n = sum(((dist >= 0) & (dist % dil == 0) & (dist <= win)).astype(int) for win, dil in PATTERNS)
        c[:, C_PAT + b * P:C_PAT + (b + 1) * P] = np.where(n > 0, -np.log(np.maximum(n, 1)), BIG)
    d = i % HD
    inv = np.float32(ROPE_THETA) ** (-np.arange(0, ROPE_DIM, 2, dtype=np.float32) / np.float32(ROPE_DIM))
    c[:, C_INV] = np.where(d < ROPE_DIM, inv[d % half], 0.0)
    c[:, C_MSK] = d < ROPE_DIM
    c[:, C_UNM] = d >= ROPE_DIM
    for g, w in enumerate(WINDOWS):
        c[:, C_CNT + 16 * g:C_CNT + 16 * (g + 1)] = 1.0 / np.minimum(np.arange(1, 17), w)
    return c


class Stage:

    def __init__(self, k, name, prev):
        self.k, self.name, self.prev, self.ends, self.s = k, name, prev, [], {}

    def sem(self, name):
        if name not in self.s:
            self.s[name] = self.k.new_sem(f"{self.name}_{name}")
        return self.s[name]

    def join(self, eng):
        if self.prev is not None:
            for s, v in self.prev.ends:
                eng.wait_ge(s, v)

    def sp(self, e): pass
    def act(self, e): pass
    def dve(self, e): pass
    def pe(self, e): pass


class Kern:
    def __init__(self, nc, ctx):
        self.nc, self.ctx, self.sems = nc, ctx, []
        self.top = (nc.sbuf_base + 31) // 32 * 32

    def new_sem(self, name):
        s = self.ctx.enter_context(self.nc.semaphore(name))
        self.sems.append(s)
        return s

    def at(self, name, off, cols, dt=F32, parts=P):
        assert off + cols <= self.arena_words, (name, off, cols)
        return self.nc.alloc_sbuf_tensor_at(name, [parts, cols], dt, offset=self.arena + 4 * off)

    def keep(self, name, cols, dt=F32):
        t = self.nc.alloc_sbuf_tensor_at(name, [P, cols], dt, offset=self.top)
        self.top += 4 * ((cols + 7) // 8 * 8)
        return t

    def slot(self, u):
        return u % 2

    def const(self, c):
        return self.cst[:, c:c + P]

    def col(self, c):
        return self.pcol[:, c:c + 1]

    def pick(self, h, n):
        return self.cst[0:n, C_ID + h:C_ID + h + 1].broadcast_to([n, P])

    def ones(self, n, w):
        return self.cst[0:n, C_ONE:C_ONE + 1].broadcast_to([n, w])

    def hh(self, i):
        return self.hhi[:, i * T:(i + 1) * T]

    def hl(self, i):
        return self.hlo[:, i * T:(i + 1) * T]

    def stream_sems(self, tag):
        self.landed = [self.new_sem(f"{tag}_unit_landed_{i}") for i in range(2)]
        self.hi_done = self.new_sem(f"{tag}_unit_hi_done")
        self.split = self.new_sem(f"{tag}_unit_split")
        self.unit_used = self.new_sem(f"{tag}_unit_used")
        self.units = 0


def units(k, n):
    k.units += n
    return k.units - n



def load_unit(k, sp, u0, du, src, cols):
    slot = k.slot(u0)
    if not (isinstance(du, int) and u0 + du < 2):
        sp.wait_ge(k.split, du + (u0 - 1))
    n = src.shape[1]
    dst = k.wraw[:, slot * SLOT:slot * SLOT + n * cols].rearrange("p (k n) -> p k n", n=cols)
    sp.dma_start(dst, src).then_inc(k.landed[slot], 16)


def hi_unit(k, act, u0, du):
    slot = k.slot(u0)
    act.wait_ge(k.landed[slot], landed_value(u0, du))
    if not (isinstance(du, int) and u0 + du < 2):
        act.wait_ge(k.unit_used, du + (u0 - 1))
    act.activation(k.whi[:, slot * SLOT:(slot + 1) * SLOT], k.wraw[:, slot * SLOT:(slot + 1) * SLOT],
                   ACT.Copy).then_inc(k.hi_done, 1)


def landed_value(u0, du):
    return du * 8 + 16 * (u0 // 2 + 1)


def lo_units(k, pool, n):
    def one(slot, value):
        a = slot * SLOT
        pool.wait_ge(k.hi_done, value)
        pool.tensor_tensor(k.wlo[:, a:a + SLOT], k.wraw[:, a:a + SLOT], k.whi[:, a:a + SLOT],
                           ALU.subtract).then_inc(k.split, 1)
    with pool.Fori(0, n // 2) as i:
        one(0, i * 2 + 1)
        one(1, i * 2 + 2)
    if n % 2:
        one(0, n)


def fm_unit(k, pe, u0, kt, cols, xh, xl, outs):
    a = k.slot(u0) * SLOT
    for c, out in enumerate(outs):
        for i in range(kt):
            w = slice(a + i * cols + c * P, a + i * cols + (c + 1) * P)
            pe.matmul(out, k.whi[:, w], xh(i), start=i == 0, stop=False)
            pe.matmul(out, k.whi[:, w], xl(i), start=False, stop=False)
            mm = pe.matmul(out, k.wlo[:, w], xh(i), start=False, stop=i == kt - 1)
    return mm


def tm_unit(k, pe, u0, kt, cols, off, width, xh, xl, out):
    a = k.slot(u0) * SLOT
    for t in range(TT):
        tok = slice(t * P, (t + 1) * P)
        for i in range(kt):
            w = slice(a + i * cols + off, a + i * cols + off + width)
            pe.matmul(out(t), xh(i)[:, tok], k.whi[:, w], start=i == 0, stop=False)
            pe.matmul(out(t), xl(i)[:, tok], k.whi[:, w], start=False, stop=False)
            mm = pe.matmul(out(t), xh(i)[:, tok], k.wlo[:, w], start=False, stop=i == kt - 1)
    return mm



class Norm(Stage):

    def __init__(self, k, name, prev, wcol, final=False):
        super().__init__(k, name, prev)
        self.wcol, self.final = wcol, final
        self.sq = k.at(f"{name}_sq", 0, KD * T)
        self.h = k.xT if final else k.at(f"{name}_h", KD * T, KD * T)
        self.r = k.at(f"{name}_r", 2 * KD * T, 2 * T)
        self.ends = [(self.sem("scaled" if final else "lo"), KD)]

    def act(self, act):
        k = self.k
        self.join(act)
        for t in range(KD):
            act.activation(self.sq[:, t * T:(t + 1) * T], k.xT[:, t * T:(t + 1) * T],
                           ACT.Square).then_inc(self.sem("sq"), 1)
        act.wait_ge(self.sem("sum"), 1)
        act.activation(self.r[:, 0:T], k.ps[:, 4, :], ACT.Sqrt, bias=k.eps[:, 0:1],
                       scale=1.0 / D).then_inc(self.sem("root"), 1)
        if not self.final:
            for t in range(KD):
                act.wait_ge(self.sem("scaled"), t + 1)
                act.activation(k.hhi[:, t * T:(t + 1) * T], self.h[:, t * T:(t + 1) * T],
                               ACT.Copy).then_inc(self.sem("hi"), 1)

    def pe(self, pe):
        k = self.k
        self.join(pe)
        for t in range(KD):
            pe.wait_ge(self.sem("sq"), t + 1)
            mm = pe.matmul(k.ps[:, 4, :], k.const(C_ONE), self.sq[:, t * T:(t + 1) * T],
                           start=t == 0, stop=t == KD - 1)
        mm.then_inc(self.sem("sum"), 1)

    def dve(self, dve):
        k = self.k
        self.join(dve)
        dve.wait_ge(self.sem("root"), 1)
        dve.reciprocal(self.r[:, T:2 * T], self.r[:, 0:T]).then_inc(self.sem("rstd"), 1)
        dve.wait_ge(self.sem("rstd"), 1)
        for t in range(KD):
            dve.scalar_tensor_tensor(self.h[:, t * T:(t + 1) * T], k.xT[:, t * T:(t + 1) * T],
                                     k.col(self.wcol + t), self.r[:, T:2 * T], ALU.mult,
                                     ALU.mult).then_inc(self.sem("scaled"), 1)
        if not self.final:
            for t in range(KD):
                dve.wait_ge(self.sem("scaled"), t + 1)
                dve.wait_ge(self.sem("hi"), t + 1)
                dve.tensor_tensor(k.hlo[:, t * T:(t + 1) * T], self.h[:, t * T:(t + 1) * T],
                                  k.hhi[:, t * T:(t + 1) * T], ALU.subtract).then_inc(self.sem("lo"), 1)


class Seg:

    def __init__(self, kind, n, src, cols, evac, eng="act", loop=False, off=0, width=None, tiles=UT):
        self.kind, self.n, self.src, self.cols, self.evac = kind, n, src, cols, evac
        self.eng, self.loop, self.off, self.width, self.tiles = eng, loop, off, width or cols, tiles


class Project(Stage):

    def __init__(self, k, name, prev, segs):
        super().__init__(k, name, prev)
        self.segs = segs
        self.u0 = k.units
        for s in segs:
            s.u0 = units(k, s.n)
        n = k.units - self.u0
        self.out = [self.sem("out_even"), self.sem("out_odd")]
        self.ends = [(self.out[0], (n + 1) // 2), (self.out[1], n // 2)]

    def each(self, eng, body, which=lambda s: True, peel=lambda s: False):
        for s in filter(which, self.segs):
            if s.loop:
                first = 1 if peel(s) else 0
                for j in range(2 * first):
                    body(s, j, 0)
                with eng.Fori(first, s.n // 2) as i:
                    for j in range(2):
                        body(s, j, i)
            else:
                for j in range(s.n):
                    body(s, j, 0)

    def sp(self, sp):
        self.each(sp, lambda s, j, i: load_unit(self.k, sp, s.u0 + j, i * 2, s.src(j, i), s.cols),
                  peel=lambda s: s.u0 < 2)

    def pe(self, pe):
        k = self.k
        self.join(pe)

        def unit(s, j, i):
            local = s.u0 + j - self.u0
            bank = 2 * (local % 2)
            pe.wait_ge(k.split, i * 2 + (s.u0 + j + 1))
            if local >= 2 or not isinstance(i, int):
                pe.wait_ge(self.out[local % 2], i + local // 2)
            if s.kind == "fm":
                mm = fm_unit(k, pe, s.u0 + j, KD, s.cols, k.hh, k.hl,
                             [k.ps[:, bank + c, :] for c in range(s.tiles)])
                if s.off:
                    mm = tm_unit(k, pe, s.u0 + j, KD, s.cols, s.off, s.width, k.hh, k.hl,
                                 lambda t: k.ps[:, bank + 1, t * P:t * P + s.width])
            else:
                mm = tm_unit(k, pe, s.u0 + j, KD, s.cols, 0, s.cols, k.hh, k.hl,
                             lambda t: k.ps[:, bank + t // 2, t % 2 * UC:t % 2 * UC + s.cols])
            mm.then_inc(k.unit_used, 1)
        self.each(pe, unit, peel=lambda s: s.u0 - self.u0 < 2)

    def evac(self, eng, who):
        k = self.k

        def unit(s, j, i):
            local = s.u0 + j - self.u0
            bank = 2 * (local % 2)
            if s.eng == who:
                eng.wait_ge(k.unit_used, i * 2 + (s.u0 + j + 1))
                s.evac(eng, j, i, bank).then_inc(self.out[local % 2], 1)
            if who == "act":
                hi_unit(k, eng, s.u0 + j + 2, i * 2)
        self.each(eng, unit, lambda s: who == "act" or s.eng == who)

    def act(self, act):
        self.join(act)
        self.evac(act, "act")

    def dve(self, dve):
        self.join(dve)
        self.evac(dve, "dve")


class Rope(Stage):

    def __init__(self, k, name, prev, qk, t1, t2):
        super().__init__(k, name, prev)
        self.qk, self.t1, self.t2 = qk, t1, t2
        self.ends = [(self.sem("turned"), 8)]

    def pe(self, pe):
        k = self.k
        self.join(pe)
        for t in range(8):
            if t >= 4:
                pe.wait_ge(self.sem("sin"), t - 3)
            pe.matmul(k.ps[:, 4 + t % 4, :], k.const(C_ROT), self.qk[:, t * T:(t + 1) * T],
                      start=True, stop=True).then_inc(self.sem("swapped"), 1)

    def dve(self, dve):
        k = self.k
        self.join(dve)
        for t in range(8):
            scale = -HD ** -0.5 if t < 4 else 1.0
            a, b = (x[:, t % 2 * T:(t % 2 + 1) * T] for x in (self.t1, self.t2))
            tile = self.qk[:, t * T:(t + 1) * T]
            dve.scalar_tensor_tensor(a, tile, scale, k.cos[:, :], ALU.mult, ALU.mult)\
               .then_inc(self.sem("cos"), 1)
            dve.wait_ge(self.sem("swapped"), t + 1)
            dve.scalar_tensor_tensor(b, k.ps[:, 4 + t % 4, :], scale, k.sin[:, :], ALU.mult, ALU.mult)\
               .then_inc(self.sem("sin"), 1)
            dve.wait_ge(self.sem("cos"), t + 1)
            dve.wait_ge(self.sem("sin"), t + 1)
            dve.tensor_tensor(tile, a, b, ALU.add).then_inc(self.sem("turned"), 1)


class Attention(Stage):


    def __init__(self, k, name, prev, q, kk, v, mask, scr, yhi, ylo):
        super().__init__(k, name, prev)
        self.q, self.kk, self.v, self.mask, self.yhi, self.ylo = q, kk, v, mask, yhi, ylo
        self.ns = k.at(f"{name}_negscores", scr, 2 * T)
        self.p = k.at(f"{name}_probs", scr + 2 * T, 2 * T)
        self.pt = k.at(f"{name}_probsT", scr + 4 * T, 2 * TT * T)
        self.N = HEADS * TT
        self.stat = k.stat
        self.ends = [(self.sem("lo"), HEADS)]

    def pe(self, pe):
        k = self.k
        self.join(pe)
        for n in range(self.N + 2):
            if n < self.N:
                h, i = divmod(n, TT)
                if n >= 2:
                    pe.wait_ge(self.sem("masked"), n - 1)
                pe.matmul(k.ps[:, 4 + n % 2, 0:(i + 1) * P], self.q(h)[:, i * P:(i + 1) * P],
                          self.kk(h)[:, 0:(i + 1) * P], start=True, stop=True)\
                  .then_inc(self.sem("scores"), 1)
            m = n - 1
            if 0 <= m < self.N:
                i = m % TT
                pe.wait_ge(self.sem("probs"), m + 1)
                if m >= 1:
                    pe.wait_ge(self.sem("copied"), m)
                for b in range(i + 1):
                    tr = pe.transpose(k.ps[:, 6, b * P:(b + 1) * P],
                                      self.p[:, m % 2 * T + b * P:m % 2 * T + (b + 1) * P], k.const(C_ID))
                tr.then_inc(self.sem("turned"), 1)
            m = n - 2
            if m >= 0 and m % TT == TT - 1:
                h = m // TT
                pe.wait_ge(self.sem("copied"), m + 1)
                if h >= 1:
                    pe.wait_ge(self.sem("lo"), h)
                r = slice(h % 2 * HD, h % 2 * HD + HD)
                for b in range(TT):
                    mm = pe.matmul(k.ps[r, 7, b * P:T], self.v(b, h),
                                   self.pt[:, (h % 2 * TT + b) * T + b * P:(h % 2 * TT + b + 1) * T],
                                   start=b == 0, stop=b == TT - 1, skip_group_check=True)
                mm.then_inc(self.sem("values"), 1)

    def dve(self, dve):
        k = self.k
        self.join(dve)
        for n in range(self.N + 2):
            if n < self.N:
                i = n % TT
                w = (i + 1) * P
                dve.wait_ge(self.sem("scores"), n + 1)
                if n >= 2:
                    dve.wait_ge(self.sem("exp"), n - 1)
                dve.tensor_tensor_reduce(self.ns[:, n % 2 * T:n % 2 * T + w], k.ps[:, 4 + n % 2, 0:w],
                                         self.mask(i), 1.0, BIG, ALU.add, ALU.min,
                                         self.stat[:, n:n + 1]).then_inc(self.sem("masked"), 1)
            m = n - 1
            if 0 <= m < self.N:
                w = (m % TT + 1) * P
                dve.wait_ge(self.sem("exp"), m + 1)
                dve.reciprocal(self.stat[:, 64 + m:65 + m], self.stat[:, 32 + m:33 + m])\
                   .then_inc(self.sem("recip"), 1)
                dve.wait_ge(self.sem("recip"), m + 1)
                pr = self.p[:, m % 2 * T:m % 2 * T + w]
                dve.tensor_scalar(pr, pr, self.stat[:, 64 + m:65 + m], None, ALU.mult)\
                   .then_inc(self.sem("probs"), 1)
            m = n - 2
            if m >= 0 and m % TT == TT - 1:
                h = m // TT
                r = slice(h % 2 * HD, h % 2 * HD + HD)
                dve.wait_ge(self.sem("hi"), h + 1)
                dve.tensor_tensor(self.ylo[r, h // 2 * T:(h // 2 + 1) * T], k.ps[r, 7, :],
                                  self.yhi[r, h // 2 * T:(h // 2 + 1) * T], ALU.subtract)\
                   .then_inc(self.sem("lo"), 1)

    def act(self, act):
        k = self.k
        self.join(act)
        for n in range(self.N + 2):
            if n < self.N:
                w = (n % TT + 1) * P
                act.wait_ge(self.sem("masked"), n + 1)
                if n >= 2:
                    act.wait_ge(self.sem("turned"), n - 1)
                act.activation(self.p[:, n % 2 * T:n % 2 * T + w], self.ns[:, n % 2 * T:n % 2 * T + w],
                               ACT.Exp, bias=self.stat[:, n:n + 1], scale=-1.0,
                               accum_out=self.stat[:, 32 + n:33 + n]).then_inc(self.sem("exp"), 1)
            m = n - 1
            if 0 <= m < self.N:
                h, i = divmod(m, TT)
                act.wait_ge(self.sem("turned"), m + 1)
                if h >= 2 and i == 0:
                    act.wait_ge(self.sem("values"), h - 1)
                dst = self.pt[:, h % 2 * TT * T:(h % 2 + 1) * TT * T].rearrange("p (b q) -> p b q", b=TT)
                act.activation(dst[:, 0:i + 1, i * P:(i + 1) * P],
                               k.ps[:, 6, 0:(i + 1) * P].rearrange("p (b q) -> p b q", q=P),
                               ACT.Copy).then_inc(self.sem("copied"), 1)
            m = n - 2
            if m >= 0 and m % TT == TT - 1:
                h = m // TT
                r = slice(h % 2 * HD, h % 2 * HD + HD)
                act.wait_ge(self.sem("values"), h + 1)
                act.activation(self.yhi[r, h // 2 * T:(h // 2 + 1) * T], k.ps[r, 7, :],
                               ACT.Copy).then_inc(self.sem("hi"), 1)


class Conv(Stage):

    def __init__(self, k, name, prev, src, dst, tiles, wcol, bcol):
        super().__init__(k, name, prev)
        self.src, self.dst, self.tiles, self.wcol, self.bcol = src, dst, tiles, wcol, bcol
        self.ends = [(self.sem("silu"), tiles)]

    def tap(self, t, j):
        a = t * (T + CONV - 1) + j
        return self.src[:, a:a + T]

    def act(self, act):
        k = self.k
        self.join(act)
        for t in range(self.tiles):
            act.activation(self.dst[:, t * T:(t + 1) * T], self.tap(t, 0), ACT.Identity,
                           bias=k.col(self.bcol + t), scale=k.col(self.wcol + t))\
               .then_inc(self.sem("tap"), 1)
        for t in range(self.tiles):
            act.wait_ge(self.sem("taps"), t + 1)
            d = self.dst[:, t * T:(t + 1) * T]
            act.activation(d, d, ACT.Silu).then_inc(self.sem("silu"), 1)

    def dve(self, dve):
        k = self.k
        self.join(dve)
        done = 0
        for t0 in range(0, self.tiles, 4):
            for j in range(1, CONV):
                for t in range(t0, t0 + 4):
                    d = self.dst[:, t * T:(t + 1) * T]
                    if j == 1:
                        dve.wait_ge(self.sem("tap"), t + 1)
                    else:
                        dve.wait_ge(self.sem("part"), t0 // 4 * 8 + (j - 2) * 4 + t - t0 + 1)
                    ins = dve.scalar_tensor_tensor(d, self.tap(t, j), k.col(self.wcol + j * self.tiles + t),
                                                   d, ALU.mult, ALU.add)
                    ins.then_inc(self.sem("taps" if j == CONV - 1 else "part"), 1)


class Softplus(Stage):

    def __init__(self, k, name, prev, x, out, w, pre):
        super().__init__(k, name, prev)
        self.x, self.out, self.w, self.pre = x, out, w, pre
        self.ends = [(self.sem("step"), 11)]

    def act(self, act):
        k, w = self.k, self.w
        e, u, ln = (k.tmp[:, i * 64:i * 64 + w] for i in range(3))
        act.wait_ge(self.sem("step"), 2)
        act.activation(e, k.tmp[:, 192:192 + w], ACT.Exp).then_inc(self.sem("exp"), 1)
        act.wait_ge(self.sem("step"), 3)
        act.activation(ln, u, ACT.Ln).then_inc(self.sem("ln"), 1)

    def dve(self, dve):
        k, w = self.k, self.w
        e, u, ln, na, eq, num, den, x2 = (k.tmp[:, i * 64:i * 64 + w] for i in range(8))
        step = self.sem("step")
        self.join(dve)
        self.pre(dve, x2).then_inc(step, 1)
        dve.wait_ge(step, 1)
        dve.scalar_tensor_tensor(na, x2, -1.0, x2, ALU.mult, ALU.min).then_inc(step, 1)
        dve.wait_ge(self.sem("exp"), 1)
        dve.tensor_scalar(u, e, 1.0, None, ALU.add).then_inc(step, 1)
        dve.wait_ge(step, 3)
        dve.tensor_scalar(den, u, 1.0, None, ALU.subtract).then_inc(step, 1)
        dve.wait_ge(step, 4)
        dve.tensor_scalar(eq, den, 0.0, None, ALU.is_equal).then_inc(step, 1)
        dve.wait_ge(step, 5)
        dve.wait_ge(self.sem("ln"), 1)
        dve.tensor_tensor(num, ln, eq, ALU.add).then_inc(step, 1)
        dve.tensor_tensor(den, den, eq, ALU.add).then_inc(step, 1)
        dve.wait_ge(step, 7)
        dve.reciprocal(den, den).then_inc(step, 1)
        dve.wait_ge(step, 8)
        dve.tensor_tensor(num, num, den, ALU.mult).then_inc(step, 1)
        dve.wait_ge(step, 9)
        dve.tensor_tensor(num, num, e, ALU.mult).then_inc(step, 1)
        dve.wait_ge(step, 10)
        dve.scalar_tensor_tensor(self.out, x2, 0.0, num, ALU.max, ALU.add).then_inc(step, 1)


class Gates(Stage):

    def __init__(self, k, name, prev, sp, g8):
        super().__init__(k, name, prev)
        self.spf, self.g8 = sp, g8
        self.ends = [(self.sem("emt"), 1)]

    def pe(self, pe):
        k = self.k
        self.join(pe)
        for t in range(TT):
            pe.transpose(k.ps[0:MH, 4, t * P:(t + 1) * P], self.spf[:, t * MH:(t + 1) * MH], k.const(C_ID))
            tr = pe.transpose(k.ps[0:MH, 5, t * P:(t + 1) * P], self.g8[:, t * 8:t * 8 + MH], k.const(C_ID))
        tr.then_inc(self.sem("rows"), 1)
        pe.wait_ge(self.sem("scan"), 6)
        for t in range(TT):
            pe.transpose(k.ps[:, 6, t * MH:(t + 1) * MH], k.gr[0:MH, 2 * T + t * P:2 * T + (t + 1) * P],
                         k.const(C_ID)[0:MH, 0:MH])
            tr = pe.transpose(k.ps[:, 7, t * MH:(t + 1) * MH], k.gr[0:MH, t * P:(t + 1) * P],
                              k.const(C_ID)[0:MH, 0:MH])
        tr.then_inc(self.sem("cols"), 1)

    def dve(self, dve):
        k = self.k
        b, ig, a, m = (k.gr[0:MH, i * T:(i + 1) * T] for i in range(4))
        s = self.sem("scan")
        self.join(dve)
        dve.wait_ge(self.sem("rows"), 1)
        dve.tensor_copy(m, k.ps[0:MH, 4, :]).then_inc(s, 1)
        dve.wait_ge(s, 1)
        dve.tensor_tensor_scan(b, k.ones(MH, T), m, 0.0, ALU.mult, ALU.subtract).then_inc(s, 1)
        dve.wait_ge(s, 2)
        dve.tensor_tensor(a, k.ps[0:MH, 5, :], b, ALU.subtract).then_inc(s, 1)
        dve.wait_ge(s, 3)
        dve.tensor_tensor_scan(m, k.ones(MH, T), a, -BIG, ALU.mult, ALU.max).then_inc(s, 1)
        dve.wait_ge(s, 4)
        dve.tensor_tensor(ig, b, m, ALU.add).then_inc(s, 1)
        dve.wait_ge(s, 5)
        dve.tensor_scalar(b, ig, -1.0, 80.0, ALU.mult, ALU.min).then_inc(s, 1)
        dve.wait_ge(self.sem("cols"), 1)
        dve.tensor_copy(k.acol[:, 0:16], k.ps[:, 6, 0:16]).then_inc(self.sem("acol"), 1)

    def act(self, act):
        k = self.k
        act.wait_ge(self.sem("cols"), 1)
        act.wait_ge(self.sem("acol"), 1)
        act.activation(k.acol[:, 16:32], k.ps[:, 7, 0:16], ACT.Exp).then_inc(self.sem("emt"), 1)


class Mlstm(Stage):

    def __init__(self, k, name, prev, qk, v, mo, scr, sq, yt, yhi, ylo, ncol):
        super().__init__(k, name, prev)
        self.qk, self.v, self.mo, self.yhi, self.ylo, self.ncol = qk, v, mo, yhi, ylo, ncol
        self.tmp = k.at(f"{name}_gap", scr, 2 * T)
        self.e = k.at(f"{name}_decay", scr + 2 * T, 2 * T)
        self.pt = k.at(f"{name}_weighted", scr + 4 * T, TT * T)
        self.hn = k.at(f"{name}_h", scr + 4 * T + TT * T, MH * T)
        self.sq, self.yt = sq, yt
        self.ends = [(self.sem("lo"), MH), (self.sem("hi"), MH)]

    def num(self):
        return self.k.ps[:, 0:2, 0:2 * (MD + 1)].rearrange("p b (t d) -> p b t d", d=MD + 1)

    def pe(self, pe):
        k = self.k
        self.join(pe)
        for h in range(MH):
            if h >= 1:
                pe.wait_ge(self.sem("gap"), TT * h)
            pe.matmul(k.ps[:, 4, :], k.pick(h, MH), k.gr[0:MH, 3 * T:4 * T], start=True, stop=True)\
              .then_inc(self.sem("max"), 1)
            for s in range(TT):
                n = h * TT + s
                if n >= 2:
                    pe.wait_ge(self.sem("weighted"), n - 1)
                pe.matmul(k.ps[:, 5 + n % 2, s * P:T], self.qk[:, (4 + h) * T + s * P:(4 + h) * T + (s + 1) * P],
                          self.qk[:, h * T + s * P:(h + 1) * T], start=True, stop=True)\
                  .then_inc(self.sem("scores"), 1)
            pe.wait_ge(self.sem("weighted"), TT * (h + 1))
            if h >= 1:
                pe.wait_ge(self.sem("h"), h)
            for t in range(TT):
                for s in range(t + 1):
                    mm = pe.matmul(self.num()[:, t // 2, t % 2, :],
                                   self.pt[:, s * T + t * P:s * T + (t + 1) * P],
                                   self.v[:, (s * MH + h) * (MD + 1):(s * MH + h + 1) * (MD + 1)],
                                   start=s == 0, stop=s == t)
            mm.then_inc(self.sem("sums"), 1)
        pe.wait_ge(self.sem("normed"), 1)
        for h in range(MH):
            if h >= 2:
                pe.wait_ge(self.sem("yt"), h - 1)
            for t in range(TT):
                tr = pe.transpose(k.ps[:, 2 + h % 2, t * P:(t + 1) * P],
                                  self.hn[:, (h * TT + t) * P:(h * TT + t + 1) * P], k.const(C_ID))
            tr.then_inc(self.sem("fm"), 1)

    def dve(self, dve):
        k = self.k
        self.join(dve)
        st = k.stat
        step = self.sem("stat")
        ns = 0
        for h in range(MH):
            dve.wait_ge(self.sem("max"), h + 1)
            if h:
                dve.wait_ge(self.sem("ssq"), h)

            def gap(s):
                n = h * TT + s
                if n >= 2:
                    dve.wait_ge(self.sem("decay"), n - 1)
                t = self.tmp[:, n % 2 * T + s * P:(n % 2 + 1) * T]
                dve.tensor_scalar(t, k.ps[:, 4, s * P:T], k.acol[:, s * MH + h:s * MH + h + 1], 0.0,
                                  ALU.subtract, ALU.max).then_inc(self.sem("gap0"), 1)
                dve.wait_ge(self.sem("gap0"), n + 1)
                d = self.tmp[:, n % 2 * T + s * P:n % 2 * T + (s + 1) * P]
                dve.tensor_tensor(d, d, k.const(C_ST), ALU.add).then_inc(self.sem("gap"), 1)

            def weigh(s):
                n = h * TT + s
                if h >= 1 and s == 0:
                    dve.wait_ge(self.sem("sums"), h)
                dve.wait_ge(self.sem("scores"), n + 1)
                dve.wait_ge(self.sem("decay"), n + 1)
                dve.scalar_tensor_tensor(self.pt[:, s * T + s * P:(s + 1) * T], k.ps[:, 5 + n % 2, s * P:T],
                                         MD ** -0.5, self.e[:, n % 2 * T + s * P:(n % 2 + 1) * T],
                                         ALU.mult, ALU.mult).then_inc(self.sem("weighted"), 1)
            gap(0)
            for s in range(TT):
                if s + 1 < TT:
                    gap(s + 1)
                weigh(s)
            dve.wait_ge(self.sem("sums"), h + 1)
            num = self.num()
            den = st[:, h * TT:(h + 1) * TT]
            den4 = den.rearrange("p (b t) -> p b t", b=2)
            emt = k.acol[:, 16:32].rearrange("p (b t h) -> p b t h", b=2, h=MH)[:, :, :, h]
            dve.tensor_copy(den4, num[:, :, :, MD]).then_inc(step, 1)
            ns += 1
            dve.wait_ge(step, ns)
            dve.scalar_tensor_tensor(den4, den4, -1.0, den4, ALU.mult, ALU.max).then_inc(step, 1)
            ns += 1
            dve.wait_ge(step, ns)
            dve.tensor_tensor(den4, den4, emt, ALU.max).then_inc(step, 1)
            ns += 1
            dve.wait_ge(step, ns)
            dve.reciprocal(den, den).then_inc(step, 1)
            ns += 1
            dve.wait_ge(step, ns)
            hn = self.hn[:, h * T:(h + 1) * T].rearrange("p (b t d) -> p b t d", b=2, d=MD)
            dve.tensor_tensor(hn, num[:, :, :, 0:MD], den4.unsqueeze(3).broadcast_to([P, 2, 2, MD]),
                              ALU.mult).then_inc(self.sem("h"), 1)
            dve.wait_ge(self.sem("h"), h + 1)
            flat = self.hn[:, h * T:(h + 1) * T]
            dve.tensor_tensor(self.sq, flat, flat, ALU.mult).then_inc(step, 1)
            ns += 1
            dve.wait_ge(step, ns)
            dve.tensor_reduce(st[:, 16 + h * TT:16 + (h + 1) * TT],
                              self.sq.rearrange("p (t d) -> p t d", d=MD), AX.X, ALU.add)\
               .then_inc(self.sem("ssq"), 1)
        dve.wait_ge(self.sem("root"), 1)
        dve.reciprocal(st[:, 48:64], st[:, 32:48]).then_inc(step, 1)
        ns += 1
        dve.wait_ge(step, ns)
        hn = self.hn[:, :].rearrange("p (g d) -> p g d", d=MD)
        dve.tensor_tensor(hn, hn, st[:, 48:64].unsqueeze(2).broadcast_to([P, 16, MD]), ALU.mult)\
           .then_inc(self.sem("normed"), 1)
        for h in range(MH):
            y = self.yt[:, h * T:(h + 1) * T]
            dve.wait_ge(self.sem("fm"), h + 1)
            dve.scalar_tensor_tensor(y, k.ps[:, 2 + h % 2, :], k.col(self.ncol + h),
                                     self.mo[:, h * T:(h + 1) * T], ALU.mult, ALU.mult)\
               .then_inc(self.sem("yt"), 1)
        for h in range(MH):
            dve.wait_ge(self.sem("yt"), h + 1)
            dve.wait_ge(self.sem("hi"), h + 1)
            dve.tensor_tensor(self.ylo[:, h * T:(h + 1) * T], self.yt[:, h * T:(h + 1) * T],
                              self.yhi[:, h * T:(h + 1) * T], ALU.subtract).then_inc(self.sem("lo"), 1)

    def act(self, act):
        k = self.k
        self.join(act)
        for n in range(MH * TT):
            s = n % TT
            act.wait_ge(self.sem("gap"), n + 1)
            if n >= 2:
                act.wait_ge(self.sem("weighted"), n - 1)
            act.activation(self.e[:, n % 2 * T + s * P:(n % 2 + 1) * T],
                           self.tmp[:, n % 2 * T + s * P:(n % 2 + 1) * T], ACT.Exp, scale=-1.0)\
               .then_inc(self.sem("decay"), 1)
        act.wait_ge(self.sem("ssq"), MH)
        act.activation(k.stat[:, 32:48], k.stat[:, 16:32], ACT.Sqrt, bias=k.eps[:, 0:1], scale=1.0 / MD)\
           .then_inc(self.sem("root"), 1)
        for h in range(MH):
            act.wait_ge(self.sem("yt"), h + 1)
            act.activation(self.yhi[:, h * T:(h + 1) * T], self.yt[:, h * T:(h + 1) * T], ACT.Copy)\
               .then_inc(self.sem("hi"), 1)


class Branch(Stage):

    def __init__(self, k, name, prev, wgate, bcol, wup, kt, yh, yl, g, merged, add):
        super().__init__(k, name, prev)
        self.wgate, self.bcol, self.wup, self.kt = wgate, bcol, wup, kt
        self.yh, self.yl, self.g, self.merged, self.add = yh, yl, g, merged, add
        self.nup = 2 if kt == KD else 1
        self.n = 2 + self.nup
        self.u0 = units(k, 2 * self.n)
        self.ends = [(self.sem("merged" if add else "gated"), 8)]

    def sp(self, sp):
        for c in range(2):
            u = self.u0 + c * self.n
            for j in range(2):
                load_unit(self.k, sp, u + j, 0, self.wgate(c * 512 + j * UC), UC)
            for j in range(self.nup):
                w = 512 // self.nup
                load_unit(self.k, sp, u + 2 + j, 0, self.wup(c * 512 + j * w, w), w)

    def pe(self, pe):
        k = self.k
        self.join(pe)
        for c in range(2):
            u = self.u0 + c * self.n
            if c:
                pe.wait_ge(self.sem("gate"), 4)
            for j in range(2):
                pe.wait_ge(k.split, u + j + 1)
                fm_unit(k, pe, u + j, KD, UC, k.hh, k.hl, [k.ps[:, 2 * j + i, :] for i in range(2)])\
                    .then_inc(k.unit_used, 1)
            if c:
                pe.wait_ge(self.sem("gated"), 4)
            for j in range(self.nup):
                w = 512 // self.nup
                pe.wait_ge(k.split, u + 2 + j + 1)
                fm_unit(k, pe, u + 2 + j, self.kt, w, self.yh, self.yl,
                        [k.ps[:, 4 + j * (w // P) + i, :] for i in range(w // P)])\
                    .then_inc(k.unit_used, 1)

    def act(self, act):
        k = self.k
        self.join(act)
        for c in range(2):
            u = self.u0 + c * self.n
            for j in range(2):
                act.wait_ge(k.unit_used, u + j + 1)
                for i in range(2):
                    t = 2 * j + i
                    if c:
                        act.wait_ge(self.sem("gated"), t + 1)
                        if self.add:
                            act.wait_ge(self.sem("merged"), t + 1)
                    act.activation(self.g[:, t * T:(t + 1) * T], k.ps[:, t, :], ACT.Sigmoid,
                                   bias=k.col(self.bcol + 4 * c + t) if self.bcol is not None else 0.0)\
                       .then_inc(self.sem("gate"), 1)
                hi_unit(k, act, u + j + 2, 0)
            for j in range(self.nup):
                hi_unit(k, act, u + 2 + j + 2, 0)

    def dve(self, dve):
        k = self.k
        self.join(dve)
        for c in range(2):
            u = self.u0 + c * self.n
            dve.wait_ge(k.unit_used, u + self.n)
            for t in range(4):
                g = self.g[:, t * T:(t + 1) * T]
                m = self.merged[:, (4 * c + t) * T:(4 * c + t + 1) * T]
                dve.wait_ge(self.sem("gate"), 4 * c + t + 1)
                ins = dve.tensor_tensor(g if self.add else m, g, k.ps[:, 4 + t, :], ALU.mult)
                ins.then_inc(self.sem("gated"), 1)
            for t in range(4):
                if self.add:
                    g = self.g[:, t * T:(t + 1) * T]
                    m = self.merged[:, (4 * c + t) * T:(4 * c + t + 1) * T]
                    dve.wait_ge(self.sem("gated"), 4 * c + t + 1)
                    dve.tensor_tensor(m, m, g, ALU.add).then_inc(self.sem("merged"), 1)


class Split(Stage):

    def __init__(self, k, name, prev, x, hi, lo, n):
        super().__init__(k, name, prev)
        self.x, self.hi, self.lo, self.n = x, hi, lo, n
        self.ends = [(self.sem("lo"), n)]

    def act(self, act):
        self.join(act)
        for t in range(self.n):
            act.activation(self.hi[:, t * T:(t + 1) * T], self.x[:, t * T:(t + 1) * T], ACT.Copy)\
               .then_inc(self.sem("hi"), 1)

    def dve(self, dve):
        self.join(dve)
        for t in range(self.n):
            dve.wait_ge(self.sem("hi"), t + 1)
            dve.tensor_tensor(self.lo[:, t * T:(t + 1) * T], self.x[:, t * T:(t + 1) * T],
                              self.hi[:, t * T:(t + 1) * T], ALU.subtract).then_inc(self.sem("lo"), 1)


class OutProj(Stage):

    def __init__(self, k, name, prev, w, xh, xl):
        super().__init__(k, name, prev)
        self.w, self.xh, self.xl = w, xh, xl
        self.u0 = units(k, 4)
        self.ends = [(self.sem("added"), 8)]

    def sp(self, sp):
        for j in range(4):
            load_unit(self.k, sp, self.u0 + j, 0, self.w(j * UC, UC), UC)

    def pe(self, pe):
        k = self.k
        self.join(pe)
        for j in range(4):
            pe.wait_ge(k.split, self.u0 + j + 1)
            fm_unit(k, pe, self.u0 + j, KD, UC, self.xh, self.xl, [k.ps[:, 2 * j + i, :] for i in range(2)])\
                .then_inc(k.unit_used, 1)

    def act(self, act):
        for j in range(4):
            hi_unit(self.k, act, self.u0 + j + 2, 0)

    def dve(self, dve):
        k = self.k
        self.join(dve)
        for j in range(4):
            dve.wait_ge(k.unit_used, self.u0 + j + 1)
            for c in range(2 * j, 2 * j + 2):
                x = k.xT[:, c * T:(c + 1) * T]
                dve.tensor_tensor(x, x, k.ps[:, c, :], ALU.add).then_inc(self.sem("added"), 1)


class Up(Stage):

    def __init__(self, k, name, prev, src, n, fhi, flo, scr):
        super().__init__(k, name, prev)
        self.src, self.n, self.fhi, self.flo = src, n, fhi, flo
        self.r = scr[0]
        self.f = scr[1]
        self.u0 = units(k, n)
        self.ends = [(self.sem("lo"), n), (self.sem("hi"), n)]

    def sp(self, sp):
        with sp.Fori(0, self.n // 2) as i:
            for j in range(2):
                load_unit(self.k, sp, self.u0 + j, i * 2, self.src(j, i * 2), UC)

    def pe(self, pe):
        k = self.k
        self.join(pe)

        def unit(j, du):
            pe.wait_ge(k.split, du + (self.u0 + j + 1))
            if not (isinstance(du, int) and du + j < 2):
                pe.wait_ge(self.sem("r"), du + (j - 1))
            fm_unit(k, pe, self.u0 + j, KD, UC, k.hh, k.hl, [k.ps[:, 2 * j + c, :] for c in range(2)])\
                .then_inc(k.unit_used, 1)
        unit(0, 0)
        unit(1, 0)
        with pe.Fori(1, self.n // 2) as i:
            unit(0, i * 2)
            unit(1, i * 2)

    def out(self, x, j, du):
        w = UT * T
        return x[:, bass.ds(du * w + j * w, w)]

    def act(self, act):
        k = self.k
        self.join(act)

        def unit(j, du):
            w = UT * T
            r, f = self.r[:, j * w:(j + 1) * w], self.f[:, j * w:(j + 1) * w]
            act.wait_ge(k.unit_used, du + (self.u0 + j + 1))
            if not (isinstance(du, int) and du + j < 2):
                act.wait_ge(self.sem("f"), du + (j - 1))
            act.activation(r, k.ps[:, 2 * j:2 * j + 2, :].rearrange("p a b -> p (a b)"), ACT.Relu)\
               .then_inc(self.sem("r"), 1)
            hi_unit(k, act, self.u0 + j + 2, du)
            act.wait_ge(self.sem("f"), du + (j + 1))
            act.activation(self.out(self.fhi, j, du), f, ACT.Copy).then_inc(self.sem("hi"), 1)
        unit(0, 0)
        unit(1, 0)
        with act.Fori(1, self.n // 2) as i:
            unit(0, i * 2)
            unit(1, i * 2)

    def dve(self, dve):
        k = self.k
        self.join(dve)

        def unit(j, du):
            w = UT * T
            r, f = self.r[:, j * w:(j + 1) * w], self.f[:, j * w:(j + 1) * w]
            dve.wait_ge(self.sem("r"), du + (j + 1))
            if not (isinstance(du, int) and du + j < 2):
                dve.wait_ge(self.sem("hi"), du + (j - 1))
            dve.tensor_tensor(f, r, r, ALU.mult).then_inc(self.sem("f"), 1)
            dve.wait_ge(self.sem("hi"), du + (j + 1))
            dve.tensor_tensor(self.out(self.flo, j, du), f, self.out(self.fhi, j, du), ALU.subtract)\
               .then_inc(self.sem("lo"), 1)
        unit(0, 0)
        unit(1, 0)
        with dve.Fori(1, self.n // 2) as i:
            unit(0, i * 2)
            unit(1, i * 2)


class Glu(Stage):

    def __init__(self, k, name, prev, src, n, fhi, flo, scr):
        super().__init__(k, name, prev)
        self.src, self.n, self.fhi, self.flo = src, n, fhi, flo
        self.r, self.f = scr[0][:, :], scr[1][:, :]
        self.u0 = units(k, 2 * n)
        self.ends = [(self.sem("lo"), n), (self.sem("hi"), n)]

    def pairs(self, eng, body):
        body(0)
        with eng.Fori(1, self.n) as i:
            body(i)

    def sp(self, sp):
        with sp.Fori(0, self.n) as i:
            for j in range(2):
                load_unit(self.k, sp, self.u0 + j, i * 2, self.src(j, i), UC)

    def pe(self, pe):
        k = self.k
        self.join(pe)

        def pair(i):
            for j in range(2):
                pe.wait_ge(k.split, i * 2 + (self.u0 + j + 1))
                if not isinstance(i, int):
                    pe.wait_ge(self.sem("f" if j else "silu"), i)
                fm_unit(k, pe, self.u0 + j, KD, UC, k.hh, k.hl, [k.ps[:, 2 * j + c, :] for c in range(2)])\
                    .then_inc(k.unit_used, 1)
        self.pairs(pe, pair)

    def tiles(self, x, i):
        return x[:, bass.ds(i * (2 * T), 2 * T)]

    def act(self, act):
        k = self.k
        self.join(act)

        def pair(i):
            act.wait_ge(k.unit_used, i * 2 + (self.u0 + 1))
            if not isinstance(i, int):
                act.wait_ge(self.sem("f"), i)
            act.activation(self.r, k.ps[:, 0:2, :].rearrange("p a b -> p (a b)"), ACT.Silu)\
               .then_inc(self.sem("silu"), 1)
            hi_unit(k, act, self.u0 + 2, i * 2)
            hi_unit(k, act, self.u0 + 3, i * 2)
            act.wait_ge(self.sem("f"), i + 1)
            act.activation(self.tiles(self.fhi, i), self.f, ACT.Copy).then_inc(self.sem("hi"), 1)
        self.pairs(act, pair)

    def dve(self, dve):
        k = self.k
        self.join(dve)

        def pair(i):
            dve.wait_ge(self.sem("silu"), i + 1)
            dve.wait_ge(k.unit_used, i * 2 + (self.u0 + 2))
            if not isinstance(i, int):
                dve.wait_ge(self.sem("hi"), i)
                dve.wait_ge(self.sem("lo"), i)
            dve.tensor_tensor(self.f, self.r, k.ps[:, 2:4, :].rearrange("p a b -> p (a b)"), ALU.mult)\
               .then_inc(self.sem("f"), 1)
            dve.wait_ge(self.sem("hi"), i + 1)
            dve.tensor_tensor(self.tiles(self.flo, i), self.f, self.tiles(self.fhi, i), ALU.subtract)\
               .then_inc(self.sem("lo"), 1)
        self.pairs(dve, pair)


class Down(Stage):

    def __init__(self, k, name, prev, src, n, fhi, flo, last=False):
        super().__init__(k, name, prev)
        self.src, self.n, self.fhi, self.flo, self.last = src, n, fhi, flo, last
        self.u0 = units(k, n)
        self.ends = [(self.sem("added"), 8)]

    def sp(self, sp):
        k = self.k
        with sp.Fori(0, self.n // 2) as i:
            for j in range(2):
                load_unit(k, sp, self.u0 + j, i * 2, self.src(j, i * 2), D)
        if self.n % 2:
            load_unit(k, sp, self.u0 + self.n - 1, 0, self.src(0, self.n - 1), D)

    def pe(self, pe):
        k = self.k
        self.join(pe)

        def unit(j, du, first=False, last=False):
            a = k.slot(self.u0 + j) * SLOT
            pe.wait_ge(k.split, du + (self.u0 + j + 1))
            for c in range(KD):
                for i in range(2):
                    w = slice(a + i * D + c * P, a + i * D + (c + 1) * P)
                    x = bass.ds(du * (2 * T) + (j * 2 + i) * T, T)
                    pe.matmul(k.ps[:, c, :], k.whi[:, w], self.fhi[:, x], start=first and i == 0,
                              stop=False, skip_group_check=True)
                    pe.matmul(k.ps[:, c, :], k.whi[:, w], self.flo[:, x], start=False, stop=False,
                              skip_group_check=True)
                    mm = pe.matmul(k.ps[:, c, :], k.wlo[:, w], self.fhi[:, x], start=False,
                                   stop=last and i == 1, skip_group_check=True)
            mm.then_inc(k.unit_used, 1)
        odd = self.n % 2
        unit(0, 0, first=True)
        unit(1, 0)
        end = self.n - 1 if odd else self.n - 2
        with pe.Fori(1, end // 2) as i:
            unit(0, i * 2)
            unit(1, i * 2)
        if odd:
            unit(0, self.n - 1, last=True)
        else:
            unit(0, self.n - 2)
            unit(1, self.n - 2, last=True)

    def act(self, act):
        k = self.k
        n = self.n - 2 if self.last else self.n
        with act.Fori(0, n // 2) as i:
            for j in range(2):
                hi_unit(k, act, self.u0 + j + 2, i * 2)
        if n % 2:
            hi_unit(k, act, self.u0 + n - 1 + 2, 0)

    def dve(self, dve):
        k = self.k
        self.join(dve)
        dve.wait_ge(k.unit_used, self.u0 + self.n)
        for c in range(KD):
            x = k.xT[:, c * T:(c + 1) * T]
            dve.tensor_tensor(x, x, k.ps[:, c, :], ALU.add).then_inc(self.sem("added"), 1)


class Params(Stage):

    def __init__(self, k, name, prev, rows, bcasts, prow):
        super().__init__(k, name, prev)
        self.rows, self.bcasts = rows, bcasts
        self.n = rows[-1][1] + rows[-1][2]
        self.prow = prow
        self.ends = [(self.sem("cols"), 1), (self.sem("landed"), 16 * (len(rows) + len(bcasts)))]

    def sp(self, sp):
        self.join(sp)
        for src, r, n in self.rows:
            sp.dma_start(self.prow[r:r + n, :], src).then_inc(self.sem("landed"), 16)
        for dst, src in self.bcasts:
            sp.dma_start(dst, src).then_inc(self.sem("landed"), 16)

    def pe(self, pe):
        k = self.k
        self.join(pe)
        pe.wait_ge(self.sem("landed"), 16 * (len(self.rows) + len(self.bcasts)))
        pe.transpose(k.ps[:, 7, 0:self.n], self.prow[0:self.n, :], k.const(C_ID)[0:self.n, 0:self.n])\
          .then_inc(self.sem("turned"), 1)

    def dve(self, dve):
        k = self.k
        self.join(dve)
        dve.wait_ge(self.sem("turned"), 1)
        dve.tensor_copy(k.pcol[:, 0:self.n], k.ps[:, 7, 0:self.n]).then_inc(self.sem("cols"), 1)


class Fill(Stage):

    def __init__(self, k, name, prev, fills):
        super().__init__(k, name, prev)
        self.fills = fills
        self.ends = [(self.sem("filled"), len(fills))]

    def dve(self, dve):
        self.join(dve)
        for ap, value in self.fills:
            dve.memset(ap, value).then_inc(self.sem("filled"), 1)


class Setup(Stage):

    def __init__(self, k, name, prev, x, positions, table):
        super().__init__(k, name, prev)
        self.x, self.positions, self.table = x, positions, table
        self.xtm = k.at("setup_x", 0, TT * D)
        self.posi = k.at("setup_positions", TT * D, T, I32)
        self.w = [k.at(f"setup_w{i}", TT * D + (i + 1) * T, T) for i in range(4)]
        self.ends = [(self.sem("fm_act"), 4), (self.sem("fm_dve"), 4), (self.sem("step"), 18),
                     (self.sem("sines"), 2)]

    def sp(self, sp):
        sp.dma_start(self.k.cst[:, :], self.table).then_inc(self.sem("table"), 16)
        sp.dma_start(self.xtm[:, :].rearrange("p (t d) -> p t d", d=D),
                     self.x[0].rearrange("(t p) d -> p t d", p=P)).then_inc(self.sem("x"), 16)
        sp.dma_start(self.posi[:, :], self.positions.broadcast_to([P, T])).then_inc(self.sem("pos"), 16)

    def pe(self, pe):
        k = self.k
        pe.wait_ge(self.sem("table"), 16)
        pe.wait_ge(self.sem("x"), 16)
        for c in range(KD):
            for t in range(TT):
                tr = pe.transpose(k.ps[:, c, t * P:(t + 1) * P],
                                  self.xtm[:, t * D + c * P:t * D + (c + 1) * P], k.const(C_ID))
            tr.then_inc(self.sem("turned"), 1)

    def act(self, act):
        k = self.k
        for c in range(0, KD, 2):
            act.wait_ge(self.sem("turned"), c + 1)
            act.activation(k.xT[:, c * T:(c + 1) * T], k.ps[:, c, :], ACT.Copy).then_inc(self.sem("fm_act"), 1)
        act.wait_ge(self.sem("step"), 17)
        act.activation(k.sin[:, :], self.w[2][:, :], ACT.Sin).then_inc(self.sem("sines"), 1)
        act.activation(k.cos[:, :], self.w[3][:, :], ACT.Sin).then_inc(self.sem("sines"), 1)

    def dve(self, dve):
        k = self.k
        step = self.sem("step")
        done = 0

        def then(ins):
            nonlocal done
            done += 1
            ins.then_inc(step, 1)
            dve.wait_ge(step, done)
        dve.wait_ge(self.sem("table"), 16)
        dve.wait_ge(self.sem("pos"), 16)
        then(dve.memset(k.eps[:, :], EPS))
        pos, ang, rs, rc = (w[:, :] for w in self.w)
        then(dve.tensor_copy(pos, self.posi[:, :]))
        then(dve.tensor_scalar(ang, pos, k.cst[:, C_INV:C_INV + 1], None, ALU.mult))
        magic = 1.5 * 2 ** 23
        two_pi = 2 * math.pi
        hi = 6.28125
        for out, turn, shift in ((rs, 0.0, 0.0), (rc, 0.25, math.pi / 2)):
            then(dve.tensor_scalar(pos, ang, 1 / two_pi, turn, ALU.mult, ALU.add))
            then(dve.tensor_scalar(pos, pos, magic, None, ALU.add))
            then(dve.tensor_scalar(pos, pos, magic, None, ALU.subtract))
            then(dve.scalar_tensor_tensor(out, pos, -hi, ang, ALU.mult, ALU.add))
            then(dve.scalar_tensor_tensor(out, pos, -(two_pi - hi), out, ALU.mult, ALU.add))
            lim = 3.1415925
            then(dve.tensor_scalar(out, out, shift, lim, ALU.add, ALU.min))
            then(dve.tensor_scalar(out, out, -lim, None, ALU.max))
        for c in range(1, KD, 2):
            dve.wait_ge(self.sem("turned"), c + 1)
            dve.tensor_copy(k.xT[:, c * T:(c + 1) * T], k.ps[:, c, :]).then_inc(self.sem("fm_dve"), 1)
        dve.wait_ge(self.sem("sines"), 2)
        dve.tensor_scalar(k.cos[:, :], k.cos[:, :], k.cst[:, C_MSK:C_MSK + 1], k.cst[:, C_UNM:C_UNM + 1],
                          ALU.mult, ALU.add).then_inc(step, 1)


class SsdPrep(Stage):

    def __init__(self, k, name, prev, c, xs, bt, cb, rows, s):
        super().__init__(k, name, prev)
        self.c, self.xs, self.bt, self.cb, self.rows, self.s = c, xs, bt, cb, rows, s
        self.ends = [(self.sem("tm_act"), 5), (self.sem("tm_dve"), 5), (self.sem("step"), 10),
                     (self.sem("exps"), 4), (self.sem("cb"), 2)]

    def pe(self, pe):
        k = self.k
        self.join(pe)
        for c in range(10):
            if c >= 4:
                pe.wait_ge(self.sem("tm_act" if c % 2 == 0 else "tm_dve"), (c - 4) // 2 + 1)
            for t in range(TT):
                tr = pe.transpose(k.ps[:, c % 4, t * P:(t + 1) * P],
                                  self.c[:, c * T + t * P:c * T + (t + 1) * P], k.const(C_ID))
            tr.then_inc(self.sem("turned"), 1)
        for g in range(SG):
            for t in range(TT):
                a = slice((8 + g) * T + t * P, (8 + g) * T + (t + 1) * P)
                b = slice((10 + g) * T + t * P, (10 + g) * T + (t + 1) * P)
                mm = pe.matmul(k.ps[:, 4 + g, t * P:(t + 1) * P], self.c[:, a], self.c[:, b],
                               start=True, stop=True)
            mm.then_inc(self.sem("products"), 1)
        pe.wait_ge(self.sem("step"), 1)
        for t in range(TT):
            tr = pe.transpose(k.ps[0:SH, 6, t * P:(t + 1) * P], self.s["a"][:, t * SH:(t + 1) * SH],
                              k.const(C_ID))
        tr.then_inc(self.sem("arows"), 1)
        pe.wait_ge(self.sem("step"), 6)
        for t in range(TT):
            tr = pe.transpose(k.ps[:, 7, t * SH:(t + 1) * SH], self.rows[0:SH, T + t * P:T + (t + 1) * P],
                              k.const(C_ID)[0:SH, 0:SH])
        tr.then_inc(self.sem("cols"), 1)
        pe.wait_ge(self.sem("step"), 7)
        last = k.cst[:, C_ID + P - 1:C_ID + P].broadcast_to([P, P])
        pe.matmul(k.ps[:, 6, 0:TT * SH], last, self.s["loc"], start=True, stop=True)\
          .then_inc(self.sem("total"), 1)

    def tm(self, c):
        if c < 8:
            return self.xs[:, :].rearrange("p (t f) -> p t f", t=TT)[:, :, c * P:(c + 1) * P]
        return self.bt[:, :].rearrange("p (t f) -> p t f", t=TT)[:, :, (c - 8) * P:(c - 7) * P]

    def act(self, act):
        k = self.k
        self.join(act)
        act.activation(self.s["A"], self.s["a_log"], ACT.Exp).then_inc(self.sem("exps"), 1)
        for c in range(0, 10, 2):
            act.wait_ge(self.sem("turned"), c + 1)
            act.activation(self.tm(c), k.ps[:, c % 4, :].rearrange("p (t f) -> p t f", t=TT), ACT.Copy)\
               .then_inc(self.sem("tm_act"), 1)
        act.wait_ge(self.sem("step"), 9)
        act.activation(self.s["eloc"], self.s["loc"], ACT.Exp).then_inc(self.sem("exps"), 1)
        act.activation(self.s["etot"], self.s["tot"], ACT.Exp).then_inc(self.sem("exps"), 1)
        act.activation(self.s["dec"], self.s["dec"], ACT.Exp).then_inc(self.sem("exps"), 1)

    def dve(self, dve):
        k, s = self.k, self.s
        step = self.sem("step")
        self.join(dve)
        dve.wait_ge(self.sem("exps"), 1)
        h16 = lambda x: x.rearrange("p (t h) -> p t h", h=SH)
        dve.scalar_tensor_tensor(h16(s["a"]), h16(s["dt"]), -1.0,
                                 s["A"].unsqueeze(1).broadcast_to([P, TT, SH]), ALU.mult, ALU.mult)\
           .then_inc(step, 1)
        for c in range(1, 10, 2):
            dve.wait_ge(self.sem("turned"), c + 1)
            dve.tensor_copy(self.tm(c), k.ps[:, c % 4, :].rearrange("p (t f) -> p t f", t=TT))\
               .then_inc(self.sem("tm_dve"), 1)
        for g in range(SG):
            dve.wait_ge(self.sem("products"), g + 1)
            dve.tensor_tensor(self.cb[:, g * T:(g + 1) * T].rearrange("p (t f) -> p t f", f=P),
                              k.ps[:, 4 + g, :].rearrange("p (t f) -> p t f", f=P),
                              k.const(C_KEEP).unsqueeze(1).broadcast_to([P, TT, P]), ALU.mult)\
               .then_inc(self.sem("cb"), 1)
        dve.wait_ge(self.sem("arows"), 1)
        dve.tensor_copy(self.rows[0:SH, 0:T], k.ps[0:SH, 6, :]).then_inc(step, 1)
        dve.wait_ge(step, 2)
        for t in range(TT):
            dve.tensor_tensor_scan(self.rows[0:SH, T + t * P:T + (t + 1) * P], k.ones(SH, P),
                                   self.rows[0:SH, t * P:(t + 1) * P], 0.0, ALU.mult, ALU.add)\
               .then_inc(step, 1)
        dve.wait_ge(self.sem("cols"), 1)
        dve.tensor_copy(s["loc"], k.ps[:, 7, 0:TT * SH]).then_inc(step, 1)
        dve.wait_ge(self.sem("total"), 1)
        dve.tensor_copy(s["tot"], k.ps[:, 6, 0:TT * SH]).then_inc(step, 1)
        dve.wait_ge(step, 8)
        dve.tensor_tensor(s["dec"], s["tot"], s["loc"], ALU.subtract).then_inc(step, 1)
        dve.wait_ge(self.sem("exps"), 4)
        dve.tensor_tensor(s["dtdec"], s["dt"], s["dec"], ALU.mult).then_inc(step, 1)


class Ssd(Stage):

    def __init__(self, k, name, prev, c, xs, bt, cb, rows, s, sz, scr):
        super().__init__(k, name, prev)
        self.c, self.xs, self.bt, self.cb, self.rows, self.s, self.sz = c, xs, bt, cb, rows, s, sz
        self.xdt = k.at(f"{name}_xdt", scr, D)
        self.xdd = k.at(f"{name}_xdecayed", scr + D, D)
        self.e = k.at(f"{name}_decay", scr + 2 * D, 2 * D)
        self.state = k.at(f"{name}_state", scr + 4 * D, D)
        self.y = k.at(f"{name}_y", scr + 5 * D, D)
        self.ends = [(self.sem("normed"), TT)]

    def pe(self, pe):
        k = self.k
        self.join(pe)
        for t in range(TT):
            tok = slice(t * P, (t + 1) * P)
            if t:
                pe.wait_ge(self.sem("state"), t)
                pe.wait_ge(self.sem("gap"), t)
            for h in range(SH):
                mm = pe.matmul(k.ps[:, h // 4, h % 4 * P:(h % 4 + 1) * P], k.pick(h, SH),
                               self.rows[0:SH, T + t * P:T + (t + 1) * P], start=True, stop=True)
            mm.then_inc(self.sem("sums"), 1)
            if t > 1:
                pe.wait_ge(self.sem("off"), t - 1)
            if t:
                for g in range(SG):
                    mm = pe.matmul(k.ps[:, 6 + g, :], self.c[:, (10 + g) * T + t * P:(10 + g) * T + (t + 1) * P],
                                   self.state[:, g * 512:(g + 1) * 512], start=True, stop=True)
                mm.then_inc(self.sem("across"), 1)
            if t < TT - 1:
                pe.wait_ge(self.sem("gap"), t + 1)
                pe.wait_ge(self.sem("xdd"), t + 1)
                for g in range(SG):
                    mm = pe.matmul(k.ps[:, g, :], self.bt[:, t * 256 + g * P:t * 256 + (g + 1) * P],
                                   self.xdd[:, g * 512:(g + 1) * 512], start=True, stop=True)
                mm.then_inc(self.sem("states"), 1)
            pe.wait_ge(self.sem("weighted"), 2 * (t + 1))
            if t:
                pe.wait_ge(self.sem("within_read"), t)
            for h in range(SH):
                mm = pe.matmul(k.ps[:, 4 + h // 8, h % 8 * SHD:(h % 8 + 1) * SHD],
                               self.e[:, h * P:(h + 1) * P], self.xdt[:, h * SHD:(h + 1) * SHD],
                               start=True, stop=True)
            mm.then_inc(self.sem("within"), 1)

    def dve(self, dve):
        k, s = self.k, self.s
        self.join(dve)
        hd = lambda x: x.rearrange("p (h d) -> p h d", d=SHD)
        bank = lambda b: k.ps[:, b:b + 2, :].rearrange("p b (h d) -> p (b h) d", d=SHD)
        per_head = lambda x, t, w: x[:, t * SH:(t + 1) * SH].unsqueeze(2).broadcast_to([P, SH, w])
        y, xdt = hd(self.y[:, :]), hd(self.xdt[:, :])
        local = self.sem("local")
        n = 0
        for t in range(TT):
            x = hd(self.xs[:, t * D:(t + 1) * D])
            dve.wait_ge(self.sem("sums"), t + 1)
            e = self.e[:, :].rearrange("p (h t) -> p h t", t=P)
            dve.tensor_tensor(e, k.ps[:, 0:4, :].rearrange("p b (h t) -> p (b h) t", t=P),
                              per_head(s["loc"], t, P), ALU.subtract).then_inc(self.sem("gap"), 1)
            dve.wait_ge(self.sem("gap"), t + 1)
            dve.tensor_scalar(self.e[:, :], self.e[:, :], 0.0, None, ALU.min).then_inc(self.sem("min"), 1)
            if t:
                dve.wait_ge(self.sem("states"), t)
            dve.tensor_tensor(hd(self.xdd[:, :]), x, per_head(s["dtdec"], t, SHD), ALU.mult)\
               .then_inc(self.sem("xdd"), 1)
            dve.tensor_tensor(xdt, x, per_head(s["dt"], t, SHD), ALU.mult).then_inc(self.sem("xdt"), 1)
            dve.wait_ge(self.sem("exp"), t + 1)
            dve.wait_ge(self.sem("xdt"), t + 1)
            for g in range(SG):
                eg = self.e[:, g * D:(g + 1) * D].rearrange("p (h t) -> p h t", t=P)
                cb = self.cb[:, g * T + t * P:g * T + (t + 1) * P].unsqueeze(1).broadcast_to([P, SPG, P])
                dve.tensor_tensor(eg, eg, cb, ALU.mult).then_inc(self.sem("weighted"), 1)
            if t:
                dve.wait_ge(self.sem("across"), t)
                dve.wait_ge(self.sem("square"), t)
                dve.tensor_tensor(y, bank(6), per_head(s["eloc"], t, SHD), ALU.mult)\
                   .then_inc(self.sem("off"), 1)
            if t < TT - 1:
                st = hd(self.state[:, :])
                if t:
                    dve.tensor_tensor(st, st, per_head(s["etot"], t, SHD), ALU.mult)\
                       .then_inc(self.sem("aged"), 1)
                    dve.wait_ge(self.sem("aged"), t)
                dve.wait_ge(self.sem("states"), t + 1)
                if t:
                    dve.tensor_tensor(st, st, bank(0), ALU.add).then_inc(self.sem("state"), 1)
                else:
                    dve.tensor_copy(st, bank(0)).then_inc(self.sem("state"), 1)
            dve.wait_ge(self.sem("within"), t + 1)
            if t:
                dve.wait_ge(self.sem("off"), t)
                dve.tensor_tensor(y, y, bank(4), ALU.add).then_inc(self.sem("within_read"), 1)
            else:
                dve.tensor_copy(y, bank(4)).then_inc(self.sem("within_read"), 1)
            dve.tensor_tensor(xdt, x, s["D"].unsqueeze(2).broadcast_to([P, SH, SHD]), ALU.mult)\
               .then_inc(local, 1)
            n += 1
            dve.wait_ge(local, n)
            dve.wait_ge(self.sem("within_read"), t + 1)
            dve.tensor_tensor(y, y, xdt, ALU.add).then_inc(local, 1)
            n += 1
            dve.wait_ge(local, n)
            z = self.sz[:, t * D:(t + 1) * D]
            dve.tensor_tensor(z, z, self.y[:, :], ALU.mult).then_inc(self.sem("gated"), 1)
        dve.wait_ge(self.sem("root"), 1)
        dve.reciprocal(k.stat[:, 8:12], k.stat[:, 4:8]).then_inc(local, 1)
        dve.wait_ge(local, n + 1)
        for t in range(TT):
            z = self.sz[:, t * D:(t + 1) * D]
            dve.tensor_scalar(z, z, k.stat[:, 8 + t:9 + t], None, ALU.mult).then_inc(self.sem("normed"), 1)

    def act(self, act):
        k = self.k
        self.join(act)
        for t in range(TT):
            act.wait_ge(self.sem("min"), t + 1)
            act.activation(self.e[:, :], self.e[:, :], ACT.Exp).then_inc(self.sem("exp"), 1)
            act.wait_ge(self.sem("gated"), t + 1)
            act.activation(self.y[:, :], self.sz[:, t * D:(t + 1) * D], ACT.Square,
                           accum_out=k.stat[:, t:t + 1]).then_inc(self.sem("square"), 1)
        act.wait_ge(self.sem("square"), TT)
        act.activation(k.stat[:, 4:8], k.stat[:, 0:4], ACT.Sqrt, bias=k.eps[:, 0:1], scale=1.0 / D)\
           .then_inc(self.sem("root"), 1)


class SsdOut(Stage):

    def __init__(self, k, name, prev, y, wcol, yhi, ylo):
        super().__init__(k, name, prev)
        self.y, self.wcol, self.yhi, self.ylo = y, wcol, yhi, ylo
        self.ends = [(self.sem("lo"), KD)]

    def pe(self, pe):
        k = self.k
        self.join(pe)
        for c in range(KD):
            for t in range(TT):
                tr = pe.transpose(k.ps[:, c, t * P:(t + 1) * P], self.y[:, t * D + c * P:t * D + (c + 1) * P],
                                  k.const(C_ID))
            tr.then_inc(self.sem("turned"), 1)

    def act(self, act):
        k = self.k
        self.join(act)
        for c in range(KD):
            act.wait_ge(self.sem("turned"), c + 1)
            act.activation(self.yhi[:, c * T:(c + 1) * T], k.ps[:, c, :], ACT.Copy,
                           scale=k.col(self.wcol + c)).then_inc(self.sem("hi"), 1)

    def dve(self, dve):
        k = self.k
        self.join(dve)
        for c in range(KD):
            dve.wait_ge(self.sem("hi"), c + 1)
            dve.scalar_tensor_tensor(self.ylo[:, c * T:(c + 1) * T], k.ps[:, c, :], k.col(self.wcol + c),
                                     self.yhi[:, c * T:(c + 1) * T], ALU.mult, ALU.subtract)\
               .then_inc(self.sem("lo"), 1)


class PoolMix(Stage):

    def __init__(self, k, name, prev, u, a, b, pooled, wsrc, w, scol, yhi, ylo):
        super().__init__(k, name, prev)
        self.u, self.ab, self.pooled, self.wsrc, self.w = u, (a, b), pooled, wsrc, w
        self.scol, self.yhi, self.ylo = scol, yhi, ylo
        self.ends = [(self.sem("lo"), len(WINDOWS))]

    def pe(self, pe):
        k = self.k
        self.join(pe)
        for g in range(len(WINDOWS)):
            pe.wait_ge(self.sem("pooled"), g + 1)
            if g == 0:
                pe.wait_ge(self.sem("weights"), 16)
            pe.matmul(k.ps[:, 4 + g, :], self.w[:, g * P:(g + 1) * P], self.pooled[:, g * T:(g + 1) * T],
                      start=True, stop=True).then_inc(self.sem("mixed"), 1)

    def act(self, act):
        k = self.k
        self.join(act)
        act.dma_start(self.w[:, :].rearrange("p (g d) -> p g d", d=P), self.wsrc).then_inc(self.sem("weights"), 16)
        for g in range(len(WINDOWS)):
            act.wait_ge(self.sem("mixed"), g + 1)
            act.activation(self.yhi[:, g * T:(g + 1) * T], k.ps[:, 4 + g, :], ACT.Copy,
                           scale=k.col(self.scol + g)).then_inc(self.sem("hi"), 1)

    def dve(self, dve):
        k = self.k
        self.join(dve)
        step = self.sem("step")
        n, pad = 0, 16
        for g, win in enumerate(WINDOWS):
            tile = self.u[:, g * (T + pad):(g + 1) * (T + pad)]
            src, shift, side = tile, 1, 0
            if g:
                dve.wait_ge(self.sem("pooled"), g)
            while shift < win:
                dst = self.ab[side][:, :]
                dve.tensor_tensor(dst[:, pad:], src[:, pad:], src[:, pad - shift:T + pad - shift], ALU.add)\
                   .then_inc(step, 1)
                n += 1
                dve.wait_ge(step, n)
                src, shift, side = dst, 2 * shift, 1 - side
            out = self.pooled[:, g * T:(g + 1) * T]
            dve.scalar_tensor_tensor(out, src[:, pad:], 1.0 / win, tile[:, pad:], ALU.mult, ALU.subtract)\
               .then_inc(step, 1)
            head = self.ab[side][:, pad:2 * pad]
            dve.tensor_tensor(head, src[:, pad:2 * pad], k.cst[:, C_CNT + 16 * g:C_CNT + 16 * (g + 1)],
                              ALU.mult).then_inc(step, 1)
            n += 2
            dve.wait_ge(step, n)
            dve.tensor_tensor(out[:, 0:16], head, tile[:, pad:2 * pad], ALU.subtract)\
               .then_inc(self.sem("pooled"), 1)
        for g in range(len(WINDOWS)):
            dve.wait_ge(self.sem("hi"), g + 1)
            dve.scalar_tensor_tensor(self.ylo[:, g * T:(g + 1) * T], k.ps[:, 4 + g, :],
                                     k.col(self.scol + g), self.yhi[:, g * T:(g + 1) * T],
                                     ALU.mult, ALU.subtract).then_inc(self.sem("lo"), 1)


class Dup(Stage):

    def __init__(self, k, name, prev, pairs):
        super().__init__(k, name, prev)
        self.pairs = pairs
        self.ends = [(self.sem("copied"), 16 * len(pairs))]

    def act(self, act):
        self.join(act)
        for dst, src in self.pairs:
            act.dma_start(dst, src).then_inc(self.sem("copied"), 16)


class Select(Stage):

    def __init__(self, k, name, prev, qi, ki, wi, r, sc, m8):
        super().__init__(k, name, prev)
        self.qi, self.ki, self.wi, self.r, self.sc, self.m8 = qi, ki, wi, r, sc, m8
        self.ends = [(self.sem("mask"), TT - 1)]

    def pe(self, pe):
        k = self.k
        self.join(pe)
        for n in range((TT - 1) * IH):
            i, h = n // IH + 1, n % IH
            if n >= 2:
                pe.wait_ge(self.sem("relu"), n - 1)
            r = slice(h % 2 * HD, (h % 2 + 1) * HD)
            pe.matmul(k.ps[:, 4 + n % 2, 0:(i + 1) * P], self.qi[r, h // 2 * T + i * P:h // 2 * T + (i + 1) * P],
                      self.ki[r, 0:(i + 1) * P], start=True, stop=True).then_inc(self.sem("dots"), 1)

    def act(self, act):
        k = self.k
        self.join(act)
        for n in range((TT - 1) * IH):
            w = (n // IH + 2) * P
            act.wait_ge(self.sem("dots"), n + 1)
            if n >= 2:
                act.wait_ge(self.sem("score"), n - 1)
            act.activation(self.r[:, n % 2 * T:n % 2 * T + w], k.ps[:, 4 + n % 2, 0:w], ACT.Relu)\
               .then_inc(self.sem("relu"), 1)

    def score(self, i):
        return self.sc[:, (i - 1) * T:(i - 1) * T + (i + 1) * P]

    def dve(self, dve):
        k = self.k
        self.join(dve)
        for n in range((TT - 1) * IH):
            i, h = n // IH + 1, n % IH
            w = (i + 1) * P
            sc, r = self.score(i), self.r[:, n % 2 * T:n % 2 * T + w]
            wi = self.wi[:, i * IH + h:i * IH + h + 1]
            dve.wait_ge(self.sem("relu"), n + 1)
            if h:
                dve.wait_ge(self.sem("score"), n)
                dve.scalar_tensor_tensor(sc, r, wi, sc, ALU.mult, ALU.add).then_inc(self.sem("score"), 1)
            else:
                dve.tensor_scalar(sc, r, wi, None, ALU.mult).then_inc(self.sem("score"), 1)
        dve.wait_ge(self.sem("score"), (TT - 1) * IH)
        for i in range(1, TT):
            d = self.score(i)[:, i * P:(i + 1) * P]
            dve.tensor_tensor(d, d, k.const(C_QK), ALU.subtract).then_inc(self.sem("causal"), 1)
        dve.wait_ge(self.sem("causal"), TT - 1)

        def largest(i):
            dve.max(self.m8[:, 8 * i:8 * i + 8], self.score(i)).then_inc(self.sem("largest"), 1)

        def take(i, value):
            dve.wait_ge(self.sem("largest"), value)
            dve.match_replace(self.score(i), self.m8[:, 8 * i:8 * i + 8], self.score(i), TAKEN)\
               .then_inc(self.sem("taken"), 1)
        for i in range(1, TT):
            largest(i)
        for i in range(1, TT):
            take(i, i)
        for r in range(1, TOPK // 8):
            for i in range(1, TT):
                dve.wait_ge(self.sem("taken"), (TT - 1) * (r - 1) + i)
                largest(i)
            for i in range(1, TT):
                take(i, (TT - 1) * r + i)
        dve.wait_ge(self.sem("taken"), (TT - 1) * (TOPK // 8))
        for i in range(1, TT):
            dve.tensor_scalar(self.score(i), self.score(i), TAKEN / 1.5, BIG, ALU.is_gt, ALU.mult)\
               .then_inc(self.sem("mask"), 1)


class Store(Stage):

    def __init__(self, k, name, prev, out):
        super().__init__(k, name, prev)
        self.out = out
        self.y = k.at("store_y", 0, TT * D)

    def pe(self, pe):
        k = self.k
        self.join(pe)
        for t in range(TT):
            for c in range(KD):
                tr = pe.transpose(k.ps[:, 2 * t + c // 4, c % 4 * P:(c % 4 + 1) * P],
                                  k.xT[:, c * T + t * P:c * T + (t + 1) * P], k.const(C_ID))
                if c % 4 == 3:
                    tr.then_inc(self.sem("turned"), 1)

    def half(self, t, b):
        return self.y[:, t * D + b * 512:t * D + (b + 1) * 512]

    def act(self, act):
        self.join(act)
        for t in range(TT):
            act.wait_ge(self.sem("turned"), 2 * t + 1)
            act.activation(self.half(t, 0), self.k.ps[:, 2 * t, :], ACT.Copy).then_inc(self.sem("low"), 1)

    def dve(self, dve):
        self.join(dve)
        for t in range(TT):
            dve.wait_ge(self.sem("turned"), 2 * t + 2)
            dve.tensor_copy(self.half(t, 1), self.k.ps[:, 2 * t + 1, :]).then_inc(self.sem("high"), 1)

    def sp(self, sp):
        for t in range(TT):
            sp.wait_ge(self.sem("low"), t + 1)
            sp.wait_ge(self.sem("high"), t + 1)
            sp.dma_start(self.out[0, t * P:(t + 1) * P, :], self.y[:, t * D:(t + 1) * D])\
              .then_inc(self.sem("stored"), 16)
        sp.wait_ge(self.sem("stored"), 16 * TT)



def weight(w, l, r0, rows, c0, cols):
    v = w[bass.ds(l, 1), r0:r0 + rows, bass.ds(c0, cols)] if isinstance(r0, int) else \
        w[bass.ds(l, 1), bass.ds(r0, rows), bass.ds(c0, cols)]
    return v.rearrange("l (k p) n -> p (l k) n", p=P)


def rows_of(w, l, a, n):
    return w[bass.ds(l, 1), a:a + n * P].rearrange("l (a p) -> (l a) p", p=P)


def emit(k, stages, lead=None):
    nc = k.nc
    with nc.Block(no_gpsimd_drain=True) as block:
        @block.sync
        def _(sp):
            for s in stages:
                s.sp(sp)

        @block.scalar
        def _(act):
            if lead:
                hi_unit(k, act, 0, 0)
                hi_unit(k, act, 1, 0)
            for s in stages:
                s.act(act)

        @block.vector
        def _(dve):
            for s in stages:
                s.dve(dve)

        @block.tensor
        def _(pe):
            for s in stages:
                s.pe(pe)

        if lead:
            @block.gpsimd
            def _(pool):
                lo_units(k, pool, k.units)


def first_layer(k, l, A):
    k.stream_sems("first")
    st = []

    def add(cls, name, *a, **kw):
        st.append(cls(k, name, st[-1] if st else None, *a, **kw))
        return st[-1]
    o_qk, o_v = 0, 4096
    o_mv = o_v + 2048
    o_mo = o_mv + TT * MH * (MD + 1)
    o_cv = o_mo + 2048
    o_ya = up8(o_cv + 8 * (T + CONV - 1))
    o_scr = o_ya + 4096
    o_vb = o_scr + 6144
    qk = k.at("qk", o_qk, 8 * T)
    v = k.at("v", o_v, TT * 512)
    mv = k.at("mv", o_mv, TT * MH * (MD + 1))
    mo = k.at("mo", o_mo, 4 * T)
    cv = k.at("conv_in", o_cv, 8 * (T + CONV - 1))
    mqk = k.at("conv_out", o_qk, 8 * T)
    vb = k.at("token_bias", o_vb, 1032)
    k.tmp = k.at("softplus_tmp", o_vb, 512)
    k.gr = k.at("gate_rows", o_cv, 4 * T)
    prow = k.at("param_rows", o_vb + 1032, P)
    ya = [k.at(f"ya_{p}", o_ya + i * 2048, 2048, F32R) for i, p in enumerate(("hi", "lo"))]
    yb = [k.at(f"yb_{p}", o_cv + i * 2048, 2048, F32R) for i, p in enumerate(("hi", "lo"))]
    NMIX, CW, CB, MN, NMLP, B1, B2 = 0, 8, 40, 48, 52, 60, 88
    cw = A["conv_w"][bass.ds(l, 1), :, :].rearrange("l j (a p) -> (l j a) p", p=P)
    add(Params, "params", [
        (rows_of(A["norm_mix_w"], l, 0, 8), NMIX, 8), (cw, CW, 32), (rows_of(A["conv_b"], l, 0, 8), CB, 8),
        (rows_of(A["mlstm_norm_w"], l, 0, 4), MN, 4), (rows_of(A["norm_mlp_w"], l, 0, 8), NMLP, 8),
        (rows_of(A["b_in"], l, 0, 28), B1, 28), (rows_of(A["b_in"], l, GA, 16), B2, 16)],
        [(vb[:, a:a + n], A["b_in"][bass.ds(l, 1), c:c + n].broadcast_to([P, n]))
         for a, c, n in ((0, AV, 512), (512, MV, 512), (1024, MI, 8))], prow)
    add(Norm, "norm_mix", NMIX)
    cv3 = cv[:, :].rearrange("p (t w) -> p t w", w=T + CONV - 1)
    add(Fill, "fill", [(mv[:, :], 1.0), (cv3[:, :, 0:CONV - 1], 0.0)])
    w_in = A["w_in"]

    def src(c0):
        return lambda j, i: weight(w_in, l, 0, D, i * (2 * UC) + (c0 + j * UC), UC)

    def pair(bank):
        return k.ps[:, bank:bank + 2, :]

    def fm_out(dst, w, pad, bcol, func):
        def evac(act, j, i, bank):
            for c in range(UT):
                ins = act.activation(dst[:, bass.ds(i * (4 * w) + (2 * j + c) * w + pad, T)], k.ps[:, bank + c, :],
                                     func, bias=k.pcol[:, bass.ds(i * 4 + bcol + 2 * j + c, 1)])
            return ins
        return evac

    def v_out(dve, j, i, bank):
        return dve.tensor_tensor(
            v[:, :].rearrange("p (t f) -> p t f", t=TT)[:, :, j * UC:(j + 1) * UC],
            pair(bank).rearrange("p b (t f) -> p (b t) f", t=2),
            vb[:, j * UC:(j + 1) * UC].unsqueeze(1).broadcast_to([P, TT, UC]), ALU.add)

    def mv_out(dve, j, i, bank):
        dst = mv[:, :].rearrange("p (t h d) -> p t h d", h=MH, d=MD + 1)[:, :, 2 * j:2 * j + 2, 0:MD]
        bias = vb[:, 512 + j * UC:512 + (j + 1) * UC].rearrange("p (h d) -> p h d", d=MD)
        for t in range(TT):
            ins = dve.tensor_tensor(dst[:, t], k.ps[:, bank + t // 2, t % 2 * UC:(t % 2 + 1) * UC]
                                    .rearrange("p (h d) -> p h d", d=MD), bias, ALU.add)
        return ins

    g8 = k.small[:, 0:32]

    def gate_out(dve, j, i, bank):
        return dve.tensor_tensor(
            g8.rearrange("p (t f) -> p t f", f=8),
            pair(bank).rearrange("p b (t f) -> p (b t) f", t=2)[:, :, 0:8],
            vb[:, 1024:1032].unsqueeze(1).broadcast_to([P, TT, 8]), ALU.add)
    add(Project, "proj", [
        Seg("fm", 4, src(AQ), UC, fm_out(qk, T, 0, B1, ACT.Identity), loop=True),
        Seg("tm", 2, src(AV), UC, v_out, eng="dve"),
        Seg("fm", 4, src(MQ), UC, fm_out(cv, T + CONV - 1, CONV - 1, B1 + 12, ACT.Identity), loop=True),
        Seg("tm", 2, src(MV), UC, mv_out, eng="dve"),
        Seg("fm", 2, src(MO), UC, fm_out(mo, T, 0, B1 + 24, ACT.Sigmoid)),
        Seg("tm", 1, lambda j, i: weight(w_in, l, 0, D, MI, 8), 8, gate_out, eng="dve")])
    t1, t2 = k.at("rope_cos", o_scr, 2 * T), k.at("rope_sin", o_scr + 2 * T, 2 * T)
    add(Rope, "rope", qk, t1, t2)

    def head(x, t0):
        return lambda h: x[h % 2 * HD:(h % 2 + 1) * HD, (t0 + h // 2) * T:(t0 + h // 2 + 1) * T]
    add(Attention, "att", head(qk, 0), head(qk, 4), lambda b, h: v[:, b * 512 + h * HD:b * 512 + (h + 1) * HD],
        lambda i: k.cst[:, C_PAT + (TT - 1 - i) * P:C_PAT + TT * P], o_scr, *ya)
    add(Conv, "conv", cv, mqk, 8, CW, CB)
    spf = k.small[:, 32:48]
    add(Softplus, "forget", None, spf, 16, lambda dve, x2: dve.tensor_scalar(
        x2.rearrange("p (t f) -> p t f", f=MH), g8.rearrange("p (t f) -> p t f", f=8)[:, :, MH:2 * MH],
        -1.0, None, ALU.mult))
    add(Gates, "gates", spf, g8)
    add(Mlstm, "mlstm", mqk, mv, mo, o_scr, k.at("mlstm_sq", o_scr, T)[:, :], k.at("mlstm_y", o_v, 4 * T), *yb, MN)
    g, merged = k.at("gate", 4096, 4 * T), k.at("merged", 0, 8 * T)

    def tiles(x):
        return lambda i: x[:, i * T:(i + 1) * T]
    for i, (n, bcol, gcol, w, y) in enumerate((("att", B2, GA, "w_proj_att", ya),
                                               ("mlstm", B2 + 8, GB, "w_proj_mlstm", yb))):
        add(Branch, f"branch_{n}", lambda c, gcol=gcol: weight(w_in, l, 0, D, gcol + c, UC), bcol,
            lambda c, n, w=w: weight(A[w], l, 0, 512, c, n), 4, tiles(y[0]), tiles(y[1]), g, merged, i > 0)
    mix = [k.at(f"mixed_{p}", 4096 + i * 4096, 4096, F32R) for i, p in enumerate(("hi", "lo"))]
    add(Split, "split_mixed", merged, *mix, 8)
    add(OutProj, "out", lambda c, n: weight(A["w_out"], l, 0, D, c, n), tiles(mix[0]), tiles(mix[1]))
    add(Norm, "norm_mlp", NMLP)
    f = [k.at(f"ff_{p}", i * 8192, 8192, F32R) for i, p in enumerate(("hi", "lo"))]
    scr = [k.at(f"ff_{p}", 16384 + i * 2048, 2048) for i, p in enumerate(("relu", "square"))]
    for half in range(2):
        add(Up, f"up{half}", lambda j, i, half=half: weight(A["w_ff1"], l, 0, D, i * UC + (half * DFF // 2 + j * UC), UC),
            8, *f, scr)
        add(Down, f"down{half}", lambda j, i, half=half: weight(A["w_ff2"], l, i * 256 + (half * DFF // 2 + j * 256), 256, 0, D),
            8, *f, last=half == 1)
    return st


def second_layer(k, A, out):
    k.stream_sems("second")
    st = []
    l = 0

    def add(cls, name, *a, **kw):
        st.append(cls(k, "s_" + name, st[-1] if st else None, *a, **kw))
        return st[-1]
    W = T + CONV - 1
    o_sz = up8(12 * W)
    o_c = o_sz + 4096
    o_scr = o_c + 12 * T
    o_small = o_scr + 6 * D + 1024
    o_rows = o_small + 1088
    xbc = k.at("s_conv_in", 0, 12 * W)
    xs, bt = k.at("s_x_tm", 0, 4096), k.at("s_b_tm", 4096, 1024)
    sz = k.at("s_silu_z", o_sz, 4096)
    c = k.at("s_conv_out", o_c, 12 * T)
    cb = k.at("s_cb", o_scr + 6 * D, 1024)
    k.tmp = k.at("s_softplus_tmp", o_scr, 512)
    rows = k.at("s_rows", o_rows, 2 * T)
    prow = k.at("s_param_rows", o_rows + 2 * T, P)
    sm = k.at("s_small", o_small, 1088)
    s, at = {}, 0
    for n, w in (("dt_raw", 64), ("dt", 64), ("a", 64), ("loc", 64), ("tot", 64), ("eloc", 64), ("etot", 64),
                 ("dec", 64), ("dtdec", 64), ("a_log", 16), ("A", 16), ("D", 16), ("dt_bias", 16)):
        s[n] = sm[:, at:at + w]
        at += w
    FIN1, N1, CW, CB, SN, PS, N2, FIN2 = 0, 8, 16, 64, 76, 84, 88, 96
    add(Params, "params", [
        (A["final_norm_w"].rearrange("(a p) -> a p", p=P), FIN1, 8), (rows_of(A["norm1_w_2"], l, 0, 8), N1, 8),
        (A["conv_w_2"][0].rearrange("j (a p) -> (j a) p", p=P), CW, 48), (rows_of(A["conv_b_2"], l, 0, 12), CB, 12),
        (rows_of(A["ssd_norm_w_2"], l, 0, 8), SN, 8), (rows_of(A["pool_scale_2"], l, 0, 4), PS, 4),
        (rows_of(A["norm2_w_2"], l, 0, 8), N2, 8),
        (A["final_norm_w_2"].rearrange("(a p) -> a p", p=P), FIN2, 8)],
        [(s[n], A[x][0:1, :].broadcast_to([P, SH])) for n, x in (("dt_bias", "dt_bias_2"), ("a_log", "a_log_2"),
                                                              ("D", "d_skip_2"))], prow)
    add(Norm, "norm_first", FIN1, final=True)
    add(Norm, "norm1", N1)
    xbc3 = xbc[:, :].rearrange("p (t w) -> p t w", w=W)
    add(Fill, "fill", [(xbc3[:, :, 0:CONV - 1], 0.0)])
    w_in = A["w_in_2"]

    def src(c0):
        return lambda j, i: weight(w_in, l, 0, D, i * (2 * UC) + (c0 + j * UC), UC)

    def pair(bank):
        return k.ps[:, bank:bank + 2, :]

    def fm_out(dst, w, pad, scale=1.0):
        def evac(act, j, i, bank):
            return act.activation(
                dst[:, bass.ds(i * (4 * w) + 2 * j * w, 2 * w)].rearrange("p (c w) -> p c w", c=2)[:, :, pad:pad + T],
                pair(bank), ACT.Copy, scale=scale)
        return evac

    def z_out(act, j, i, bank):
        return act.activation(
            sz[:, :].rearrange("p (t f) -> p t f", t=TT)[:, :, bass.ds(i * (2 * UC) + j * UC, UC)],
            pair(bank).rearrange("p b (t f) -> p (b t) f", t=2), ACT.Silu)

    def dt_out(dve, j, i, bank):
        return dve.tensor_tensor(
            s["dt_raw"].rearrange("p (t f) -> p t f", f=SH),
            pair(bank).rearrange("p b (t f) -> p (b t) f", t=2)[:, :, 0:SH],
            s["dt_bias"].unsqueeze(1).broadcast_to([P, TT, SH]), ALU.add)
    add(Project, "proj_ssd", [
        Seg("fm", 6, src(XBC2), UC, fm_out(xbc, W, CONV - 1), loop=True),
        Seg("tm", 4, src(Z2), UC, z_out, loop=True),
        Seg("tm", 1, lambda j, i: weight(w_in, l, 0, D, DT2, SH), SH, dt_out, eng="dve")])
    add(Conv, "conv", xbc, c, 12, CW, CB)
    add(Softplus, "dt", None, s["dt"], 64, lambda dve, x2: dve.tensor_copy(x2, s["dt_raw"]))
    add(SsdPrep, "prep", c, xs, bt, cb, rows, s)
    add(Ssd, "ssd", c, xs, bt, cb, rows, s, sz, o_scr)
    ys = [k.at(f"ys_{p}", o_c + i * 4096, 4096, F32R) for i, p in enumerate(("hi", "lo"))]
    add(SsdOut, "ssd_out", sz, SN, *ys)
    g, merged = k.at("s_gate", 4096, 4 * T), k.at("s_merged", 0, 8 * T)

    def tiles(x):
        return lambda i: x[:, i * T:(i + 1) * T]

    def branch(n, b, w, kt, y, more):
        add(Branch, f"branch_{n}", lambda c: weight(w_in, l, 0, D, G2 + b * D + c, UC), None,
            lambda c, n: weight(A[w], l, 0, kt * P, c, n), kt, tiles(y[0]), tiles(y[1]), g, merged, more)
    branch("ssd", 0, "w_up_ssd_2", KD, ys, False)
    q = k.at("s_q", 4096, 4 * T)
    kd = [k.at(f"s_k{i}", 6144 + i * T, T) for i in range(2)]
    v = k.at("s_v", 7168, TT * P)
    qi, ki = k.at("s_qi", 7680, 2 * T), k.at("s_ki", 8704, T)
    pad = 16
    u = k.at("s_u", 9216, 4 * (T + pad))
    ab = [k.at(f"s_window{i}", 11328 + i * (T + pad), T + pad) for i in range(2)]
    pooled = k.at("s_pooled", 12384, 4 * T)
    pw = k.at("s_pool_w", 14432, 4 * P)
    ya = [k.at(f"s_ya_{p}", 14944 + i * 2048, 2048, F32R) for i, p in enumerate(("hi", "lo"))]
    yp = [k.at(f"s_yp_{p}", 19040 + i * 2048, 2048, F32R) for i, p in enumerate(("hi", "lo"))]
    sc = k.at("s_scores", 23136, 3 * T)
    r = k.at("s_relu", 14944, 2 * T)
    wi, m8 = k.small[:, 0:16], k.small[:, 16:48]
    u3 = u[:, :].rearrange("p (t w) -> p t w", w=T + pad)
    add(Fill, "fill2", [(u3[:, :, 0:pad], 0.0), (ab[0][:, 0:pad], 0.0), (ab[1][:, 0:pad], 0.0)])

    def kv_out(act, j, i, bank):
        act.activation(kd[0][0:HD, :], k.ps[0:HD, bank, :], ACT.Copy)
        act.activation(kd[1][HD:P, :], k.ps[HD:P, bank, :], ACT.Copy)
        return act.activation(v[:, :], k.ps[:, bank + 1, :], ACT.Copy)

    def ki_out(act, j, i, bank):
        act.activation(ki[0:HD, :], k.ps[0:HD, bank, :], ACT.Copy)
        return act.activation(wi.rearrange("p (t h) -> p t h", h=IH),
                              k.ps[:, bank + 1, :].rearrange("p (t f) -> p t f", f=P)[:, :, 0:IH],
                              ACT.Copy, scale=IH ** -0.5 * HD ** -0.5)
    add(Project, "proj_att", [
        Seg("fm", 2, src(Q2), UC, fm_out(q, T, 0, -HD ** -0.5)),
        Seg("fm", 1, src(K2), UC, kv_out, off=P, width=P, tiles=1),
        Seg("fm", 1, src(QI2), UC, fm_out(qi, T, 0)),
        Seg("fm", 1, lambda j, i: weight(w_in, l, 0, D, KI2, P), P, ki_out, off=HD, width=IH, tiles=1),
        Seg("fm", 2, src(U2), UC, fm_out(u, T + pad, pad))])
    add(Dup, "dup", [(kd[0][HD:P, :], kd[0][0:HD, :]), (kd[1][0:HD, :], kd[1][HD:P, :]),
                     (ki[HD:P, :], ki[0:HD, :])])
    add(PoolMix, "pool", u, *ab, pooled, A["pool_w_2"][0].rearrange("g c d -> c g d"), pw, PS, *yp)
    sel = add(Select, "select", qi, ki, wi, r, sc, m8)
    add(Attention, "att", lambda h: q[h % 2 * HD:(h % 2 + 1) * HD, h // 2 * T:(h // 2 + 1) * T],
        lambda h: kd[h // 4][h % 2 * HD:(h % 2 + 1) * HD, :],
        lambda b, h: v[:, b * P + h // 4 * HD:b * P + (h // 4 + 1) * HD],
        lambda i: sel.score(i) if i else k.const(C_QK), 7680, *ya)
    branch("att", 1, "w_up_attn_2", 4, ya, True)
    branch("pool", 2, "w_up_pool_2", 4, yp, True)
    mix = [k.at(f"s_mixed_{p}", 6144 + i * 4096, 4096, F32R) for i, p in enumerate(("hi", "lo"))]
    add(Split, "split_mixed", merged, *mix, 8)
    add(OutProj, "out", lambda c, n: weight(A["w_out_2"], l, 0, D, c, n), tiles(mix[0]), tiles(mix[1]))
    add(Norm, "norm2", N2)
    f = [k.at(f"s_ff_{p}", i * 11264, 11264, F32R) for i, p in enumerate(("hi", "lo"))]
    scr = [k.at(f"s_ff_{p}", 22528 + i * 1024, 1024) for i, p in enumerate(("silu", "product"))]

    add(Glu, "up", lambda j, i: weight(A["w_ffn_in_2"], l, 0, D, i * UC + j * FF2, UC), FF2 // UC, *f, scr)
    add(Down, "down", lambda j, i: weight(A["w_ffn_out_2"], l, i * 256 + j * 256, 256, 0, D), 11, *f, last=True)
    add(Norm, "norm_last", FIN2, final=True)
    add(Store, "store", out)
    return st


def program(nc, A, table, out):
    with ExitStack() as ctx:
        k = Kern(nc, ctx)
        k.xT = k.keep("xT", KD * T)
        k.hhi, k.hlo = k.keep("h_hi", KD * T, F32R), k.keep("h_lo", KD * T, F32R)
        k.wraw = k.keep("w_raw", 2 * SLOT)
        k.whi, k.wlo = k.keep("w_hi", 2 * SLOT, F32R), k.keep("w_lo", 2 * SLOT, F32R)
        k.cst = k.keep("constants", C_END)
        k.cos, k.sin = k.keep("cos", T), k.keep("sin", T)
        k.pcol = k.keep("param_cols", 104)
        k.stat = k.keep("stat", 96)
        k.acol = k.keep("gate_cols", 32)
        k.small = k.keep("small", 48)
        k.eps = k.keep("eps", 8)
        k.arena = k.top
        k.arena_words = (nc.sbuf_usable_end() - k.arena) // 4 if callable(nc.sbuf_usable_end) else (nc.sbuf_usable_end - k.arena) // 4
        k.ps = ctx.enter_context(nc.psum_tensor("ps", [P, 8, 512], F32))
        emit(k, [Setup(k, "setup", None, A["x"], A["positions"], table)])
        with ExitStack() as k.ctx:
            k.sems = []
            with nc.Fori(0, DEPTH) as l:
                emit(k, first_layer(k, l, A), lead=True)
                ids = [s.num for s in k.sems]
                assert max(ids) - min(ids) + 1 == len(ids)
                nc.sync.sem_clear(range(min(ids), max(ids) + 1))
                nc.all_engine_barrier()
        with ExitStack() as k.ctx:
            emit(k, second_layer(k, A, out), lead=True)


_INS = ['x', 'positions', 'norm_mix_w', 'w_in', 'b_in', 'conv_w', 'conv_b', 'mlstm_norm_w', 'w_proj_att',
        'w_proj_mlstm', 'w_out', 'norm_mlp_w', 'w_ff1', 'w_ff2', 'final_norm_w', 'norm1_w_2', 'w_in_2',
        'conv_w_2', 'conv_b_2', 'dt_bias_2', 'a_log_2', 'd_skip_2', 'ssd_norm_w_2', 'pool_w_2',
        'pool_scale_2', 'w_up_ssd_2', 'w_up_attn_2', 'w_up_pool_2', 'w_out_2', 'norm2_w_2',
        'w_ffn_in_2', 'w_ffn_out_2', 'final_norm_w_2']


def kernel(**inputs):
    import concourse.bacc as _bacc
    from concourse.bass_utils import run_bass_kernel_spmd as _run

    nc = _bacc.Bacc("TRN2", target_bir_lowering=False, num_devices=1)
    arrays, args = {}, {}
    for name in _INS:
        a = np.ascontiguousarray(inputs[name])
        arrays[f"in_{name}"] = a
        args[name] = nc.dram_tensor(f"in_{name}", a.shape, mybir.dt.from_np(a.dtype), kind="ExternalInput").ap()
    arrays["constants_table"] = constants()
    table = nc.dram_tensor("constants_table", (P, C_END), F32, kind="ExternalInput").ap()
    out = nc.dram_tensor("out_x", (1, T, D), F32, kind="ExternalOutput").ap()
    program(nc, args, table, out)
    r = _run(nc, [arrays], core_ids=[0])
    return r.results[0]["out_x"]
```

```python
import math
from contextlib import ExitStack

import numpy as np

import concourse.bass as bass
from concourse import mybir

F32 = mybir.dt.float32
F32R = mybir.dt.float32r
I32 = mybir.dt.int32
ACT = mybir.ActivationFunctionType
ALU = mybir.AluOpType
AX = mybir.AxisListType

P = 128
T = 512
TT = T // P
D = 1024
KD = D // P
DEPTH = 2
EPS = 1e-6
BIG = 1e30
SLOT = 2048
UC = SLOT // KD
UT = UC // P

HEADS, HD = 8, 64
MH, MD = 4, 128
CONV = 4
DFF = 4 * D
AQ, AK, AV, MQ, MK, MV, MO = (512 * i for i in range(7))
MI = 3584
GA = MI + 2 * MH
GB = GA + D
NPAT = 3
PATTERNS = ((128, 1), (512, 4), (2048, 16))
ROPE_THETA, ROPE_DIM = 500000.0, HD // 4

SH, SHD, SG = 16, 64, 2
SPG = SH // SG
XC = 1536
Z2, XBC2 = 0, D
DT2 = XBC2 + XC
Q2 = DT2 + SH
K2 = Q2 + 512
QI2 = K2 + 256
KI2 = QI2 + 256
IH = 4
U2 = KI2 + 64 + IH
G2 = U2 + 512
FF2 = 2816
TOPK = 128
TAKEN = -3e38
WINDOWS = (2, 4, 8, 16)

C_ID, C_ONE, C_ROT, C_QK, C_ST, C_KEEP, C_PAT = (P * i for i in range(7))
C_INV = C_PAT + TT * P
C_MSK, C_UNM = C_INV + 1, C_INV + 2
C_CNT = C_INV + 3
C_END = C_CNT + len(WINDOWS) * 16


def up8(n):
    return (n + 7) // 8 * 8


def constants():
    c = np.zeros((P, C_END), np.float32)
    i = np.arange(P)
    c[:, C_ID:C_ID + P] = np.eye(P)
    c[:, C_ONE:C_ONE + P] = 1.0
    half = ROPE_DIM // 2
    for p in range(P):
        d = p % HD
        if d < half:
            c[p + half, C_ROT + p] = -1.0
        elif d < ROPE_DIM:
            c[p - half, C_ROT + p] = 1.0
    c[:, C_QK:C_QK + P] = np.where(i[None, :] > i[:, None], BIG, 0.0)
    c[:, C_ST:C_ST + P] = np.where(i[:, None] > i[None, :], BIG, 0.0)
    c[:, C_KEEP:C_KEEP + P] = i[:, None] <= i[None, :]
    for b in range(TT):
        dist = i[:, None] - i[None, :] + (TT - 1 - b) * P
        n = sum(((dist >= 0) & (dist % dil == 0) & (dist <= win)).astype(int) for win, dil in PATTERNS)
        c[:, C_PAT + b * P:C_PAT + (b + 1) * P] = np.where(n > 0, -np.log(np.maximum(n, 1)), BIG)
    d = i % HD
    inv = np.float32(ROPE_THETA) ** (-np.arange(0, ROPE_DIM, 2, dtype=np.float32) / np.float32(ROPE_DIM))
    c[:, C_INV] = np.where(d < ROPE_DIM, inv[d % half], 0.0)
    c[:, C_MSK] = d < ROPE_DIM
    c[:, C_UNM] = d >= ROPE_DIM
    for g, w in enumerate(WINDOWS):
        c[:, C_CNT + 16 * g:C_CNT + 16 * (g + 1)] = 1.0 / np.minimum(np.arange(1, 17), w)
    return c


class Stage:

    side, base, budget = None, 0, 0

    def __init__(self, k, name, prev):
        self.k, self.name, self.prev, self.ends, self.s = k, name, prev, [], {}

    def beside(self, side, base, budget):
        self.side, self.base, self.budget = side, base, budget
        return base + budget

    def side_pe(self, pe, n, steps):
        if self.side:
            self.side.emit_pe(pe, self.base + self.budget * (n + 1) // steps)

    def side_out(self, who, eng, n, steps):
        if self.side:
            self.side.emit_out(who, eng, self.base + self.budget * n // steps)

    def sem(self, name):
        if name not in self.s:
            self.s[name] = self.k.new_sem(f"{self.name}_{name}")
        return self.s[name]

    def join(self, eng):
        for p in self.prev:
            for s, v in p.ends:
                eng.wait_ge(s, v)

    def sp(self, e): pass
    def act(self, e): pass
    def dve(self, e): pass
    def pe(self, e): pass


class Kern:
    def __init__(self, nc, ctx):
        self.nc, self.ctx, self.sems = nc, ctx, []
        self.top = (nc.sbuf_base + 31) // 32 * 32

    def new_sem(self, name):
        s = self.ctx.enter_context(self.nc.semaphore(name))
        self.sems.append(s)
        return s

    def at(self, name, off, cols, dt=F32, parts=P):
        assert off + cols <= self.arena_words, (name, off, cols)
        return self.nc.alloc_sbuf_tensor_at(name, [parts, cols], dt, offset=self.arena + 4 * off)

    def keep(self, name, cols, dt=F32):
        t = self.nc.alloc_sbuf_tensor_at(name, [P, cols], dt, offset=self.top)
        self.top += 4 * ((cols + 7) // 8 * 8)
        return t

    def slot(self, u):
        return u % 2

    def const(self, c):
        return self.cst[:, c:c + P]

    def col(self, c):
        return self.pcol[:, c:c + 1]

    def pick(self, h, n):
        return self.cst[0:n, C_ID + h:C_ID + h + 1].broadcast_to([n, P])

    def ones(self, n, w):
        return self.cst[0:n, C_ONE:C_ONE + 1].broadcast_to([n, w])

    def hh(self, i):
        return self.hhi[:, i * T:(i + 1) * T]

    def hl(self, i):
        return self.hlo[:, i * T:(i + 1) * T]

    def stream_sems(self, tag):
        self.landed = [self.new_sem(f"{tag}_unit_landed_{i}") for i in range(2)]
        self.hi_done = self.new_sem(f"{tag}_unit_hi_done")
        self.split = self.new_sem(f"{tag}_unit_split")
        self.unit_used = self.new_sem(f"{tag}_unit_used")
        self.units = 0


def units(k, n):
    k.units += n
    return k.units - n



def load_unit(k, sp, u0, du, src, cols):
    slot = k.slot(u0)
    if not (isinstance(du, int) and u0 + du < 2):
        sp.wait_ge(k.split, du + (u0 - 1))
    n = src.shape[1]
    dst = k.wraw[:, slot * SLOT:slot * SLOT + n * cols].rearrange("p (k n) -> p k n", n=cols)
    sp.dma_start(dst, src).then_inc(k.landed[slot], 16)


def hi_unit(k, act, u0, du):
    slot = k.slot(u0)
    act.wait_ge(k.landed[slot], landed_value(u0, du))
    if not (isinstance(du, int) and u0 + du < 2):
        act.wait_ge(k.unit_used, du + (u0 - 1))
    act.activation(k.whi[:, slot * SLOT:(slot + 1) * SLOT], k.wraw[:, slot * SLOT:(slot + 1) * SLOT],
                   ACT.Copy).then_inc(k.hi_done, 1)


def landed_value(u0, du):
    return du * 8 + 16 * (u0 // 2 + 1)


def lo_units(k, pool, n):
    def one(slot, value):
        a = slot * SLOT
        pool.wait_ge(k.hi_done, value)
        pool.tensor_tensor(k.wlo[:, a:a + SLOT], k.wraw[:, a:a + SLOT], k.whi[:, a:a + SLOT],
                           ALU.subtract).then_inc(k.split, 1)
    with pool.Fori(0, n // 2) as i:
        one(0, i * 2 + 1)
        one(1, i * 2 + 2)
    if n % 2:
        one(0, n)


def fm_unit(k, pe, u0, kt, cols, xh, xl, outs, ready=None, done=None):
    a = k.slot(u0) * SLOT
    if ready:
        for i in range(kt):
            pe.wait_ge(ready, i + 1)
            for c, out in enumerate(outs):
                w = slice(a + i * cols + c * P, a + i * cols + (c + 1) * P)
                pe.matmul(out, k.whi[:, w], xh(i), start=i == 0, stop=False, skip_group_check=True)
                pe.matmul(out, k.whi[:, w], xl(i), start=False, stop=False, skip_group_check=True)
                mm = pe.matmul(out, k.wlo[:, w], xh(i), start=False, stop=i == kt - 1, skip_group_check=True)
                if done and i == kt - 1 and c < len(outs) - 1:
                    mm.then_inc(done, 1)
        return mm
    for c, out in enumerate(outs):
        for i in range(kt):
            w = slice(a + i * cols + c * P, a + i * cols + (c + 1) * P)
            pe.matmul(out, k.whi[:, w], xh(i), start=i == 0, stop=False)
            pe.matmul(out, k.whi[:, w], xl(i), start=False, stop=False)
            mm = pe.matmul(out, k.wlo[:, w], xh(i), start=False, stop=i == kt - 1)
        if done and c < len(outs) - 1:
            mm.then_inc(done, 1)
    return mm


def tm_unit(k, pe, u0, kt, cols, off, width, xh, xl, out):
    a = k.slot(u0) * SLOT
    for t in range(TT):
        tok = slice(t * P, (t + 1) * P)
        for i in range(kt):
            w = slice(a + i * cols + off, a + i * cols + off + width)
            pe.matmul(out(t), xh(i)[:, tok], k.whi[:, w], start=i == 0, stop=False)
            pe.matmul(out(t), xl(i)[:, tok], k.whi[:, w], start=False, stop=False)
            mm = pe.matmul(out(t), xh(i)[:, tok], k.wlo[:, w], start=False, stop=i == kt - 1)
    return mm



class Stats(Stage):

    SLOTS = 3
    AT = 22528

    def __init__(self, k, name, prev, tile=None, emitted=False):
        super().__init__(k, name, prev)
        self.tile, self.emitted = tile, emitted
        self.sq = k.at(f"{name}_squares", self.AT, self.SLOTS * T)
        self.ends = [(self.sem("rstd"), 1)]
        self.ahead = None

    def slot(self, t):
        return self.sq[:, t % self.SLOTS * T:(t % self.SLOTS + 1) * T]

    def square(self, act, t):
        k = self.k
        if t == 0:
            act.activation(k.eps[:, 1:2], k.eps[:, 0:1], ACT.Sqrt)
        if self.tile:
            s, v = self.tile(t)
            act.wait_ge(s, v)
        if t >= self.SLOTS:
            act.wait_ge(self.sem("summed"), t - self.SLOTS + 1)
        act.activation(self.slot(t), k.xT[:, t * T:(t + 1) * T], ACT.Square).then_inc(self.sem("squared"), 1)

    def sum(self, pe, t):
        pe.wait_ge(self.sem("squared"), t + 1)
        pe.matmul(self.k.ps[:, 0, :], self.k.const(C_ONE), self.slot(t), start=t == 0, stop=t == KD - 1,
                  skip_group_check=True).then_inc(self.sem("summed"), 1)

    def act(self, act):
        k = self.k
        if not self.emitted:
            self.join(act)
            for t in range(KD):
                self.square(act, t)
        act.wait_ge(self.sem("summed"), KD)
        act.activation(k.rstd[:, :], k.ps[:, 0, :], ACT.Sqrt, bias=k.eps[:, 0:1],
                       scale=1.0 / D).then_inc(self.sem("root"), 1)
        if self.ahead is not None:
            hi_unit(k, act, self.ahead, 0)

    def pe(self, pe):
        if not self.emitted:
            self.join(pe)
            for t in range(KD):
                self.sum(pe, t)

    def dve(self, dve):
        k = self.k
        dve.wait_ge(self.sem("root"), 1)
        dve.reciprocal(k.rstd[:, :], k.rstd[:, :]).then_inc(self.sem("rstd"), 1)


class Norm(Stage):

    def __init__(self, k, name, prev, wcol, final=False):
        super().__init__(k, name, prev)
        self.wcol, self.final = wcol, final
        self.h = k.xT if final else k.at(f"{name}_h", KD * T, KD * T)
        self.ready = self.sem("scaled" if final else "lo")
        self.ends = [(self.ready, KD)]

    def act(self, act):
        k = self.k
        if not self.final:
            self.join(act)
            for t in range(KD):
                act.wait_ge(self.sem("scaled"), t + 1)
                act.activation(k.hhi[:, t * T:(t + 1) * T], self.h[:, t * T:(t + 1) * T],
                               ACT.Copy).then_inc(self.sem("hi"), 1)

    def dve(self, dve):
        k = self.k
        self.join(dve)
        for t in range(KD + 1):
            if t < KD:
                dve.scalar_tensor_tensor(self.h[:, t * T:(t + 1) * T], k.xT[:, t * T:(t + 1) * T],
                                         k.col(self.wcol + t), k.rstd[:, :], ALU.mult,
                                         ALU.mult).then_inc(self.sem("scaled"), 1)
            if t and not self.final:
                dve.wait_ge(self.sem("scaled"), t)
                dve.wait_ge(self.sem("hi"), t)
                dve.tensor_tensor(k.hlo[:, (t - 1) * T:t * T], self.h[:, (t - 1) * T:t * T],
                                  k.hhi[:, (t - 1) * T:t * T], ALU.subtract).then_inc(self.sem("lo"), 1)


class Seg:

    def __init__(self, kind, n, src, cols, evac, eng="act", loop=False, off=0, width=None, tiles=UT):
        self.kind, self.n, self.src, self.cols, self.evac = kind, n, src, cols, evac
        self.eng, self.loop, self.off, self.width, self.tiles = eng, loop, off, width or cols, tiles


class Project(Stage):

    def __init__(self, k, name, prev, norm, segs):
        super().__init__(k, name, prev)
        self.norm = norm
        self.segs = segs
        self.u0 = k.units
        for s in segs:
            s.u0 = units(k, s.n)
        n = k.units - self.u0
        self.out = [self.sem("out_even"), self.sem("out_odd")]
        self.ends = [(self.out[0], (n + 1) // 2), (self.out[1], n // 2)]

    def each(self, eng, body, which=lambda s: True, peel=lambda s: False):
        for s in filter(which, self.segs):
            if s.loop:
                first = 1 if peel(s) else 0
                for j in range(2 * first):
                    body(s, j, 0)
                with eng.Fori(first, s.n // 2) as i:
                    for j in range(2):
                        body(s, j, i)
            else:
                for j in range(s.n):
                    body(s, j, 0)

    def sp(self, sp):
        self.each(sp, lambda s, j, i: load_unit(self.k, sp, s.u0 + j, i * 2, s.src(j, i), s.cols),
                  peel=lambda s: s.u0 < 2)

    def pe(self, pe):
        k = self.k

        def unit(s, j, i):
            local = s.u0 + j - self.u0
            bank = 2 * (local % 2)
            pe.wait_ge(k.split, i * 2 + (s.u0 + j + 1))
            if local >= 2 or not isinstance(i, int):
                pe.wait_ge(self.out[local % 2], i + local // 2)
            if s.kind == "fm":
                mm = fm_unit(k, pe, s.u0 + j, KD, s.cols, k.hh, k.hl,
                             [k.ps[:, bank + c, :] for c in range(s.tiles)],
                             self.norm.ready if local == 0 and isinstance(i, int) else None)
                if s.off:
                    mm = tm_unit(k, pe, s.u0 + j, KD, s.cols, s.off, s.width, k.hh, k.hl,
                                 lambda t: k.ps[:, bank + 1, t * P:t * P + s.width])
            else:
                mm = tm_unit(k, pe, s.u0 + j, KD, s.cols, 0, s.cols, k.hh, k.hl,
                             lambda t: k.ps[:, bank + t // 2, t % 2 * UC:t % 2 * UC + s.cols])
            mm.then_inc(k.unit_used, 1)
        self.each(pe, unit, peel=lambda s: s.u0 - self.u0 < 2)

    def evac(self, eng, who):
        k = self.k

        def unit(s, j, i):
            local = s.u0 + j - self.u0
            bank = 2 * (local % 2)
            if s.eng == who:
                eng.wait_ge(k.unit_used, i * 2 + (s.u0 + j + 1))
                s.evac(eng, j, i, bank).then_inc(self.out[local % 2], 1)
            if who == "act":
                hi_unit(k, eng, s.u0 + j + 2, i * 2)
        self.each(eng, unit, lambda s: who == "act" or s.eng == who)

    def act(self, act):
        self.join(act)
        self.evac(act, "act")

    def dve(self, dve):
        self.join(dve)
        self.evac(dve, "dve")


class Job:

    def __init__(self, who, evac, c=None, tm=None, need=()):
        self.who, self.evac, self.c, self.tm, self.need = who, evac, c, tm, need


class Jobs(Stage):

    PIECE = 6

    def __init__(self, k, name, prev):
        super().__init__(k, name, prev)
        self.units, self.jobs, self.pieces = [], [], []
        self.at = {"pe": 0, "act": 0, "dve": 0}
        self.joined = set()
        self.early = 0

    def unit(self, src, kt, cols, xh, xl, jobs):
        u = units(self.k, 1)
        self.units.append((u, src, cols))
        for job in jobs:
            job.n, job.u, job.kt, job.cols, job.xh, job.xl = len(self.jobs), u, kt, cols, xh, xl
            job.last = job is jobs[-1]
            if not job.last:
                self.early += 1
            job.early = self.early
            self.jobs.append(job)
            if job.c is not None:
                steps = [(job, None, i) for i in range(kt)]
                per = self.PIECE // 3
            else:
                steps = [(job, t, i) for t in range(job.tm[0], job.tm[1]) for i in range(kt)]
                per = self.PIECE * 2 // 3
            for a in range(0, len(steps), per):
                self.pieces.append(steps[a:a + per])
            job.end = len(self.pieces)
        return len(self.pieces)

    def ends_at(self, upto=None):
        n = sum(1 for job in self.jobs if upto is None or job.end <= upto)
        return [(self.bank(b), (n + 3 - b) // 4) for b in range(min(4, n))]

    def read(self, job):
        return self.bank(job.n % 4), job.n // 4 + 1

    def bank(self, b):
        return self.sem(f"bank{b}")

    def sp(self, sp):
        for u, src, cols in self.units:
            load_unit(self.k, sp, u, 0, src, cols)

    def start(self, who, eng):
        if who not in self.joined:
            self.joined.add(who)
            self.join(eng)

    def done(self, eng, job):
        if job.last:
            eng.wait_ge(self.k.unit_used, job.u + 1)
        else:
            eng.wait_ge(self.sem("job"), job.early)

    def emit_pe(self, pe, upto):
        k = self.k
        while self.at["pe"] < min(upto, len(self.pieces)):
            self.start("pe", pe)
            piece = self.pieces[self.at["pe"]]
            self.at["pe"] += 1
            for job, t, i in piece:
                b, a = job.n % 4, k.slot(job.u) * SLOT + i * job.cols
                t0 = 0 if t is None else job.tm[0]
                first = i == 0 and t in (None, t0)
                if first:
                    pe.wait_ge(k.split, job.u + 1)
                    if job.n >= 4:
                        pe.wait_ge(self.bank(b), job.n // 4)
                    for s, v in job.need:
                        pe.wait_ge(s, v)
                if t is None:
                    w = slice(a + job.c * P, a + (job.c + 1) * P)
                    out, ops = k.ps[:, b, :], [(k.whi[:, w], job.xh(i)), (k.whi[:, w], job.xl(i)),
                                               (k.wlo[:, w], job.xh(i))]
                    end = i == job.kt - 1
                    stop = end
                else:
                    _, t1, off, width, pitch = job.tm
                    w = slice(a + off, a + off + width)
                    tok = slice(t * P, (t + 1) * P)
                    out = k.ps[:, b, (t - t0) * pitch:(t - t0) * pitch + width]
                    ops = [(job.xh(i)[:, tok], k.whi[:, w]), (job.xl(i)[:, tok], k.whi[:, w]),
                           (job.xh(i)[:, tok], k.wlo[:, w])]
                    stop = i == job.kt - 1
                    end = stop and t == t1 - 1
                for n, (lhs, rhs) in enumerate(ops):
                    mm = pe.matmul(out, lhs, rhs, start=i == 0 and n == 0, stop=stop and n == 2)
                if end:
                    mm.then_inc(k.unit_used if job.last else self.sem("job"), 1)

    def emit_out(self, who, eng, upto):
        while self.at[who] < len(self.jobs) and self.jobs[self.at[who]].end <= upto:
            job = self.jobs[self.at[who]]
            self.at[who] += 1
            if job.who == who:
                self.start(who, eng)
                self.done(eng, job)
                job.evac(eng, job.n % 4).then_inc(self.bank(job.n % 4), 1)
            if who == "act" and job.last and job.u + 2 < self.k.units:
                hi_unit(self.k, eng, job.u + 2, 0)


class Rest(Stage):

    def __init__(self, k, name, prev, jobs, upto=None):
        super().__init__(k, name, prev)
        self.jobs, self.upto = jobs, upto or len(jobs.pieces)
        self.ends = [e for p in prev for e in p.ends] + jobs.ends_at(upto)

    def pe(self, pe):
        self.jobs.emit_pe(pe, self.upto)

    def act(self, act):
        self.jobs.emit_out("act", act, self.upto)

    def dve(self, dve):
        self.jobs.emit_out("dve", dve, self.upto)


class Rope(Stage):

    def __init__(self, k, name, prev, qk, t1, t2):
        super().__init__(k, name, prev)
        self.qk, self.t1, self.t2 = qk, t1, t2
        self.ends = [(self.sem("turned"), 8)]

    def pe(self, pe):
        k = self.k
        self.join(pe)
        for t in range(8):
            if t >= 4:
                pe.wait_ge(self.sem("sin"), t - 3)
            pe.matmul(k.ps[:, 4 + t % 4, :], k.const(C_ROT), self.qk[:, t * T:(t + 1) * T],
                      start=True, stop=True).then_inc(self.sem("swapped"), 1)
            self.side_pe(pe, t, 8)

    def dve(self, dve):
        k = self.k
        self.join(dve)
        for t in range(8):
            self.side_out("dve", dve, t, 8)
            scale = -HD ** -0.5 if t < 4 else 1.0
            a, b = (x[:, t % 2 * T:(t % 2 + 1) * T] for x in (self.t1, self.t2))
            tile = self.qk[:, t * T:(t + 1) * T]
            dve.scalar_tensor_tensor(a, tile, scale, k.cos[:, :], ALU.mult, ALU.mult)\
               .then_inc(self.sem("cos"), 1)
            dve.wait_ge(self.sem("swapped"), t + 1)
            dve.scalar_tensor_tensor(b, k.ps[:, 4 + t % 4, :], scale, k.sin[:, :], ALU.mult, ALU.mult)\
               .then_inc(self.sem("sin"), 1)
            dve.wait_ge(self.sem("cos"), t + 1)
            dve.wait_ge(self.sem("sin"), t + 1)
            dve.tensor_tensor(tile, a, b, ALU.add).then_inc(self.sem("turned"), 1)

    def act(self, act):
        self.side_out("act", act, 7, 8)


class Attention(Stage):


    def __init__(self, k, name, prev, q, kk, v, mask, scr, ns, yhi, ylo):
        super().__init__(k, name, prev)
        self.q, self.kk, self.v, self.mask, self.yhi, self.ylo = q, kk, v, mask, yhi, ylo
        self.ns = k.at(f"{name}_negscores", ns, 3 * T)
        self.p = k.at(f"{name}_probs", scr, 3 * T)
        self.pt = k.at(f"{name}_probsT", scr + 3 * T, 2 * TT * T)
        self.N = HEADS * TT
        self.stat = k.stat
        self.ends = [(self.sem("lo"), HEADS)]

    def pe(self, pe):
        k = self.k
        self.join(pe)
        for n in range(self.N + 3):
            if n < self.N:
                h, i = divmod(n, TT)
                if n >= 2:
                    pe.wait_ge(self.sem("masked"), n - 1)
                pe.matmul(k.ps[:, 4 + n % 2, 0:(i + 1) * P], self.q(h)[:, i * P:(i + 1) * P],
                          self.kk(h)[:, 0:(i + 1) * P], start=True, stop=True)\
                  .then_inc(self.sem("scores"), 1)
            m = n - 2
            if 0 <= m < self.N:
                i = m % TT
                pe.wait_ge(self.sem("probs"), m + 1)
                if m >= 1:
                    pe.wait_ge(self.sem("copied"), m)
                for b in range(i + 1):
                    tr = pe.transpose(k.ps[:, 6, b * P:(b + 1) * P],
                                      self.p[:, m % 3 * T + b * P:m % 3 * T + (b + 1) * P], k.const(C_ID))
                tr.then_inc(self.sem("turned"), 1)
            m = n - 3
            if m >= 0 and m % TT == TT - 1:
                h = m // TT
                pe.wait_ge(self.sem("copied"), m + 1)
                if h >= 1:
                    pe.wait_ge(self.sem("lo"), h)
                r = slice(h % 2 * HD, h % 2 * HD + HD)
                for b in range(TT):
                    mm = pe.matmul(k.ps[r, 7, b * P:T], self.v(b, h),
                                   self.pt[:, (h % 2 * TT + b) * T + b * P:(h % 2 * TT + b + 1) * T],
                                   start=b == 0, stop=b == TT - 1, skip_group_check=True)
                mm.then_inc(self.sem("values"), 1)
            self.side_pe(pe, n, self.N + 3)

    def dve(self, dve):
        k = self.k
        self.join(dve)
        for n in range(self.N + 3):
            self.side_out("dve", dve, n, self.N + 3)
            if n < self.N:
                i = n % TT
                w = (i + 1) * P
                dve.wait_ge(self.sem("scores"), n + 1)
                if n >= 3:
                    dve.wait_ge(self.sem("exp"), n - 2)
                dve.tensor_tensor_reduce(self.ns[:, n % 3 * T:n % 3 * T + w], k.ps[:, 4 + n % 2, 0:w],
                                         self.mask(i), 1.0, BIG, ALU.add, ALU.min,
                                         self.stat[:, n:n + 1]).then_inc(self.sem("masked"), 1)
            m = n - 1
            if 0 <= m < self.N:
                w = (m % TT + 1) * P
                dve.wait_ge(self.sem("exp"), m + 1)
                dve.reciprocal(self.stat[:, 64 + m:65 + m], self.stat[:, 32 + m:33 + m])\
                   .then_inc(self.sem("recip"), 1)
                dve.wait_ge(self.sem("recip"), m + 1)
                pr = self.p[:, m % 3 * T:m % 3 * T + w]
                dve.tensor_scalar(pr, pr, self.stat[:, 64 + m:65 + m], None, ALU.mult)\
                   .then_inc(self.sem("probs"), 1)
            m = n - 3
            if m >= 0 and m % TT == TT - 1:
                h = m // TT
                r = slice(h % 2 * HD, h % 2 * HD + HD)
                dve.wait_ge(self.sem("hi"), h + 1)
                dve.tensor_tensor(self.ylo[r, h // 2 * T:(h // 2 + 1) * T], k.ps[r, 7, :],
                                  self.yhi[r, h // 2 * T:(h // 2 + 1) * T], ALU.subtract)\
                   .then_inc(self.sem("lo"), 1)

    def act(self, act):
        k = self.k
        self.join(act)
        for n in range(self.N + 3):
            self.side_out("act", act, n, self.N + 3)
            if n < self.N:
                w = (n % TT + 1) * P
                act.wait_ge(self.sem("masked"), n + 1)
                if n >= 3:
                    act.wait_ge(self.sem("turned"), n - 2)
                act.activation(self.p[:, n % 3 * T:n % 3 * T + w], self.ns[:, n % 3 * T:n % 3 * T + w],
                               ACT.Exp, bias=self.stat[:, n:n + 1], scale=-1.0,
                               accum_out=self.stat[:, 32 + n:33 + n]).then_inc(self.sem("exp"), 1)
            m = n - 2
            if 0 <= m < self.N:
                h, i = divmod(m, TT)
                act.wait_ge(self.sem("turned"), m + 1)
                if h >= 2 and i == 0:
                    act.wait_ge(self.sem("values"), h - 1)
                dst = self.pt[:, h % 2 * TT * T:(h % 2 + 1) * TT * T].rearrange("p (b q) -> p b q", b=TT)
                act.activation(dst[:, 0:i + 1, i * P:(i + 1) * P],
                               k.ps[:, 6, 0:(i + 1) * P].rearrange("p (b q) -> p b q", q=P),
                               ACT.Copy).then_inc(self.sem("copied"), 1)
            m = n - 3
            if m >= 0 and m % TT == TT - 1:
                h = m // TT
                r = slice(h % 2 * HD, h % 2 * HD + HD)
                act.wait_ge(self.sem("values"), h + 1)
                act.activation(self.yhi[r, h // 2 * T:(h // 2 + 1) * T], k.ps[r, 7, :],
                               ACT.Copy).then_inc(self.sem("hi"), 1)


class Conv(Stage):

    def __init__(self, k, name, prev, src, dst, tiles, wcol, bcol):
        super().__init__(k, name, prev)
        self.src, self.dst, self.tiles, self.wcol, self.bcol = src, dst, tiles, wcol, bcol
        self.ends = [(self.sem("silu"), tiles)]

    def tap(self, t, j):
        a = t * (T + CONV - 1) + j
        return self.src[:, a:a + T]

    def act(self, act):
        k = self.k
        self.join(act)
        for t in range(self.tiles):
            self.side_out("act", act, t, 2 * self.tiles)
            act.activation(self.dst[:, t * T:(t + 1) * T], self.tap(t, 0), ACT.Identity,
                           bias=k.col(self.bcol + t), scale=k.col(self.wcol + t))\
               .then_inc(self.sem("tap"), 1)
        for t in range(self.tiles):
            self.side_out("act", act, t + self.tiles, 2 * self.tiles)
            act.wait_ge(self.sem("taps"), t + 1)
            d = self.dst[:, t * T:(t + 1) * T]
            act.activation(d, d, ACT.Silu).then_inc(self.sem("silu"), 1)

    def dve(self, dve):
        k = self.k
        self.join(dve)
        for t0 in range(0, self.tiles, 4):
            for j in range(1, CONV):
                self.side_out("dve", dve, t0 // 4 * 3 + j - 1, self.tiles // 4 * 3)
                for t in range(t0, t0 + 4):
                    d = self.dst[:, t * T:(t + 1) * T]
                    if j == 1:
                        dve.wait_ge(self.sem("tap"), t + 1)
                    else:
                        dve.wait_ge(self.sem("part"), t0 // 4 * 8 + (j - 2) * 4 + t - t0 + 1)
                    ins = dve.scalar_tensor_tensor(d, self.tap(t, j), k.col(self.wcol + j * self.tiles + t),
                                                   d, ALU.mult, ALU.add)
                    ins.then_inc(self.sem("taps" if j == CONV - 1 else "part"), 1)


    def pe(self, pe):
        self.side_pe(pe, 0, 1)


class Softplus(Stage):

    def __init__(self, k, name, prev, x, out, w, pre):
        super().__init__(k, name, prev)
        self.x, self.out, self.w, self.pre = x, out, w, pre
        self.ends = [(self.sem("step"), 11)]

    def pe(self, pe):
        self.side_pe(pe, 0, 1)

    def act(self, act):
        k, w = self.k, self.w
        self.side_out("act", act, 0, 1)
        e, u, ln = (k.tmp[:, i * 64:i * 64 + w] for i in range(3))
        act.wait_ge(self.sem("step"), 2)
        act.activation(e, k.tmp[:, 192:192 + w], ACT.Exp).then_inc(self.sem("exp"), 1)
        act.wait_ge(self.sem("step"), 3)
        act.activation(ln, u, ACT.Ln).then_inc(self.sem("ln"), 1)

    def dve(self, dve):
        k, w = self.k, self.w
        e, u, ln, na, eq, num, den, x2 = (k.tmp[:, i * 64:i * 64 + w] for i in range(8))
        step = self.sem("step")
        self.side_out("dve", dve, 0, 1)
        self.join(dve)
        self.pre(dve, x2).then_inc(step, 1)
        dve.wait_ge(step, 1)
        dve.scalar_tensor_tensor(na, x2, -1.0, x2, ALU.mult, ALU.min).then_inc(step, 1)
        dve.wait_ge(self.sem("exp"), 1)
        dve.tensor_scalar(u, e, 1.0, None, ALU.add).then_inc(step, 1)
        dve.wait_ge(step, 3)
        dve.tensor_scalar(den, u, 1.0, None, ALU.subtract).then_inc(step, 1)
        dve.wait_ge(step, 4)
        dve.tensor_scalar(eq, den, 0.0, None, ALU.is_equal).then_inc(step, 1)
        dve.wait_ge(step, 5)
        dve.wait_ge(self.sem("ln"), 1)
        dve.tensor_tensor(num, ln, eq, ALU.add).then_inc(step, 1)
        dve.tensor_tensor(den, den, eq, ALU.add).then_inc(step, 1)
        dve.wait_ge(step, 7)
        dve.reciprocal(den, den).then_inc(step, 1)
        dve.wait_ge(step, 8)
        dve.tensor_tensor(num, num, den, ALU.mult).then_inc(step, 1)
        dve.wait_ge(step, 9)
        dve.tensor_tensor(num, num, e, ALU.mult).then_inc(step, 1)
        dve.wait_ge(step, 10)
        dve.scalar_tensor_tensor(self.out, x2, 0.0, num, ALU.max, ALU.add).then_inc(step, 1)


class Gates(Stage):

    def __init__(self, k, name, prev, sp, g8):
        super().__init__(k, name, prev)
        self.spf, self.g8 = sp, g8
        self.ends = [(self.sem("emt"), 1)]

    def pe(self, pe):
        k = self.k
        self.join(pe)
        for t in range(TT):
            pe.transpose(k.ps[0:MH, 4, t * P:(t + 1) * P], self.spf[:, t * MH:(t + 1) * MH], k.const(C_ID))
            tr = pe.transpose(k.ps[0:MH, 5, t * P:(t + 1) * P], self.g8[:, t * 8:t * 8 + MH], k.const(C_ID))
        tr.then_inc(self.sem("rows"), 1)
        self.side_pe(pe, 0, 2)
        pe.wait_ge(self.sem("scan"), 6)
        for t in range(TT):
            pe.transpose(k.ps[:, 6, t * MH:(t + 1) * MH], k.gr[0:MH, 2 * T + t * P:2 * T + (t + 1) * P],
                         k.const(C_ID)[0:MH, 0:MH])
            tr = pe.transpose(k.ps[:, 7, t * MH:(t + 1) * MH], k.gr[0:MH, t * P:(t + 1) * P],
                              k.const(C_ID)[0:MH, 0:MH])
        tr.then_inc(self.sem("cols"), 1)
        self.side_pe(pe, 1, 2)

    def dve(self, dve):
        k = self.k
        self.side_out("dve", dve, 0, 2)
        b, ig, a, m = (k.gr[0:MH, i * T:(i + 1) * T] for i in range(4))
        s = self.sem("scan")
        self.join(dve)
        dve.wait_ge(self.sem("rows"), 1)
        dve.tensor_copy(m, k.ps[0:MH, 4, :]).then_inc(s, 1)
        dve.wait_ge(s, 1)
        dve.tensor_tensor_scan(b, k.ones(MH, T), m, 0.0, ALU.mult, ALU.subtract).then_inc(s, 1)
        dve.wait_ge(s, 2)
        dve.tensor_tensor(a, k.ps[0:MH, 5, :], b, ALU.subtract).then_inc(s, 1)
        dve.wait_ge(s, 3)
        dve.tensor_tensor_scan(m, k.ones(MH, T), a, -BIG, ALU.mult, ALU.max).then_inc(s, 1)
        dve.wait_ge(s, 4)
        dve.tensor_tensor(ig, b, m, ALU.add).then_inc(s, 1)
        dve.wait_ge(s, 5)
        dve.tensor_scalar(b, ig, -1.0, 80.0, ALU.mult, ALU.min).then_inc(s, 1)
        dve.wait_ge(self.sem("cols"), 1)
        dve.tensor_copy(k.acol[:, 0:16], k.ps[:, 6, 0:16]).then_inc(self.sem("acol"), 1)

    def act(self, act):
        k = self.k
        self.side_out("act", act, 1, 2)
        act.wait_ge(self.sem("cols"), 1)
        act.wait_ge(self.sem("acol"), 1)
        act.activation(k.acol[:, 16:32], k.ps[:, 7, 0:16], ACT.Exp).then_inc(self.sem("emt"), 1)


class Mlstm(Stage):

    H_AT = 2 * T + TT * (TT + 1) // 2 * P
    SCRATCH = H_AT + MH * T

    def __init__(self, k, name, prev, qk, v, mo, mo_ready, scr, mb, yhi, ylo, ncol):
        super().__init__(k, name, prev)
        self.qk, self.v, self.mo, self.yhi, self.ylo, self.ncol = qk, v, mo, yhi, ylo, ncol
        self.mo_ready = mo_ready
        self.e = k.at(f"{name}_decay", scr, 2 * T)
        self.sq = k.at(f"{name}_squares", scr, T)
        self.pt = k.at(f"{name}_weighted", scr + 2 * T, self.H_AT - 2 * T)
        self.hn = k.at(f"{name}_h", scr + self.H_AT, MH * T)
        self.mb = k.at(f"{name}_maxima", mb, MH * T)
        self.yt = k.at(f"{name}_y", mb, MH * T)
        self.ends = [(self.sem("lo"), MH), (self.sem("hi"), MH)]
        self.steps = MH * (TT + 1) + MH + 1

    def num(self):
        return self.k.ps[:, 6:8, 0:2 * (MD + 1)].rearrange("p b (t d) -> p b t d", d=MD + 1)

    def weights(self, s, a, b):
        off = sum(T - x * P for x in range(s)) - s * P
        return self.pt[:, off + a:off + b]

    def pe(self, pe):
        k = self.k
        self.join(pe)
        step = 0
        for h in range(MH):
            pe.matmul(k.ps[:, 4 + h, :], k.pick(h, MH), k.gr[0:MH, 3 * T:4 * T], start=True, stop=True)\
              .then_inc(self.sem("spread"), 1)
        for h in range(MH):
            if h == 0:
                pe.wait_ge(self.sem("maxima"), MH)
            for s in range(TT):
                n = h * TT + s
                if n >= 2:
                    pe.wait_ge(self.sem("weighted"), n - 1)
                pe.matmul(k.ps[:, 4 + n % 2, s * P:T], self.qk[:, (4 + h) * T + s * P:(4 + h) * T + (s + 1) * P],
                          self.qk[:, h * T + s * P:(h + 1) * T], start=True, stop=True)\
                  .then_inc(self.sem("scores"), 1)
                self.side_pe(pe, step, self.steps)
                step += 1
            pe.wait_ge(self.sem("weighted"), TT * (h + 1))
            if h >= 1:
                pe.wait_ge(self.sem("h"), h)
            for t in range(TT):
                for s in range(t + 1):
                    mm = pe.matmul(self.num()[:, t // 2, t % 2, :], self.weights(s, t * P, (t + 1) * P),
                                   self.v[:, (s * MH + h) * (MD + 1):(s * MH + h + 1) * (MD + 1)],
                                   start=s == 0, stop=s == t)
            mm.then_inc(self.sem("sums"), 1)
            self.side_pe(pe, step, self.steps)
            step += 1
        pe.wait_ge(self.sem("normed"), 1)
        for h in range(MH):
            if h >= 2:
                pe.wait_ge(self.sem("yt"), h - 1)
            for t in range(TT):
                tr = pe.transpose(k.ps[:, 4 + h % 2, t * P:(t + 1) * P],
                                  self.hn[:, (h * TT + t) * P:(h * TT + t + 1) * P], k.const(C_ID))
            tr.then_inc(self.sem("fm"), 1)
            self.side_pe(pe, step, self.steps)
            step += 1
        self.side_pe(pe, step, self.steps)

    def dve(self, dve):
        k = self.k
        self.join(dve)
        st = k.stat
        step = self.sem("stat")
        ns = 0

        def gap(h, s):
            n = h * TT + s
            if n >= 2:
                dve.wait_ge(self.sem("weighted"), n - 1)
            t = self.e[:, n % 2 * T + s * P:(n % 2 + 1) * T]
            dve.tensor_scalar(t, self.mb[:, h * T + s * P:(h + 1) * T], k.acol[:, s * MH + h:s * MH + h + 1],
                              0.0, ALU.subtract, ALU.max).then_inc(self.sem("gap0"), 1)
            dve.wait_ge(self.sem("gap0"), n + 1)
            d = self.e[:, n % 2 * T + s * P:n % 2 * T + (s + 1) * P]
            dve.tensor_tensor(d, d, k.const(C_ST), ALU.add).then_inc(self.sem("gap"), 1)

        def weigh(h, s):
            n = h * TT + s
            if h >= 1 and s == 0:
                dve.wait_ge(self.sem("sums"), h)
            dve.wait_ge(self.sem("scores"), n + 1)
            dve.wait_ge(self.sem("decay"), n + 1)
            dve.scalar_tensor_tensor(self.weights(s, s * P, T), k.ps[:, 4 + n % 2, s * P:T],
                                     MD ** -0.5, self.e[:, n % 2 * T + s * P:(n % 2 + 1) * T],
                                     ALU.mult, ALU.mult).then_inc(self.sem("weighted"), 1)
        for h in range(MH):
            if h == 0:
                dve.wait_ge(self.sem("maxima"), MH)
            else:
                dve.wait_ge(self.sem("ssq"), h)
            gap(h, 0)
            for s in range(TT):
                self.side_out("dve", dve, h * (TT + 1) + s, self.steps)
                if s + 1 < TT:
                    gap(h, s + 1)
                weigh(h, s)
            self.side_out("dve", dve, h * (TT + 1) + TT, self.steps)
            dve.wait_ge(self.sem("sums"), h + 1)
            num = self.num()
            den = st[:, h * TT:(h + 1) * TT]
            den4 = den.rearrange("p (b t) -> p b t", b=2)
            emt = k.acol[:, 16:32].rearrange("p (b t h) -> p b t h", b=2, h=MH)[:, :, :, h]
            dve.tensor_copy(den4, num[:, :, :, MD]).then_inc(step, 1)
            dve.wait_ge(step, ns + 1)
            dve.scalar_tensor_tensor(den4, den4, -1.0, den4, ALU.mult, ALU.max).then_inc(step, 1)
            dve.wait_ge(step, ns + 2)
            dve.tensor_tensor(den4, den4, emt, ALU.max).then_inc(step, 1)
            dve.wait_ge(step, ns + 3)
            dve.reciprocal(den, den).then_inc(step, 1)
            dve.wait_ge(step, ns + 4)
            hn = self.hn[:, h * T:(h + 1) * T].rearrange("p (b t d) -> p b t d", b=2, d=MD)
            dve.tensor_tensor(hn, num[:, :, :, 0:MD], den4.unsqueeze(3).broadcast_to([P, 2, 2, MD]),
                              ALU.mult).then_inc(self.sem("h"), 1)
            dve.wait_ge(self.sem("h"), h + 1)
            dve.wait_ge(self.sem("weighted"), TT * (h + 1))
            flat = self.hn[:, h * T:(h + 1) * T]
            dve.tensor_tensor(self.sq[:, :], flat, flat, ALU.mult).then_inc(step, 1)
            ns += 5
            dve.wait_ge(step, ns)
            dve.tensor_reduce(st[:, 16 + h * TT:16 + (h + 1) * TT],
                              self.sq[:, :].rearrange("p (t d) -> p t d", d=MD), AX.X, ALU.add)\
               .then_inc(self.sem("ssq"), 1)
        self.side_out("dve", dve, MH * (TT + 1), self.steps)
        for ready, value in self.mo_ready:
            dve.wait_ge(ready, value)
        dve.tensor_scalar(self.mo[:, :], self.mo[:, :], 0.5, 0.5, ALU.mult, ALU.add)\
           .then_inc(self.sem("out_gate"), 1)
        dve.wait_ge(self.sem("root"), 1)
        dve.reciprocal(st[:, 48:64], st[:, 32:48]).then_inc(step, 1)
        dve.wait_ge(step, ns + 1)
        hn = self.hn[:, :].rearrange("p (g d) -> p g d", d=MD)
        dve.tensor_tensor(hn, hn, st[:, 48:64].unsqueeze(2).broadcast_to([P, 16, MD]), ALU.mult)\
           .then_inc(self.sem("normed"), 1)
        for h in range(MH):
            y = self.yt[:, h * T:(h + 1) * T]
            self.side_out("dve", dve, MH * (TT + 1) + h, self.steps)
            dve.wait_ge(self.sem("fm"), h + 1)
            if h == 0:
                dve.wait_ge(self.sem("out_gate"), 1)
            dve.scalar_tensor_tensor(y, k.ps[:, 4 + h % 2, :], k.col(self.ncol + h),
                                     self.mo[:, h * T:(h + 1) * T], ALU.mult, ALU.mult)\
               .then_inc(self.sem("yt"), 1)
        for h in range(MH):
            dve.wait_ge(self.sem("yt"), h + 1)
            dve.wait_ge(self.sem("hi"), h + 1)
            dve.tensor_tensor(self.ylo[:, h * T:(h + 1) * T], self.yt[:, h * T:(h + 1) * T],
                              self.yhi[:, h * T:(h + 1) * T], ALU.subtract).then_inc(self.sem("lo"), 1)

    def act(self, act):
        k = self.k
        self.join(act)
        for h in range(MH):
            act.wait_ge(self.sem("spread"), h + 1)
            act.activation(self.mb[:, h * T:(h + 1) * T], k.ps[:, 4 + h, :], ACT.Copy)\
               .then_inc(self.sem("maxima"), 1)
        for n in range(MH * TT):
            h, s = divmod(n, TT)
            self.side_out("act", act, h * (TT + 1) + s, self.steps)
            act.wait_ge(self.sem("gap"), n + 1)
            e = self.e[:, n % 2 * T + s * P:(n % 2 + 1) * T]
            act.activation(e, e, ACT.Exp, scale=-1.0).then_inc(self.sem("decay"), 1)
        self.side_out("act", act, MH * (TT + 1), self.steps)
        act.wait_ge(self.sem("ssq"), MH)
        act.activation(k.stat[:, 32:48], k.stat[:, 16:32], ACT.Sqrt, bias=k.eps[:, 0:1], scale=1.0 / MD)\
           .then_inc(self.sem("root"), 1)
        for h in range(MH):
            self.side_out("act", act, MH * (TT + 1) + h, self.steps)
            act.wait_ge(self.sem("yt"), h + 1)
            act.activation(self.yhi[:, h * T:(h + 1) * T], self.yt[:, h * T:(h + 1) * T], ACT.Copy)\
               .then_inc(self.sem("hi"), 1)


class Branches(Jobs):

    def __init__(self, k, name, prev, g, merged):
        super().__init__(k, name, prev)
        self.g, self.merged, self.gated = g, merged, 0
        self.users = [None] * 4
        self.final = {}

    def gate(self, wgate, half, bias=None, free=()):
        k = self.k
        self.gates = []
        for j in range(2):
            jobs = []
            for t in range(2 * j, 2 * j + 2):
                waits = [self.read(self.users[t])] if self.users[t] else list(free)

                def evac(act, bank, t=t, waits=waits):
                    for s, v in waits:
                        act.wait_ge(s, v)
                    more = {} if bias is None else {"bias": bias(4 * half + t)}
                    return act.activation(self.g[:, t * T:(t + 1) * T], k.ps[:, bank, :], ACT.Tanh,
                                          scale=0.5, **more)
                jobs.append(Job("act", evac, c=t % 2))
            at = self.unit(wgate(half * 512 + j * UC), KD, UC, k.hh, k.hl, jobs)
            self.gates += jobs
        return at

    def up(self, wup, kt, y, half, add, need=(), free=()):
        k = self.k
        nup = 2 if kt == KD else 1
        w = 512 // nup
        for j in range(nup):
            jobs = []
            for c in range(w // P):
                t = j * (w // P) + c
                waits = [self.read(self.gates[t])] + (list(free) if t == 0 else [])
                if add:
                    self.gated += 1

                def evac(dve, bank, t=t, n=self.gated, waits=waits):
                    g = self.g[:, t * T:(t + 1) * T]
                    m = self.merged[:, (4 * half + t) * T:(4 * half + t + 1) * T]
                    for s, v in waits:
                        dve.wait_ge(s, v)
                    ins = dve.scalar_tensor_tensor(g if add else m, g, 1.0, k.ps[:, bank, :], ALU.add, ALU.mult)
                    if not add:
                        return ins
                    ins.then_inc(self.sem("gated"), 1)
                    dve.wait_ge(self.sem("gated"), n)
                    return dve.tensor_tensor(m, m, g, ALU.add)
                jobs.append(Job("dve", evac, c=c, need=need if t == 0 else ()))
                self.users[t] = self.final[4 * half + t] = jobs[-1]
            at = self.unit(wup(half * 512 + j * w, w), kt, w, y[0], y[1], jobs)
        return at


class Split(Stage):

    def __init__(self, k, name, prev, x, hi, lo, n, tile):
        super().__init__(k, name, prev)
        self.x, self.hi, self.lo, self.n, self.tile = x, hi, lo, n, tile
        self.ready = self.sem("lo")
        self.ends = [(self.ready, n)]

    def act(self, act):
        for t in range(self.n):
            s, v = self.tile(t)
            act.wait_ge(s, v)
            act.activation(self.hi[:, t * T:(t + 1) * T], self.x[:, t * T:(t + 1) * T], ACT.Copy)\
               .then_inc(self.sem("hi"), 1)

    def dve(self, dve):
        self.join(dve)
        for t in range(self.n):
            dve.wait_ge(self.sem("hi"), t + 1)
            dve.tensor_tensor(self.lo[:, t * T:(t + 1) * T], self.x[:, t * T:(t + 1) * T],
                              self.hi[:, t * T:(t + 1) * T], ALU.subtract).then_inc(self.sem("lo"), 1)


class OutProj(Stage):

    def __init__(self, k, name, prev, w, x, xh, xl):
        super().__init__(k, name, prev)
        self.w, self.x, self.xh, self.xl = w, x, xh, xl
        self.u0 = units(k, 4)
        self.ends = [(self.sem("added"), 8)]

    def tile(self, t):
        return self.sem("added"), t + 1

    def sp(self, sp):
        for j in range(4):
            load_unit(self.k, sp, self.u0 + j, 0, self.w(j * UC, UC), UC)

    def pe(self, pe):
        k = self.k
        for j in range(4):
            pe.wait_ge(k.split, self.u0 + j + 1)
            fm_unit(k, pe, self.u0 + j, KD, UC, self.xh, self.xl, [k.ps[:, 2 * j + i, :] for i in range(2)],
                    self.x.ready if j == 0 else None, self.sem("even")).then_inc(k.unit_used, 1)
            if j:
                self.stats.sum(pe, 2 * j - 2)
                self.stats.sum(pe, 2 * j - 1)
        self.stats.sum(pe, 6)
        self.stats.sum(pe, 7)

    def act(self, act):
        for j in range(4):
            if j < 3:
                hi_unit(self.k, act, self.u0 + j + 2, 0)
            self.stats.square(act, 2 * j)
            self.stats.square(act, 2 * j + 1)
        self.stats.ahead = self.u0 + 5

    def dve(self, dve):
        k = self.k
        for j in range(4):
            for c in range(2 * j, 2 * j + 2):
                if c % 2:
                    dve.wait_ge(k.unit_used, self.u0 + j + 1)
                else:
                    dve.wait_ge(self.sem("even"), j + 1)
                x = k.xT[:, c * T:(c + 1) * T]
                dve.scalar_tensor_tensor(x, k.ps[:, c, :], 0.5, x, ALU.mult, ALU.add)\
                   .then_inc(self.sem("added"), 1)


class Up(Stage):

    def __init__(self, k, name, prev, before, src, n, fhi, flo, scr):
        super().__init__(k, name, prev)
        self.before = before
        self.src, self.n, self.fhi, self.flo = src, n, fhi, flo
        self.r = scr[0]
        self.f = scr[1]
        self.u0 = units(k, n)
        self.ends = [(self.sem("lo"), n), (self.sem("hi"), n)]
        self.banks = [(self.sem("r"), n)]

    def sp(self, sp):
        with sp.Fori(0, self.n // 2) as i:
            for j in range(2):
                load_unit(self.k, sp, self.u0 + j, i * 2, self.src(j, i * 2), UC)

    def pe(self, pe):
        k = self.k
        after_down = isinstance(self.before, Down)

        def unit(j, du):
            pe.wait_ge(k.split, du + (self.u0 + j + 1))
            if isinstance(du, int) and du + j < 2:
                if after_down:
                    pe.wait_ge(*self.before.tile(2 * j + 1))
            else:
                pe.wait_ge(self.sem("r"), du + (j - 1))
            fm_unit(k, pe, self.u0 + j, KD, UC, k.hh, k.hl, [k.ps[:, 2 * j + c, :] for c in range(2)],
                    self.before.ready if not after_down and isinstance(du, int) and du + j == 0 else None)\
                .then_inc(k.unit_used, 1)
        unit(0, 0)
        unit(1, 0)
        with pe.Fori(1, self.n // 2) as i:
            unit(0, i * 2)
            unit(1, i * 2)

    def out(self, x, j, du):
        w = UT * T
        return x[:, bass.ds(du * w + j * w, w)]

    def act(self, act):
        k = self.k
        self.join(act)

        def unit(j, du):
            w = UT * T
            r, f = self.r[:, j * w:(j + 1) * w], self.f[:, j * w:(j + 1) * w]
            act.wait_ge(k.unit_used, du + (self.u0 + j + 1))
            if not (isinstance(du, int) and du + j < 2):
                act.wait_ge(self.sem("f"), du + (j - 1))
            act.activation(r, k.ps[:, 2 * j:2 * j + 2, :].rearrange("p a b -> p (a b)"), ACT.Relu)\
               .then_inc(self.sem("r"), 1)
            hi_unit(k, act, self.u0 + j + 2, du)
            act.wait_ge(self.sem("f"), du + (j + 1))
            act.activation(self.out(self.fhi, j, du), f, ACT.Copy).then_inc(self.sem("hi"), 1)
        unit(0, 0)
        unit(1, 0)
        with act.Fori(1, self.n // 2) as i:
            unit(0, i * 2)
            unit(1, i * 2)

    def dve(self, dve):
        k = self.k
        self.join(dve)

        def unit(j, du):
            w = UT * T
            r, f = self.r[:, j * w:(j + 1) * w], self.f[:, j * w:(j + 1) * w]
            dve.wait_ge(self.sem("r"), du + (j + 1))
            if not (isinstance(du, int) and du + j < 2):
                dve.wait_ge(self.sem("hi"), du + (j - 1))
            dve.tensor_tensor(f, r, r, ALU.mult).then_inc(self.sem("f"), 1)
            dve.wait_ge(self.sem("hi"), du + (j + 1))
            dve.tensor_tensor(self.out(self.flo, j, du), f, self.out(self.fhi, j, du), ALU.subtract)\
               .then_inc(self.sem("lo"), 1)
        unit(0, 0)
        unit(1, 0)
        with dve.Fori(1, self.n // 2) as i:
            unit(0, i * 2)
            unit(1, i * 2)


class Glu(Stage):

    def __init__(self, k, name, prev, norm, src, n, fhi, flo, scr):
        super().__init__(k, name, prev)
        self.norm = norm
        self.src, self.n, self.fhi, self.flo = src, n, fhi, flo
        self.r, self.f = scr[0][:, :], scr[1][:, :]
        self.u0 = units(k, 2 * n)
        self.ends = [(self.sem("lo"), n), (self.sem("hi"), n)]
        self.banks = [(self.sem("silu"), n), (self.sem("f"), n)]

    def pairs(self, eng, body):
        body(0)
        with eng.Fori(1, self.n) as i:
            body(i)

    def sp(self, sp):
        with sp.Fori(0, self.n) as i:
            for j in range(2):
                load_unit(self.k, sp, self.u0 + j, i * 2, self.src(j, i), UC)

    def pe(self, pe):
        k = self.k

        def pair(i):
            for j in range(2):
                pe.wait_ge(k.split, i * 2 + (self.u0 + j + 1))
                if not isinstance(i, int):
                    pe.wait_ge(self.sem("f" if j else "silu"), i)
                fm_unit(k, pe, self.u0 + j, KD, UC, k.hh, k.hl, [k.ps[:, 2 * j + c, :] for c in range(2)],
                        self.norm.ready if isinstance(i, int) and j == 0 else None).then_inc(k.unit_used, 1)
        self.pairs(pe, pair)

    def tiles(self, x, i):
        return x[:, bass.ds(i * (2 * T), 2 * T)]

    def act(self, act):
        k = self.k
        self.join(act)

        def pair(i):
            act.wait_ge(k.unit_used, i * 2 + (self.u0 + 1))
            if not isinstance(i, int):
                act.wait_ge(self.sem("f"), i)
            act.activation(self.r, k.ps[:, 0:2, :].rearrange("p a b -> p (a b)"), ACT.Silu)\
               .then_inc(self.sem("silu"), 1)
            hi_unit(k, act, self.u0 + 2, i * 2)
            hi_unit(k, act, self.u0 + 3, i * 2)
            act.wait_ge(self.sem("f"), i + 1)
            act.activation(self.tiles(self.fhi, i), self.f, ACT.Copy).then_inc(self.sem("hi"), 1)
        self.pairs(act, pair)

    def dve(self, dve):
        k = self.k
        self.join(dve)

        def pair(i):
            dve.wait_ge(self.sem("silu"), i + 1)
            dve.wait_ge(k.unit_used, i * 2 + (self.u0 + 2))
            if not isinstance(i, int):
                dve.wait_ge(self.sem("hi"), i)
                dve.wait_ge(self.sem("lo"), i)
            dve.tensor_tensor(self.f, self.r, k.ps[:, 2:4, :].rearrange("p a b -> p (a b)"), ALU.mult)\
               .then_inc(self.sem("f"), 1)
            dve.wait_ge(self.sem("hi"), i + 1)
            dve.tensor_tensor(self.tiles(self.flo, i), self.f, self.tiles(self.fhi, i), ALU.subtract)\
               .then_inc(self.sem("lo"), 1)
        self.pairs(dve, pair)


class Down(Stage):

    def __init__(self, k, name, prev, up, src, n, fhi, flo, last=False):
        super().__init__(k, name, prev)
        self.up, self.stats = up, None
        self.src, self.n, self.fhi, self.flo, self.last = src, n, fhi, flo, last
        self.u0 = units(k, n)
        self.ends = [(self.sem("added"), 8)]

    def tile(self, t):
        return self.sem("added"), t + 1

    def sp(self, sp):
        k = self.k
        with sp.Fori(0, self.n // 2) as i:
            for j in range(2):
                load_unit(k, sp, self.u0 + j, i * 2, self.src(j, i * 2), D)
        if self.n % 2:
            load_unit(k, sp, self.u0 + self.n - 1, 0, self.src(0, self.n - 1), D)

    def pe(self, pe):
        k = self.k

        def unit(j, du, first=False, last=False):
            a = k.slot(self.u0 + j) * SLOT
            pe.wait_ge(k.split, du + (self.u0 + j + 1))
            pe.wait_ge(self.up.sem("lo"), du + (j + 1))
            for n, c in enumerate((4, 5, 6, 7, 0, 1, 2, 3) if first else range(KD)):
                if first and n == 4:
                    for s, v in self.up.banks:
                        pe.wait_ge(s, v)
                for i in range(2):
                    w = slice(a + i * D + c * P, a + i * D + (c + 1) * P)
                    x = bass.ds(du * (2 * T) + (j * 2 + i) * T, T)
                    pe.matmul(k.ps[:, c, :], k.whi[:, w], self.fhi[:, x], start=first and i == 0,
                              stop=False, skip_group_check=True)
                    pe.matmul(k.ps[:, c, :], k.whi[:, w], self.flo[:, x], start=False, stop=False,
                              skip_group_check=True)
                    mm = pe.matmul(k.ps[:, c, :], k.wlo[:, w], self.fhi[:, x], start=False,
                                   stop=last and i == 1, skip_group_check=True)
                if last and c < KD - 1:
                    mm.then_inc(self.sem("tile"), 1)
                if n == KD - 1:
                    mm.then_inc(k.unit_used, 1)
                if last and self.stats and c >= 2:
                    self.stats.sum(pe, c - 2)
            if last and self.stats:
                self.stats.sum(pe, KD - 2)
                self.stats.sum(pe, KD - 1)
        odd = self.n % 2
        unit(0, 0, first=True)
        unit(1, 0)
        end = self.n - 1 if odd else self.n - 2
        with pe.Fori(1, end // 2) as i:
            unit(0, i * 2)
            unit(1, i * 2)
        if odd:
            unit(0, self.n - 1, last=True)
        else:
            unit(0, self.n - 2)
            unit(1, self.n - 2, last=True)

    def act(self, act):
        k = self.k
        n = self.n - 2 if self.last else self.n
        with act.Fori(0, n // 2) as i:
            for j in range(2):
                hi_unit(k, act, self.u0 + j + 2, i * 2)
        if n % 2:
            hi_unit(k, act, self.u0 + n - 1 + 2, 0)
        if self.stats:
            for t in range(KD):
                self.stats.square(act, t)

    def dve(self, dve):
        k = self.k
        for c in range(KD):
            if c < KD - 1:
                dve.wait_ge(self.sem("tile"), c + 1)
            else:
                dve.wait_ge(k.unit_used, self.u0 + self.n)
            x = k.xT[:, c * T:(c + 1) * T]
            dve.tensor_tensor(x, x, k.ps[:, c, :], ALU.add).then_inc(self.sem("added"), 1)


class Params(Stage):

    def __init__(self, k, name, prev, rows, bcasts, prow, half=None):
        super().__init__(k, name, prev)
        self.rows, self.bcasts, self.half = rows, bcasts, half
        self.n = rows[-1][1] + rows[-1][2]
        self.prow = prow
        self.ends = [(self.sem("cols"), 1)]
        self.spread = [(self.sem("spread"), 16 * len(bcasts))]
        if half:
            self.ends.append((self.sem("halved"), 1))

    def sp(self, sp):
        self.join(sp)
        for src, r, n in self.rows:
            sp.dma_start(self.prow[r:r + n, :], src).then_inc(self.sem("landed"), 16)
        for dst, src in self.bcasts:
            sp.dma_start(dst, src).then_inc(self.sem("spread"), 16)

    def pe(self, pe):
        k = self.k
        self.join(pe)
        pe.wait_ge(self.sem("landed"), 16 * len(self.rows))
        pe.transpose(k.ps[:, 7, 0:self.n], self.prow[0:self.n, :], k.const(C_ID)[0:self.n, 0:self.n])\
          .then_inc(self.sem("turned"), 1)

    def dve(self, dve):
        k = self.k
        self.join(dve)
        dve.wait_ge(self.sem("turned"), 1)
        dve.tensor_copy(k.pcol[:, 0:self.n], k.ps[:, 7, 0:self.n]).then_inc(self.sem("cols"), 1)
        if self.half:
            a, n = self.half
            dve.wait_ge(self.sem("cols"), 1)
            dve.tensor_scalar(k.hbias[:, 0:n], k.pcol[:, a:a + n], 0.5, None, ALU.mult)\
               .then_inc(self.sem("halved"), 1)


class Fill(Stage):

    def __init__(self, k, name, prev, fills, more=()):
        super().__init__(k, name, prev)
        self.fills = fills
        self.ends = [(self.sem("filled"), len(fills)), *more]

    def dve(self, dve):
        self.join(dve)
        for ap, value in self.fills:
            dve.memset(ap, value).then_inc(self.sem("filled"), 1)


class Setup(Stage):

    def __init__(self, k, name, prev, x, positions, table):
        super().__init__(k, name, prev)
        self.x, self.positions, self.table = x, positions, table
        self.xtm = k.at("setup_x", 0, TT * D)
        self.posi = k.at("setup_positions", TT * D, T, I32)
        self.w = [k.at(f"setup_w{i}", TT * D + (i + 1) * T, T) for i in range(4)]
        self.ends = [(self.sem("fm_act"), 4), (self.sem("fm_dve"), 4), (self.sem("step"), 18),
                     (self.sem("sines"), 2)]

    def sp(self, sp):
        sp.dma_start(self.k.cst[:, :], self.table).then_inc(self.sem("table"), 16)
        sp.dma_start(self.xtm[:, :].rearrange("p (t d) -> p t d", d=D),
                     self.x[0].rearrange("(t p) d -> p t d", p=P)).then_inc(self.sem("x"), 16)
        sp.dma_start(self.posi[:, :], self.positions.broadcast_to([P, T])).then_inc(self.sem("pos"), 16)

    def pe(self, pe):
        k = self.k
        pe.wait_ge(self.sem("table"), 16)
        pe.wait_ge(self.sem("x"), 16)
        for c in range(KD):
            for t in range(TT):
                tr = pe.transpose(k.ps[:, c, t * P:(t + 1) * P],
                                  self.xtm[:, t * D + c * P:t * D + (c + 1) * P], k.const(C_ID))
            tr.then_inc(self.sem("turned"), 1)

    def act(self, act):
        k = self.k
        for c in range(0, KD, 2):
            act.wait_ge(self.sem("turned"), c + 1)
            act.activation(k.xT[:, c * T:(c + 1) * T], k.ps[:, c, :], ACT.Copy).then_inc(self.sem("fm_act"), 1)
        act.wait_ge(self.sem("step"), 17)
        act.activation(k.sin[:, :], self.w[2][:, :], ACT.Sin).then_inc(self.sem("sines"), 1)
        act.activation(k.cos[:, :], self.w[3][:, :], ACT.Sin).then_inc(self.sem("sines"), 1)

    def dve(self, dve):
        k = self.k
        step = self.sem("step")
        done = 0

        def then(ins):
            nonlocal done
            done += 1
            ins.then_inc(step, 1)
            dve.wait_ge(step, done)
        dve.wait_ge(self.sem("table"), 16)
        dve.wait_ge(self.sem("pos"), 16)
        then(dve.memset(k.eps[:, :], EPS))
        pos, ang, rs, rc = (w[:, :] for w in self.w)
        then(dve.tensor_copy(pos, self.posi[:, :]))
        then(dve.tensor_scalar(ang, pos, k.cst[:, C_INV:C_INV + 1], None, ALU.mult))
        magic = 1.5 * 2 ** 23
        two_pi = 2 * math.pi
        hi = 6.28125
        for out, turn, shift in ((rs, 0.0, 0.0), (rc, 0.25, math.pi / 2)):
            then(dve.tensor_scalar(pos, ang, 1 / two_pi, turn, ALU.mult, ALU.add))
            then(dve.tensor_scalar(pos, pos, magic, None, ALU.add))
            then(dve.tensor_scalar(pos, pos, magic, None, ALU.subtract))
            then(dve.scalar_tensor_tensor(out, pos, -hi, ang, ALU.mult, ALU.add))
            then(dve.scalar_tensor_tensor(out, pos, -(two_pi - hi), out, ALU.mult, ALU.add))
            lim = 3.1415925
            then(dve.tensor_scalar(out, out, shift, lim, ALU.add, ALU.min))
            then(dve.tensor_scalar(out, out, -lim, None, ALU.max))
        for c in range(1, KD, 2):
            dve.wait_ge(self.sem("turned"), c + 1)
            dve.tensor_copy(k.xT[:, c * T:(c + 1) * T], k.ps[:, c, :]).then_inc(self.sem("fm_dve"), 1)
        dve.wait_ge(self.sem("sines"), 2)
        dve.tensor_scalar(k.cos[:, :], k.cos[:, :], k.cst[:, C_MSK:C_MSK + 1], k.cst[:, C_UNM:C_UNM + 1],
                          ALU.mult, ALU.add).then_inc(step, 1)


class SsdPrep(Stage):

    def __init__(self, k, name, prev, c, xs, bt, cb, rows, s):
        super().__init__(k, name, prev)
        self.c, self.xs, self.bt, self.cb, self.rows, self.s = c, xs, bt, cb, rows, s
        self.ends = [(self.sem("tm_act"), 5), (self.sem("tm_dve"), 5), (self.sem("step"), 10),
                     (self.sem("exps"), 4), (self.sem("cb"), 2)]

    def pe(self, pe):
        k = self.k
        self.join(pe)
        for c in range(10):
            if c >= 2:
                pe.wait_ge(self.sem("tm_act" if c % 2 == 0 else "tm_dve"), c // 2)
            for t in range(TT):
                tr = pe.transpose(k.ps[:, 4 + c % 2, t * P:(t + 1) * P],
                                  self.c[:, c * T + t * P:c * T + (t + 1) * P], k.const(C_ID))
            tr.then_inc(self.sem("turned"), 1)
            self.side_pe(pe, c, 10)
        for g in range(SG):
            for t in range(TT):
                a = slice((8 + g) * T + t * P, (8 + g) * T + (t + 1) * P)
                b = slice((10 + g) * T + t * P, (10 + g) * T + (t + 1) * P)
                mm = pe.matmul(k.ps[:, 6 + g, t * P:(t + 1) * P], self.c[:, a], self.c[:, b],
                               start=True, stop=True)
            mm.then_inc(self.sem("products"), 1)
        pe.wait_ge(self.sem("step"), 1)
        pe.wait_ge(self.sem("tm_act"), 5)
        pe.wait_ge(self.sem("tm_dve"), 5)
        for t in range(TT):
            tr = pe.transpose(k.ps[0:SH, 4, t * P:(t + 1) * P], self.s["a"][:, t * SH:(t + 1) * SH],
                              k.const(C_ID))
        tr.then_inc(self.sem("arows"), 1)
        pe.wait_ge(self.sem("step"), 6)
        for t in range(TT):
            tr = pe.transpose(k.ps[:, 5, t * SH:(t + 1) * SH], self.rows[0:SH, T + t * P:T + (t + 1) * P],
                              k.const(C_ID)[0:SH, 0:SH])
        tr.then_inc(self.sem("cols"), 1)
        pe.wait_ge(self.sem("step"), 7)
        pe.wait_ge(self.sem("cb"), 1)
        last = k.cst[:, C_ID + P - 1:C_ID + P].broadcast_to([P, P])
        pe.matmul(k.ps[:, 6, 0:TT * SH], last, self.s["loc"], start=True, stop=True)\
          .then_inc(self.sem("total"), 1)

    def tm(self, c):
        if c < 8:
            return self.xs[:, :].rearrange("p (t f) -> p t f", t=TT)[:, :, c * P:(c + 1) * P]
        return self.bt[:, :].rearrange("p (t f) -> p t f", t=TT)[:, :, (c - 8) * P:(c - 7) * P]

    def act(self, act):
        k = self.k
        self.join(act)
        act.activation(self.s["A"], self.s["a_log"], ACT.Exp).then_inc(self.sem("exps"), 1)
        for c in range(0, 10, 2):
            self.side_out("act", act, c, 10)
            act.wait_ge(self.sem("turned"), c + 1)
            act.activation(self.tm(c), k.ps[:, 4, :].rearrange("p (t f) -> p t f", t=TT), ACT.Copy)\
               .then_inc(self.sem("tm_act"), 1)
        act.wait_ge(self.sem("step"), 9)
        act.activation(self.s["eloc"], self.s["loc"], ACT.Exp).then_inc(self.sem("exps"), 1)
        act.activation(self.s["etot"], self.s["tot"], ACT.Exp).then_inc(self.sem("exps"), 1)
        act.activation(self.s["dec"], self.s["dec"], ACT.Exp).then_inc(self.sem("exps"), 1)

    def dve(self, dve):
        k, s = self.k, self.s
        step = self.sem("step")
        self.join(dve)
        dve.wait_ge(self.sem("exps"), 1)
        h16 = lambda x: x.rearrange("p (t h) -> p t h", h=SH)
        dve.scalar_tensor_tensor(h16(s["a"]), h16(s["dt"]), -1.0,
                                 s["A"].unsqueeze(1).broadcast_to([P, TT, SH]), ALU.mult, ALU.mult)\
           .then_inc(step, 1)
        for c in range(1, 10, 2):
            dve.wait_ge(self.sem("turned"), c + 1)
            dve.tensor_copy(self.tm(c), k.ps[:, 5, :].rearrange("p (t f) -> p t f", t=TT))\
               .then_inc(self.sem("tm_dve"), 1)
        for g in range(SG):
            dve.wait_ge(self.sem("products"), g + 1)
            dve.tensor_tensor(self.cb[:, g * T:(g + 1) * T].rearrange("p (t f) -> p t f", f=P),
                              k.ps[:, 6 + g, :].rearrange("p (t f) -> p t f", f=P),
                              k.const(C_KEEP).unsqueeze(1).broadcast_to([P, TT, P]), ALU.mult)\
               .then_inc(self.sem("cb"), 1)
        dve.wait_ge(self.sem("arows"), 1)
        dve.tensor_copy(self.rows[0:SH, 0:T], k.ps[0:SH, 4, :]).then_inc(step, 1)
        dve.wait_ge(step, 2)
        for t in range(TT):
            dve.tensor_tensor_scan(self.rows[0:SH, T + t * P:T + (t + 1) * P], k.ones(SH, P),
                                   self.rows[0:SH, t * P:(t + 1) * P], 0.0, ALU.mult, ALU.add)\
               .then_inc(step, 1)
        dve.wait_ge(self.sem("cols"), 1)
        dve.tensor_copy(s["loc"], k.ps[:, 5, 0:TT * SH]).then_inc(step, 1)
        dve.wait_ge(self.sem("total"), 1)
        dve.tensor_copy(s["tot"], k.ps[:, 6, 0:TT * SH]).then_inc(step, 1)
        dve.wait_ge(step, 8)
        dve.tensor_tensor(s["dec"], s["tot"], s["loc"], ALU.subtract).then_inc(step, 1)
        dve.wait_ge(self.sem("exps"), 4)
        dve.tensor_tensor(s["dtdec"], s["dt"], s["dec"], ALU.mult).then_inc(step, 1)


class Ssd(Stage):

    def __init__(self, k, name, prev, c, xs, bt, cb, rows, s, sz, scr):
        super().__init__(k, name, prev)
        self.c, self.xs, self.bt, self.cb, self.rows, self.s, self.sz = c, xs, bt, cb, rows, s, sz
        self.xdt = k.at(f"{name}_xdt", scr, D)
        self.xdd = k.at(f"{name}_xdecayed", scr + D, D)
        self.e = k.at(f"{name}_decay", scr + 2 * D, 2 * D)
        self.state = k.at(f"{name}_state", scr + 4 * D, D)
        self.y = k.at(f"{name}_y", scr + 5 * D, D)
        self.ends = [(self.sem("normed"), TT)]

    STEPS = 4 * TT

    def pe(self, pe):
        k = self.k
        self.join(pe)
        for t in range(TT):
            if t:
                pe.wait_ge(self.sem("within_read"), t)
                pe.wait_ge(self.sem("state"), t)
            for g in range(SG):
                for h in range(g * SPG, (g + 1) * SPG):
                    mm = pe.matmul(k.ps[:, 4 + h // 4, h % 4 * P:(h % 4 + 1) * P], k.pick(h, SH),
                                   self.rows[0:SH, T + t * P:T + (t + 1) * P], start=True, stop=True)
                mm.then_inc(self.sem("sums"), 1)
            self.side_pe(pe, 4 * t, self.STEPS)
            if t:
                pe.wait_ge(self.sem("gap"), SG * t + 1)
                for g in range(SG):
                    mm = pe.matmul(k.ps[:, 4 + g, :], self.c[:, (10 + g) * T + t * P:(10 + g) * T + (t + 1) * P],
                                   self.state[:, g * 512:(g + 1) * 512], start=True, stop=True)
                mm.then_inc(self.sem("across"), 1)
            self.side_pe(pe, 4 * t + 1, self.STEPS)
            pe.wait_ge(self.sem("gap"), SG * (t + 1))
            if t < TT - 1:
                pe.wait_ge(self.sem("xdd"), t + 1)
                for g in range(SG):
                    mm = pe.matmul(k.ps[:, 6 + g, :], self.bt[:, t * 256 + g * P:t * 256 + (g + 1) * P],
                                   self.xdd[:, g * 512:(g + 1) * 512], start=True, stop=True)
                mm.then_inc(self.sem("states"), 1)
            self.side_pe(pe, 4 * t + 2, self.STEPS)
            pe.wait_ge(self.sem("xdt"), t + 1)
            pe.wait_ge(self.sem("weighted"), SG * (t + 1))
            if t:
                pe.wait_ge(self.sem("off"), t)
            for h in range(SH):
                mm = pe.matmul(k.ps[:, 4 + h // SPG, h % SPG * SHD:(h % SPG + 1) * SHD],
                               self.e[:, h * P:(h + 1) * P], self.xdt[:, h * SHD:(h + 1) * SHD],
                               start=True, stop=True)
            mm.then_inc(self.sem("within"), 1)
            self.side_pe(pe, 4 * t + 3, self.STEPS)

    def dve(self, dve):
        k, s = self.k, self.s
        self.join(dve)
        hd = lambda x: x.rearrange("p (h d) -> p h d", d=SHD)
        bank = lambda b: k.ps[:, b:b + 2, :].rearrange("p b (h d) -> p (b h) d", d=SHD)
        per_head = lambda x, t, w: x[:, t * SH:(t + 1) * SH].unsqueeze(2).broadcast_to([P, SH, w])
        y, xdt = hd(self.y[:, :]), hd(self.xdt[:, :])
        local = self.sem("local")
        n = 0
        for t in range(TT):
            x = hd(self.xs[:, t * D:(t + 1) * D])
            if t:
                dve.wait_ge(self.sem("within"), t)
            for g in range(SG):
                dve.wait_ge(self.sem("sums"), SG * t + g + 1)
                dve.tensor_tensor(self.e[:, g * D:(g + 1) * D].rearrange("p (h t) -> p h t", t=P),
                                  k.ps[:, 4 + 2 * g:6 + 2 * g, :].rearrange("p b (h t) -> p (b h) t", t=P),
                                  s["loc"][:, t * SH + g * SPG:t * SH + (g + 1) * SPG].unsqueeze(2)
                                  .broadcast_to([P, SPG, P]), ALU.subtract).then_inc(self.sem("gap"), 1)
            for g in range(SG):
                e = self.e[:, g * D:(g + 1) * D]
                dve.wait_ge(self.sem("gap"), SG * t + g + 1)
                dve.tensor_scalar(e, e, 0.0, None, ALU.min).then_inc(self.sem("min"), 1)
            if t:
                dve.wait_ge(self.sem("states"), t)
            dve.tensor_tensor(hd(self.xdd[:, :]), x, per_head(s["dtdec"], t, SHD), ALU.mult)\
               .then_inc(self.sem("xdd"), 1)
            dve.tensor_tensor(xdt, x, per_head(s["dt"], t, SHD), ALU.mult).then_inc(self.sem("xdt"), 1)
            for g in range(SG):
                dve.wait_ge(self.sem("exp"), SG * t + g + 1)
                eg = self.e[:, g * D:(g + 1) * D].rearrange("p (h t) -> p h t", t=P)
                cb = self.cb[:, g * T + t * P:g * T + (t + 1) * P].unsqueeze(1).broadcast_to([P, SPG, P])
                dve.tensor_tensor(eg, eg, cb, ALU.mult).then_inc(self.sem("weighted"), 1)
            if t:
                dve.wait_ge(self.sem("across"), t)
                dve.wait_ge(self.sem("square"), t)
                dve.tensor_tensor(y, bank(4), per_head(s["eloc"], t, SHD), ALU.mult)\
                   .then_inc(self.sem("off"), 1)
            if t < TT - 1:
                st = hd(self.state[:, :])
                if t:
                    dve.tensor_tensor(st, st, per_head(s["etot"], t, SHD), ALU.mult)\
                       .then_inc(self.sem("aged"), 1)
                    dve.wait_ge(self.sem("aged"), t)
                dve.wait_ge(self.sem("states"), t + 1)
                if t:
                    dve.tensor_tensor(st, st, bank(6), ALU.add).then_inc(self.sem("state"), 1)
                else:
                    dve.tensor_copy(st, bank(6)).then_inc(self.sem("state"), 1)
            dve.wait_ge(self.sem("within"), t + 1)
            if t:
                dve.wait_ge(self.sem("off"), t)
                dve.tensor_tensor(y, y, bank(4), ALU.add).then_inc(self.sem("within_read"), 1)
            else:
                dve.tensor_copy(y, bank(4)).then_inc(self.sem("within_read"), 1)
            dve.tensor_tensor(xdt, x, s["D"].unsqueeze(2).broadcast_to([P, SH, SHD]), ALU.mult)\
               .then_inc(local, 1)
            n += 1
            dve.wait_ge(local, n)
            dve.wait_ge(self.sem("within_read"), t + 1)
            dve.tensor_tensor(y, y, xdt, ALU.add).then_inc(local, 1)
            n += 1
            dve.wait_ge(local, n)
            z = self.sz[:, t * D:(t + 1) * D]
            dve.tensor_tensor(z, z, self.y[:, :], ALU.mult).then_inc(self.sem("gated"), 1)
        dve.wait_ge(self.sem("root"), 1)
        dve.reciprocal(k.stat[:, 8:12], k.stat[:, 4:8]).then_inc(local, 1)
        dve.wait_ge(local, n + 1)
        for t in range(TT):
            z = self.sz[:, t * D:(t + 1) * D]
            dve.tensor_scalar(z, z, k.stat[:, 8 + t:9 + t], None, ALU.mult).then_inc(self.sem("normed"), 1)

    def act(self, act):
        k = self.k
        self.join(act)
        for t in range(TT):
            self.side_out("act", act, 4 * t, self.STEPS)
            for g in range(SG):
                e = self.e[:, g * D:(g + 1) * D]
                act.wait_ge(self.sem("min"), SG * t + g + 1)
                act.activation(e, e, ACT.Exp).then_inc(self.sem("exp"), 1)
            self.side_out("act", act, 4 * t + 3, self.STEPS)
            act.wait_ge(self.sem("gated"), t + 1)
            act.activation(self.y[:, :], self.sz[:, t * D:(t + 1) * D], ACT.Square,
                           accum_out=k.stat[:, t:t + 1]).then_inc(self.sem("square"), 1)
        act.wait_ge(self.sem("square"), TT)
        act.activation(k.stat[:, 4:8], k.stat[:, 0:4], ACT.Sqrt, bias=k.eps[:, 0:1], scale=1.0 / D)\
           .then_inc(self.sem("root"), 1)


class SsdOut(Stage):

    def __init__(self, k, name, prev, y, wcol, yhi, ylo):
        super().__init__(k, name, prev)
        self.y, self.wcol, self.yhi, self.ylo = y, wcol, yhi, ylo
        self.ends = [(self.sem("lo"), KD)]

    def pe(self, pe):
        k = self.k
        self.join(pe)
        for c in range(KD):
            if c >= 4:
                pe.wait_ge(self.sem("lo"), c - 3)
            for t in range(TT):
                tr = pe.transpose(k.ps[:, 4 + c % 4, t * P:(t + 1) * P], self.y[:, t * D + c * P:t * D + (c + 1) * P],
                                  k.const(C_ID))
            tr.then_inc(self.sem("turned"), 1)

    def act(self, act):
        k = self.k
        self.join(act)
        for c in range(KD):
            act.wait_ge(self.sem("turned"), c + 1)
            act.activation(self.yhi[:, c * T:(c + 1) * T], k.ps[:, 4 + c % 4, :], ACT.Copy,
                           scale=k.col(self.wcol + c)).then_inc(self.sem("hi"), 1)

    def dve(self, dve):
        k = self.k
        self.join(dve)
        for c in range(KD):
            dve.wait_ge(self.sem("hi"), c + 1)
            dve.scalar_tensor_tensor(self.ylo[:, c * T:(c + 1) * T], k.ps[:, 4 + c % 4, :], k.col(self.wcol + c),
                                     self.yhi[:, c * T:(c + 1) * T], ALU.mult, ALU.subtract)\
               .then_inc(self.sem("lo"), 1)


class PoolMix(Stage):

    def __init__(self, k, name, prev, u, a, b, pooled, wsrc, w, scol, yhi, ylo):
        super().__init__(k, name, prev)
        self.u, self.ab, self.pooled, self.wsrc, self.w = u, (a, b), pooled, wsrc, w
        self.scol, self.yhi, self.ylo = scol, yhi, ylo
        self.ends = [(self.sem("lo"), len(WINDOWS))]

    def pe(self, pe):
        k = self.k
        self.join(pe)
        self.side_pe(pe, 0, 5)
        for g in range(len(WINDOWS)):
            pe.wait_ge(self.sem("pooled"), g + 1)
            if g == 0:
                pe.wait_ge(self.sem("weights"), 16)
            pe.matmul(k.ps[:, 4 + g, :], self.w[:, g * P:(g + 1) * P], self.pooled[:, g * T:(g + 1) * T],
                      start=True, stop=True).then_inc(self.sem("mixed"), 1)
            self.side_pe(pe, g + 1, 5)

    def act(self, act):
        k = self.k
        self.join(act)
        act.dma_start(self.w[:, :].rearrange("p (g d) -> p g d", d=P), self.wsrc).then_inc(self.sem("weights"), 16)
        for g in range(len(WINDOWS)):
            self.side_out("act", act, g + 1, 5)
            act.wait_ge(self.sem("mixed"), g + 1)
            act.activation(self.yhi[:, g * T:(g + 1) * T], k.ps[:, 4 + g, :], ACT.Copy,
                           scale=k.col(self.scol + g)).then_inc(self.sem("hi"), 1)

    def dve(self, dve):
        k = self.k
        self.join(dve)
        step = self.sem("step")
        n, pad = 0, 16
        for g, win in enumerate(WINDOWS):
            tile = self.u[:, g * (T + pad):(g + 1) * (T + pad)]
            src, shift, side = tile, 1, 0
            self.side_out("dve", dve, g + 1, 5)
            if g:
                dve.wait_ge(self.sem("pooled"), g)
            while shift < win:
                dst = self.ab[side][:, :]
                dve.tensor_tensor(dst[:, pad:], src[:, pad:], src[:, pad - shift:T + pad - shift], ALU.add)\
                   .then_inc(step, 1)
                n += 1
                dve.wait_ge(step, n)
                src, shift, side = dst, 2 * shift, 1 - side
            out = self.pooled[:, g * T:(g + 1) * T]
            dve.scalar_tensor_tensor(out, src[:, pad:], 1.0 / win, tile[:, pad:], ALU.mult, ALU.subtract)\
               .then_inc(step, 1)
            head = self.ab[side][:, pad:2 * pad]
            dve.tensor_tensor(head, src[:, pad:2 * pad], k.cst[:, C_CNT + 16 * g:C_CNT + 16 * (g + 1)],
                              ALU.mult).then_inc(step, 1)
            n += 2
            dve.wait_ge(step, n)
            dve.tensor_tensor(out[:, 0:16], head, tile[:, pad:2 * pad], ALU.subtract)\
               .then_inc(self.sem("pooled"), 1)
        for g in range(len(WINDOWS)):
            dve.wait_ge(self.sem("hi"), g + 1)
            dve.scalar_tensor_tensor(self.ylo[:, g * T:(g + 1) * T], k.ps[:, 4 + g, :],
                                     k.col(self.scol + g), self.yhi[:, g * T:(g + 1) * T],
                                     ALU.mult, ALU.subtract).then_inc(self.sem("lo"), 1)


class Dup(Stage):

    def __init__(self, k, name, prev, pairs):
        super().__init__(k, name, prev)
        self.pairs = pairs
        self.ends = [(self.sem("copied"), 16 * len(pairs))]

    def act(self, act):
        self.join(act)
        for dst, src in self.pairs:
            act.dma_start(dst, src).then_inc(self.sem("copied"), 16)


class Select(Stage):

    def __init__(self, k, name, prev, qi, ki, wi, r, sc, m8):
        super().__init__(k, name, prev)
        self.qi, self.ki, self.wi, self.r, self.sc, self.m8 = qi, ki, wi, r, sc, m8
        self.ends = [(self.sem("mask"), TT - 1)]

    DOTS = (TT - 1) * IH
    STEPS = DOTS + TOPK // 8

    def pe(self, pe):
        k = self.k
        self.join(pe)
        for n in range((TT - 1) * IH):
            i, h = n // IH + 1, n % IH
            if n >= 2:
                pe.wait_ge(self.sem("relu"), n - 1)
            r = slice(h % 2 * HD, (h % 2 + 1) * HD)
            pe.matmul(k.ps[:, 4 + n % 2, 0:(i + 1) * P], self.qi[r, h // 2 * T + i * P:h // 2 * T + (i + 1) * P],
                      self.ki[r, 0:(i + 1) * P], start=True, stop=True).then_inc(self.sem("dots"), 1)
            self.side_pe(pe, n, self.STEPS)
        self.side_pe(pe, self.STEPS - 1, self.STEPS)

    def act(self, act):
        k = self.k
        self.join(act)
        for n in range((TT - 1) * IH):
            w = (n // IH + 2) * P
            self.side_out("act", act, n, self.STEPS)
            act.wait_ge(self.sem("dots"), n + 1)
            if n >= 2:
                act.wait_ge(self.sem("score"), n - 1)
            act.activation(self.r[:, n % 2 * T:n % 2 * T + w], k.ps[:, 4 + n % 2, 0:w], ACT.Relu)\
               .then_inc(self.sem("relu"), 1)
        self.side_out("act", act, self.STEPS, self.STEPS)

    def score(self, i):
        return self.sc[:, (i - 1) * T:(i - 1) * T + (i + 1) * P]

    def dve(self, dve):
        k = self.k
        self.join(dve)
        for n in range((TT - 1) * IH):
            i, h = n // IH + 1, n % IH
            w = (i + 1) * P
            self.side_out("dve", dve, n, self.STEPS)
            sc, r = self.score(i), self.r[:, n % 2 * T:n % 2 * T + w]
            wi = self.wi[:, i * IH + h:i * IH + h + 1]
            dve.wait_ge(self.sem("relu"), n + 1)
            if h:
                dve.wait_ge(self.sem("score"), n)
                dve.scalar_tensor_tensor(sc, r, wi, sc, ALU.mult, ALU.add).then_inc(self.sem("score"), 1)
            else:
                dve.tensor_scalar(sc, r, wi, None, ALU.mult).then_inc(self.sem("score"), 1)
        dve.wait_ge(self.sem("score"), (TT - 1) * IH)
        for i in range(1, TT):
            d = self.score(i)[:, i * P:(i + 1) * P]
            dve.tensor_tensor(d, d, k.const(C_QK), ALU.subtract).then_inc(self.sem("causal"), 1)
        dve.wait_ge(self.sem("causal"), TT - 1)

        def largest(i):
            dve.max(self.m8[:, 8 * i:8 * i + 8], self.score(i)).then_inc(self.sem("largest"), 1)

        def take(i, value):
            dve.wait_ge(self.sem("largest"), value)
            dve.match_replace(self.score(i), self.m8[:, 8 * i:8 * i + 8], self.score(i), TAKEN)\
               .then_inc(self.sem("taken"), 1)
        for i in range(1, TT):
            largest(i)
        for i in range(1, TT):
            take(i, i)
        for r in range(1, TOPK // 8):
            self.side_out("dve", dve, self.DOTS + r, self.STEPS)
            for i in range(1, TT):
                dve.wait_ge(self.sem("taken"), (TT - 1) * (r - 1) + i)
                largest(i)
            for i in range(1, TT):
                take(i, (TT - 1) * r + i)
        dve.wait_ge(self.sem("taken"), (TT - 1) * (TOPK // 8))
        for i in range(1, TT):
            dve.tensor_scalar(self.score(i), self.score(i), TAKEN / 1.5, BIG, ALU.is_gt, ALU.mult)\
               .then_inc(self.sem("mask"), 1)


class Store(Stage):

    def __init__(self, k, name, prev, norm, out):
        super().__init__(k, name, prev)
        self.norm, self.out = norm, out
        self.y = k.at("store_y", 0, TT * D)

    def pe(self, pe):
        k = self.k
        for c in range(KD):
            pe.wait_ge(self.norm.ready, c + 1)
            for t in range(TT):
                tr = pe.transpose(k.ps[:, 2 * t + c // 4, c % 4 * P:(c % 4 + 1) * P],
                                  k.xT[:, c * T + t * P:c * T + (t + 1) * P], k.const(C_ID))
                if c % 4 == 3:
                    tr.then_inc(self.sem("turned"), 1)

    def half(self, t, b):
        return self.y[:, t * D + b * 512:t * D + (b + 1) * 512]

    def act(self, act):
        self.join(act)
        for t in range(TT):
            act.wait_ge(self.sem("turned"), t + 1)
            act.activation(self.half(t, 0), self.k.ps[:, 2 * t, :], ACT.Copy).then_inc(self.sem("low"), 1)

    def dve(self, dve):
        self.join(dve)
        for t in range(TT):
            dve.wait_ge(self.sem("turned"), TT + t + 1)
            dve.tensor_copy(self.half(t, 1), self.k.ps[:, 2 * t + 1, :]).then_inc(self.sem("high"), 1)

    def sp(self, sp):
        for t in range(TT):
            sp.wait_ge(self.sem("low"), t + 1)
            sp.wait_ge(self.sem("high"), t + 1)
            sp.dma_start(self.out[0, t * P:(t + 1) * P, :], self.y[:, t * D:(t + 1) * D])\
              .then_inc(self.sem("stored"), 16)
        sp.wait_ge(self.sem("stored"), 16 * TT)



def weight(w, l, r0, rows, c0, cols):
    v = w[bass.ds(l, 1), r0:r0 + rows, bass.ds(c0, cols)] if isinstance(r0, int) else \
        w[bass.ds(l, 1), bass.ds(r0, rows), bass.ds(c0, cols)]
    return v.rearrange("l (k p) n -> p (l k) n", p=P)


def rows_of(w, l, a, n):
    return w[bass.ds(l, 1), a:a + n * P].rearrange("l (a p) -> (l a) p", p=P)


def emit(k, stages, lead=None):
    nc = k.nc
    with nc.Block(no_gpsimd_drain=True) as block:
        @block.sync
        def _(sp):
            for s in stages:
                s.sp(sp)

        @block.scalar
        def _(act):
            if lead:
                hi_unit(k, act, 0, 0)
                hi_unit(k, act, 1, 0)
            for s in stages:
                s.act(act)

        @block.vector
        def _(dve):
            for s in stages:
                s.dve(dve)

        @block.tensor
        def _(pe):
            for s in stages:
                s.pe(pe)

        if lead:
            @block.gpsimd
            def _(pool):
                lo_units(k, pool, k.units)


BESIDE1 = {"rope": 10, "att": 39, "conv": 8, "forget": 4, "gates": 4, "mlstm": 20}
BESIDE2 = {"conv": 20, "dt": 4, "prep": 8, "ssd": 32, "dup": 2, "select": 48, "att": 28, "pool": 8}


def first_layer(k, l, A):
    k.stream_sems("first")
    st = []

    def add(cls, name, *a, prev=None, **kw):
        st.append(cls(k, name, st[-1:] if prev is None else prev, *a, **kw))
        return st[-1]
    o_qk, o_v = 0, 4096
    o_mv = o_v + 2048
    o_mo = o_mv + TT * MH * (MD + 1)
    o_cv = o_mo + 2048
    o_ya = up8(o_cv + 8 * (T + CONV - 1))
    o_scr = o_ya + 4096
    o_vb = o_scr + 6144
    qk = k.at("qk", o_qk, 8 * T)
    v = k.at("v", o_v, TT * 512)
    mv = k.at("mv", o_mv, TT * MH * (MD + 1))
    mo = k.at("mo", o_mo, 4 * T)
    cv = k.at("conv_in", o_cv, 8 * (T + CONV - 1))
    mqk = k.at("conv_out", o_qk, 8 * T)
    vb = k.at("token_bias", o_vb, 1032)
    k.tmp = k.at("softplus_tmp", o_scr, 512)
    k.gr = k.at("gate_rows", o_scr + Mlstm.H_AT, 4 * T)
    prow = k.at("param_rows", o_vb + 1032, P)
    ya = [k.at(f"ya_{p}", o_ya + i * 2048, 2048, F32R) for i, p in enumerate(("hi", "lo"))]
    yb = [k.at(f"yb_{p}", o_qk + i * 2048, 2048, F32R) for i, p in enumerate(("hi", "lo"))]
    NMIX, CW, CB, MN, NMLP, B1, B2 = 0, 8, 40, 48, 52, 60, 88
    cw = A["conv_w"][bass.ds(l, 1), :, :].rearrange("l j (a p) -> (l j a) p", p=P)
    params = add(Params, "params", [
        (rows_of(A["norm_mix_w"], l, 0, 8), NMIX, 8), (cw, CW, 32), (rows_of(A["conv_b"], l, 0, 8), CB, 8),
        (rows_of(A["mlstm_norm_w"], l, 0, 4), MN, 4), (rows_of(A["norm_mlp_w"], l, 0, 8), NMLP, 8),
        (rows_of(A["b_in"], l, 0, 28), B1, 28), (rows_of(A["b_in"], l, GA, 16), B2, 16)],
        [(vb[:, a:a + n], A["b_in"][bass.ds(l, 1), c:c + n].broadcast_to([P, n]))
         for a, c, n in ((0, AV, 512), (512, MV, 512), (1024, MI, 8))], prow, half=(B1 + 24, 20))
    norm = add(Norm, "norm_mix", NMIX)
    cv3 = cv[:, :].rearrange("p (t w) -> p t w", w=T + CONV - 1)
    fill = add(Fill, "fill", [(mv[:, :], 1.0), (cv3[:, :, 0:CONV - 1], 0.0)], params.spread)
    w_in = A["w_in"]

    def src(c0):
        return lambda j, i: weight(w_in, l, 0, D, i * (2 * UC) + (c0 + j * UC), UC)

    def fm_out(dst, w, pad, bcol, func):
        def evac(act, j, i, bank):
            for c in range(UT):
                ins = act.activation(dst[:, bass.ds(i * (4 * w) + (2 * j + c) * w + pad, T)], k.ps[:, bank + c, :],
                                     func, bias=k.pcol[:, bass.ds(i * 4 + bcol + 2 * j + c, 1)])
            return ins
        return evac

    def v_out(dve, j, i, bank):
        return dve.tensor_tensor(
            v[:, :].rearrange("p (t f) -> p t f", t=TT)[:, :, j * UC:(j + 1) * UC],
            k.ps[:, bank:bank + 2, :].rearrange("p b (t f) -> p (b t) f", t=2),
            vb[:, j * UC:(j + 1) * UC].unsqueeze(1).broadcast_to([P, TT, UC]), ALU.add)
    proj = add(Project, "proj", norm, [
        Seg("fm", 4, src(AQ), UC, fm_out(qk, T, 0, B1, ACT.Identity), loop=True),
        Seg("tm", 2, src(AV), UC, v_out, eng="dve")], prev=[fill])

    g, merged = k.at("gate", o_scr + Mlstm.SCRATCH, 4 * T), k.at("merged", o_cv, 8 * T)
    side = add(Branches, "side", g, merged)

    def plain(c0, cols, jobs):
        return side.unit(weight(w_in, l, 0, D, c0, cols), KD, cols, k.hh, k.hl, jobs)

    def conv_in(t):
        a = t * (T + CONV - 1) + CONV - 1
        return Job("act", lambda act, bank: act.activation(
            cv[:, a:a + T], k.ps[:, bank, :], ACT.Identity, bias=k.col(B1 + 12 + t)), c=t % UT)

    def values(j, half):
        def evac(dve, bank):
            dst = mv[:, :].rearrange("p (t h d) -> p t h d", h=MH, d=MD + 1)[:, 2 * half:2 * half + 2,
                                                                             2 * j:2 * j + 2, 0:MD]
            bias = vb[:, 512 + j * UC:512 + (j + 1) * UC].rearrange("p (h d) -> p h d", d=MD)
            src = k.ps[:, bank, :].rearrange("p (t h d) -> p t h d", t=2, h=2)
            for t in range(2):
                ins = dve.tensor_tensor(dst[:, t], src[:, t], bias, ALU.add)
            return ins
        return Job("dve", evac, tm=(2 * half, 2 * half + 2, 0, UC, UC))

    def out_gate(t):
        return Job("act", lambda act, bank: act.activation(
            mo[:, t * T:(t + 1) * T], k.ps[:, bank, :], ACT.Tanh, scale=0.5, bias=k.hbias[:, t:t + 1]), c=t % UT)
    g8 = k.small[:, 0:32]

    def gate_out(dve, bank):
        return dve.tensor_tensor(
            g8.rearrange("p (t f) -> p t f", f=8), k.ps[:, bank, 0:32].rearrange("p (t f) -> p t f", f=8),
            vb[:, 1024:1032].unsqueeze(1).broadcast_to([P, TT, 8]), ALU.add)
    for j in range(4):
        conv_at = plain(MQ + j * UC, UC, [conv_in(2 * j), conv_in(2 * j + 1)])
    gates_at = plain(MI, 8, [Job("dve", gate_out, tm=(0, TT, 0, 8, 8))])
    for j in range(2):
        values_at = plain(MV + j * UC, UC, [values(j, 0), values(j, 1)])
    for j in range(2):
        plain(MO + j * UC, UC, [out_gate(2 * j), out_gate(2 * j + 1)])
    mo_ready = side.ends_at()

    t1, t2 = k.at("rope_cos", o_scr, 2 * T), k.at("rope_sin", o_scr + 2 * T, 2 * T)
    at = 0
    rope = add(Rope, "rope", qk, t1, t2, prev=[proj])
    at = rope.beside(side, at, BESIDE1["rope"])

    def head(x, t0):
        return lambda h: x[h % 2 * HD:(h % 2 + 1) * HD, (t0 + h // 2) * T:(t0 + h // 2 + 1) * T]
    att = add(Attention, "att", head(qk, 0), head(qk, 4), lambda b, h: v[:, b * 512 + h * HD:b * 512 + (h + 1) * HD],
              lambda i: k.cst[:, C_PAT + (TT - 1 - i) * P:C_PAT + TT * P], o_scr, o_mo, *ya)
    at = att.beside(side, at, BESIDE1["att"])

    def tiles(x):
        return lambda i: x[:, i * T:(i + 1) * T]

    rest = add(Rest, "to_conv", side, conv_at)
    conv = add(Conv, "conv", cv, mqk, 8, CW, CB)
    at = conv.beside(side, max(at, conv_at), BESIDE1["conv"])
    rest = add(Rest, "to_gates", side, gates_at)
    spf = k.small[:, 32:48]
    forget = add(Softplus, "forget", None, spf, 16, lambda dve, x2: dve.tensor_scalar(
        x2.rearrange("p (t f) -> p t f", f=MH), g8.rearrange("p (t f) -> p t f", f=8)[:, :, MH:2 * MH],
        -1.0, None, ALU.mult))
    at = forget.beside(side, at, BESIDE1["forget"])
    gates = add(Gates, "gates", spf, g8)
    at = gates.beside(side, at, BESIDE1["gates"])
    rest = add(Rest, "to_mlstm", side, values_at)
    mlstm = add(Mlstm, "mlstm", mqk, mv, mo, mo_ready, o_scr, o_v, *yb, MN)
    at = mlstm.beside(side, at, BESIDE1["mlstm"])

    for n, (b0, gcol, w, y, need) in enumerate(((4, GA, "w_proj_att", ya, att), (12, GB, "w_proj_mlstm", yb, mlstm))):
        for half in range(2):
            side.gate(lambda c, gcol=gcol: weight(w_in, l, 0, D, gcol + c, UC), half,
                      bias=lambda t, b0=b0: k.hbias[:, b0 + t:b0 + t + 1], free=att.ends)
            side.up(lambda c, cols, w=w: weight(A[w], l, 0, 512, c, cols), 4, (tiles(y[0]), tiles(y[1])), half,
                    n > 0, need=need.ends if half == 0 else (), free=conv.ends)
    add(Rest, "branches", side)
    mix = [k.at(f"mixed_{p}", at, 4096, F32R) for at, p in ((o_ya, "hi"), (o_v, "lo"))]
    split = add(Split, "split_mixed", merged, *mix, 8, lambda t: side.read(side.final[t]))
    proj = add(OutProj, "out", lambda c, n: weight(A["w_out"], l, 0, D, c, n), split, tiles(mix[0]), tiles(mix[1]))
    proj.stats = add(Stats, "stats_mlp", proj.tile, emitted=True)
    norm = add(Norm, "norm_mlp", NMLP)
    f = [k.at(f"ff_{p}", i * 8192, 8192, F32R) for i, p in enumerate(("hi", "lo"))]
    scr = [k.at(f"ff_{p}", 16384 + i * 2048, 2048) for i, p in enumerate(("relu", "square"))]
    before = norm
    for half in range(2):
        up = add(Up, f"up{half}", before, lambda j, i, half=half: weight(
            A["w_ff1"], l, 0, D, i * UC + (half * DFF // 2 + j * UC), UC), 8, *f, scr)
        before = add(Down, f"down{half}", up, lambda j, i, half=half: weight(
            A["w_ff2"], l, i * 256 + (half * DFF // 2 + j * 256), 256, 0, D), 8, *f, last=half == 1)
    before.stats = add(Stats, "stats_next", before.tile, emitted=True)
    return st


def second_layer(k, A, out):
    k.stream_sems("second")
    st = []
    l = 0

    def add(cls, name, *a, prev=None, **kw):
        st.append(cls(k, "s_" + name, st[-1:] if prev is None else prev, *a, **kw))
        return st[-1]
    W = T + CONV - 1
    o_sz = up8(12 * W)
    o_c = o_sz + 4096
    o_scr = o_c + 12 * T
    o_small = o_scr + 6 * D + 1024
    o_rows = o_small + 1088
    xbc = k.at("s_conv_in", 0, 12 * W)
    xs, bt = k.at("s_x_tm", 0, 4096), k.at("s_b_tm", 4096, 1024)
    sz = k.at("s_silu_z", o_sz, 4096)
    c = k.at("s_conv_out", o_c, 12 * T)
    cb = k.at("s_cb", o_scr + 6 * D, 1024)
    k.tmp = k.at("s_softplus_tmp", o_scr, 512)
    rows = k.at("s_rows", o_rows, 2 * T)
    prow = k.at("s_param_rows", o_rows + 2 * T, P)
    sm = k.at("s_small", o_small, 1088)
    s, at = {}, 0
    for n, w in (("dt_raw", 64), ("dt", 64), ("a", 64), ("loc", 64), ("tot", 64), ("eloc", 64), ("etot", 64),
                 ("dec", 64), ("dtdec", 64)):
        s[n] = sm[:, at:at + w]
        at += w
    per_head = k.at("s_per_head", o_rows + 2 * T + P, 4 * SH)
    for i, n in enumerate(("a_log", "A", "D", "dt_bias")):
        s[n] = per_head[:, i * SH:(i + 1) * SH]
    FIN1, N1, CW, CB, SN, PS, N2, FIN2 = 0, 8, 16, 64, 76, 84, 88, 96
    params = add(Params, "params", [
        (A["final_norm_w"].rearrange("(a p) -> a p", p=P), FIN1, 8), (rows_of(A["norm1_w_2"], l, 0, 8), N1, 8),
        (A["conv_w_2"][0].rearrange("j (a p) -> (j a) p", p=P), CW, 48), (rows_of(A["conv_b_2"], l, 0, 12), CB, 12),
        (rows_of(A["ssd_norm_w_2"], l, 0, 8), SN, 8), (rows_of(A["pool_scale_2"], l, 0, 4), PS, 4),
        (rows_of(A["norm2_w_2"], l, 0, 8), N2, 8),
        (A["final_norm_w_2"].rearrange("(a p) -> a p", p=P), FIN2, 8)],
        [(s[n], A[x][0:1, :].broadcast_to([P, SH])) for n, x in (("dt_bias", "dt_bias_2"), ("a_log", "a_log_2"),
                                                              ("D", "d_skip_2"))], prow)
    norm = add(Norm, "norm_first", FIN1, final=True)
    add(Stats, "stats1", lambda t, norm=norm: (norm.ready, t + 1))
    norm = add(Norm, "norm1", N1)
    xbc3 = xbc[:, :].rearrange("p (t w) -> p t w", w=W)
    fill = add(Fill, "fill", [(xbc3[:, :, 0:CONV - 1], 0.0)], params.spread)
    w_in = A["w_in_2"]

    def src(c0):
        return lambda j, i: weight(w_in, l, 0, D, i * (2 * UC) + (c0 + j * UC), UC)

    def pair(bank):
        return k.ps[:, bank:bank + 2, :]

    def fm_out(dst, w, pad, scale=1.0):
        def evac(act, j, i, bank):
            return act.activation(
                dst[:, bass.ds(i * (4 * w) + 2 * j * w, 2 * w)].rearrange("p (c w) -> p c w", c=2)[:, :, pad:pad + T],
                pair(bank), ACT.Copy, scale=scale)
        return evac

    def dt_out(dve, j, i, bank):
        return dve.tensor_tensor(
            s["dt_raw"].rearrange("p (t f) -> p t f", f=SH),
            pair(bank).rearrange("p b (t f) -> p (b t) f", t=2)[:, :, 0:SH],
            s["dt_bias"].unsqueeze(1).broadcast_to([P, TT, SH]), ALU.add)
    add(Project, "proj_ssd", norm, [
        Seg("fm", 6, src(XBC2), UC, fm_out(xbc, W, CONV - 1), loop=True),
        Seg("tm", 1, lambda j, i: weight(w_in, l, 0, D, DT2, SH), SH, dt_out, eng="dve")], prev=[fill])

    q = k.at("s_q", o_c, 4 * T)
    kd = [k.at(f"s_k{i}", o_c + (4 + i) * T, T) for i in range(2)]
    qi = k.at("s_qi", o_c + 6 * T, 2 * T)
    v, ki = k.at("s_v", 10 * T, TT * P), k.at("s_ki", 11 * T, T)
    ys = [k.at(f"ys_{p}", o_scr + i * 4096, 4096, F32R) for i, p in enumerate(("hi", "lo"))]
    g, merged = k.at("s_gate", o_c + 8 * T, 4 * T), k.at("s_merged", 0, 8 * T)
    r, sc = k.at("s_relu", o_sz, 2 * T), k.at("s_scores", o_sz + 5 * T, 3 * T)
    yahi, yalo = k.at("s_ya_hi", o_sz, 4 * T, F32R), k.at("s_ya_lo", o_c, 4 * T, F32R)
    pad = 16
    u = k.at("s_u", o_scr + 14 * T, 4 * (T + pad))
    yp = [k.at(f"s_yp_{p}", o_scr + i * 2048, 2048, F32R) for i, p in enumerate(("hi", "lo"))]
    pooled, pw = k.at("s_pooled", o_scr + 8 * T, 4 * T), k.at("s_pool_w", o_scr + 12 * T, 4 * P)
    ab = [k.at(f"s_window{i}", o_sz + 5 * T + i * (T + pad), T + pad) for i in range(2)]
    wi, m8 = k.small[:, 0:16], k.small[:, 16:48]

    side = add(Branches, "side", g, merged)

    def plain(c0, cols, jobs):
        return side.unit(weight(w_in, l, 0, D, c0, cols), KD, cols, k.hh, k.hl, jobs)

    def silu_z(j, half):
        return Job("act", lambda act, bank: act.activation(
            sz[:, :].rearrange("p (t f) -> p t f", t=TT)[:, 2 * half:2 * half + 2, j * UC:(j + 1) * UC],
            k.ps[:, bank, :].rearrange("p (t f) -> p t f", t=2), ACT.Silu), tm=(2 * half, 2 * half + 2, 0, UC, UC))

    def copy(dst, c, scale=1.0):
        return Job("act", lambda act, bank: act.activation(dst, k.ps[:, bank, :], ACT.Copy, scale=scale), c=c)

    def k_out(act, bank):
        act.activation(kd[0][0:HD, :], k.ps[0:HD, bank, :], ACT.Copy)
        return act.activation(kd[1][HD:P, :], k.ps[HD:P, bank, :], ACT.Copy)

    def wi_out(act, bank):
        return act.activation(wi.rearrange("p (t h) -> p t h", h=IH),
                              k.ps[:, bank, 0:8 * TT].rearrange("p (t f) -> p t f", f=8)[:, :, 0:IH],
                              ACT.Copy, scale=IH ** -0.5 * HD ** -0.5)
    for j in range(4):
        z_at = plain(Z2 + j * UC, UC, [silu_z(j, 0), silu_z(j, 1)])
    for j in range(2):
        plain(Q2 + j * UC, UC, [copy(q[:, t * T:(t + 1) * T], t % 2, -HD ** -0.5) for t in (2 * j, 2 * j + 1)])
    plain(K2, UC, [Job("act", k_out, c=0), Job("act", lambda act, bank: act.activation(
        v[:, :], k.ps[:, bank, :], ACT.Copy), tm=(0, TT, P, P, P))])
    plain(QI2, UC, [copy(qi[:, t * T:(t + 1) * T], t) for t in range(2)])
    keys_at = plain(KI2, P, [Job("act", lambda act, bank: act.activation(
        ki[0:HD, :], k.ps[0:HD, bank, :], ACT.Copy), c=0), Job("act", wi_out, tm=(0, TT, HD, IH, 8))])

    conv = add(Conv, "conv", xbc, c, 12, CW, CB, prev=side.prev)
    at = conv.beside(side, 0, BESIDE2["conv"])
    dt = add(Softplus, "dt", None, s["dt"], 64, lambda dve, x2: dve.tensor_copy(x2, s["dt_raw"]))
    at = dt.beside(side, at, BESIDE2["dt"])
    prep = add(SsdPrep, "prep", c, xs, bt, cb, rows, s)
    at = prep.beside(side, at, BESIDE2["prep"])
    assert at <= z_at
    add(Rest, "to_ssd", side, z_at)
    ssd = add(Ssd, "ssd", c, xs, bt, cb, rows, s, sz, o_scr)
    at = ssd.beside(side, z_at, BESIDE2["ssd"])
    assert at <= keys_at
    ssd_out = add(SsdOut, "ssd_out", sz, SN, *ys)
    add(Rest, "to_select", side, keys_at)

    def tiles(x):
        return lambda i: x[:, i * T:(i + 1) * T]

    def branch(b, w, kt, y, need):
        for half in range(2):
            gate(b, half)
            at = up(b, w, kt, y, half, need)
        return at

    def gate(b, half):
        side.gate(lambda c: weight(w_in, l, 0, D, G2 + b * D + c, UC), half, free=ssd_out.ends)

    def up(b, w, kt, y, half, need):
        return side.up(lambda c, n: weight(A[w], l, 0, kt * P, c, n), kt, (tiles(y[0]), tiles(y[1])), half, b > 0,
                       need=need.ends if half == 0 else (), free=ssd_out.ends)
    ssd_at = branch(0, "w_up_ssd_2", KD, ys, ssd_out)
    u3 = u[:, :].rearrange("p (t w) -> p t w", w=T + pad)
    for j in range(2):
        u_at = plain(U2 + j * UC, UC, [copy(u3[:, t, pad:], t % 2) for t in (2 * j, 2 * j + 1)])

    add(Dup, "dup", [(kd[0][HD:P, :], kd[0][0:HD, :]), (kd[1][0:HD, :], kd[1][HD:P, :]),
                     (ki[HD:P, :], ki[0:HD, :])])
    at = keys_at + BESIDE2["dup"]
    add(Rest, "beside_dup", side, at)
    sel = add(Select, "select", qi, ki, wi, r, sc, m8)
    at = sel.beside(side, at, BESIDE2["select"])
    assert at <= ssd_at
    add(Rest, "to_att", side, ssd_at)
    add(Fill, "fill_u", [(u3[:, :, 0:pad], 0.0)])
    att = add(Attention, "att", lambda h: q[h % 2 * HD:(h % 2 + 1) * HD, h // 2 * T:(h // 2 + 1) * T],
              lambda h: kd[h // 4][h % 2 * HD:(h % 2 + 1) * HD, :],
              lambda b, h: v[:, b * P + h // 4 * HD:b * P + (h // 4 + 1) * HD],
              lambda i: sel.score(i) if i else k.const(C_QK), o_scr, o_scr + 11 * T, yahi, yalo)
    at = att.beside(side, ssd_at, BESIDE2["att"])
    branch(1, "w_up_attn_2", 4, (yahi, yalo), att)
    add(Rest, "to_pool", side, u_at)
    add(Fill, "fill_windows", [(ab[0][:, 0:pad], 0.0), (ab[1][:, 0:pad], 0.0)])
    pool = add(PoolMix, "pool", u, *ab, pooled, A["pool_w_2"][0].rearrange("g c d -> c g d"), pw, PS, *yp)
    at = pool.beside(side, max(at, u_at), BESIDE2["pool"])
    branch(2, "w_up_pool_2", 4, yp, pool)
    add(Rest, "branches", side)
    mix = [k.at(f"s_mixed_{p}", 4096 + i * 4096, 4096, F32R) for i, p in enumerate(("hi", "lo"))]
    split = add(Split, "split_mixed", merged, *mix, 8, lambda t: side.read(side.final[t]))
    proj = add(OutProj, "out", lambda c, n: weight(A["w_out_2"], l, 0, D, c, n), split, tiles(mix[0]), tiles(mix[1]))
    proj.stats = add(Stats, "stats2", proj.tile, emitted=True)
    norm = add(Norm, "norm2", N2)
    f = [k.at(f"s_ff_{p}", i * 11264, 11264, F32R) for i, p in enumerate(("hi", "lo"))]
    scr = [k.at(f"s_ff_{p}", 22528 + i * 1024, 1024) for i, p in enumerate(("silu", "product"))]
    up = add(Glu, "up", norm, lambda j, i: weight(A["w_ffn_in_2"], l, 0, D, i * UC + j * FF2, UC), FF2 // UC, *f, scr)
    down = add(Down, "down", up, lambda j, i: weight(A["w_ffn_out_2"], l, i * 256 + j * 256, 256, 0, D), 11, *f,
               last=True)
    down.stats = add(Stats, "stats_last", down.tile, emitted=True)
    norm = add(Norm, "norm_last", FIN2, final=True)
    add(Store, "store", norm, out)
    return st


def program(nc, A, table, out):
    with ExitStack() as ctx:
        k = Kern(nc, ctx)
        k.xT = k.keep("xT", KD * T)
        k.hhi, k.hlo = k.keep("h_hi", KD * T, F32R), k.keep("h_lo", KD * T, F32R)
        k.wraw = k.keep("w_raw", 2 * SLOT)
        k.whi, k.wlo = k.keep("w_hi", 2 * SLOT, F32R), k.keep("w_lo", 2 * SLOT, F32R)
        k.cst = k.keep("constants", C_END)
        k.cos, k.sin = k.keep("cos", T), k.keep("sin", T)
        k.pcol = k.keep("param_cols", 104)
        k.stat = k.keep("stat", 96)
        k.acol = k.keep("gate_cols", 32)
        k.hbias = k.keep("half_bias", 24)
        k.small = k.keep("small", 48)
        k.eps = k.keep("eps", 8)
        k.arena = k.top
        k.arena_words = (nc.sbuf_usable_end() - k.arena) // 4 if callable(nc.sbuf_usable_end) else (nc.sbuf_usable_end - k.arena) // 4
        k.rstd = k.at("rstd", Stats.AT + Stats.SLOTS * T, T)
        k.ps = ctx.enter_context(nc.psum_tensor("ps", [P, 8, 512], F32))
        setup = Setup(k, "setup", [], A["x"], A["positions"], table)
        emit(k, [setup, Stats(k, "stats_first", [setup])])
        with ExitStack() as k.ctx:
            k.sems = []
            with nc.Fori(0, DEPTH) as l:
                emit(k, first_layer(k, l, A), lead=True)
                ids = [s.num for s in k.sems]
                assert max(ids) - min(ids) + 1 == len(ids)
                nc.sync.sem_clear(range(min(ids), max(ids) + 1))
                nc.all_engine_barrier()
        with ExitStack() as k.ctx:
            emit(k, second_layer(k, A, out), lead=True)


_INS = ['x', 'positions', 'norm_mix_w', 'w_in', 'b_in', 'conv_w', 'conv_b', 'mlstm_norm_w', 'w_proj_att',
        'w_proj_mlstm', 'w_out', 'norm_mlp_w', 'w_ff1', 'w_ff2', 'final_norm_w', 'norm1_w_2', 'w_in_2',
        'conv_w_2', 'conv_b_2', 'dt_bias_2', 'a_log_2', 'd_skip_2', 'ssd_norm_w_2', 'pool_w_2',
        'pool_scale_2', 'w_up_ssd_2', 'w_up_attn_2', 'w_up_pool_2', 'w_out_2', 'norm2_w_2',
        'w_ffn_in_2', 'w_ffn_out_2', 'final_norm_w_2']


def kernel(**inputs):
    import concourse.bacc as _bacc
    from concourse.bass_utils import run_bass_kernel_spmd as _run

    nc = _bacc.Bacc("TRN2", target_bir_lowering=False, num_devices=1)
    arrays, args = {}, {}
    for name in _INS:
        a = np.ascontiguousarray(inputs[name])
        arrays[f"in_{name}"] = a
        args[name] = nc.dram_tensor(f"in_{name}", a.shape, mybir.dt.from_np(a.dtype), kind="ExternalInput").ap()
    arrays["constants_table"] = constants()
    table = nc.dram_tensor("constants_table", (P, C_END), F32, kind="ExternalInput").ap()
    out = nc.dram_tensor("out_x", (1, T, D), F32, kind="ExternalOutput").ap()
    program(nc, args, table, out)
    r = _run(nc, [arrays], core_ids=[0])
    return r.results[0]["out_x"]
```

```python
import math
from contextlib import ExitStack

import numpy as np

import concourse.bass as bass
from concourse import mybir

F32 = mybir.dt.float32
F32R = mybir.dt.float32r
I32 = mybir.dt.int32
ACT = mybir.ActivationFunctionType
ALU = mybir.AluOpType
AX = mybir.AxisListType

P = 128
T = 512
TT = T // P
D = 1024
KD = D // P
DEPTH = 2
EPS = 1e-6
BIG = 1e30
SLOT = 2048
UC = SLOT // KD
UT = UC // P

HEADS, HD = 8, 64
MH, MD = 4, 128
CONV = 4
DFF = 4 * D
AQ, AK, AV, MQ, MK, MV, MO = (512 * i for i in range(7))
MI = 3584
GA = MI + 2 * MH
GB = GA + D
NPAT = 3
PATTERNS = ((128, 1), (512, 4), (2048, 16))
ROPE_THETA, ROPE_DIM = 500000.0, HD // 4

SH, SHD, SG = 16, 64, 2
SPG = SH // SG
XC = 1536
Z2, XBC2 = 0, D
DT2 = XBC2 + XC
Q2 = DT2 + SH
K2 = Q2 + 512
QI2 = K2 + 256
KI2 = QI2 + 256
IH = 4
U2 = KI2 + 64 + IH
G2 = U2 + 512
FF2 = 2816
TOPK = 128
TAKEN = -3e38
WINDOWS = (2, 4, 8, 16)

C_ID, C_ONE = 0, P
C_ROT, C_QK, C_ST, C_KEEP, C_PAT = (P + 8 + P * i for i in range(5))
C_INV = C_PAT + TT * P
C_MSK, C_UNM = C_INV + 1, C_INV + 2
C_CNT = C_INV + 3
C_END = C_CNT + len(WINDOWS) * 16


def up8(n):
    return (n + 7) // 8 * 8


def constants():
    c = np.zeros((P, C_END), np.float32)
    i = np.arange(P)
    c[:, C_ID:C_ID + P] = np.eye(P)
    c[:, C_ONE:C_ONE + 8] = 1.0
    half = ROPE_DIM // 2
    for p in range(P):
        d = p % HD
        if d < half:
            c[p + half, C_ROT + p] = -1.0
        elif d < ROPE_DIM:
            c[p - half, C_ROT + p] = 1.0
    c[:, C_QK:C_QK + P] = np.where(i[None, :] > i[:, None], BIG, 0.0)
    c[:, C_ST:C_ST + P] = np.where(i[:, None] > i[None, :], BIG, 0.0)
    c[:, C_KEEP:C_KEEP + P] = i[:, None] <= i[None, :]
    for b in range(TT):
        dist = i[:, None] - i[None, :] + (TT - 1 - b) * P
        n = sum(((dist >= 0) & (dist % dil == 0) & (dist <= win)).astype(int) for win, dil in PATTERNS)
        c[:, C_PAT + b * P:C_PAT + (b + 1) * P] = np.where(n > 0, -np.log(np.maximum(n, 1)), BIG)
    d = i % HD
    inv = np.float32(ROPE_THETA) ** (-np.arange(0, ROPE_DIM, 2, dtype=np.float32) / np.float32(ROPE_DIM))
    c[:, C_INV] = np.where(d < ROPE_DIM, inv[d % half], 0.0)
    c[:, C_MSK] = d < ROPE_DIM
    c[:, C_UNM] = d >= ROPE_DIM
    for g, w in enumerate(WINDOWS):
        c[:, C_CNT + 16 * g:C_CNT + 16 * (g + 1)] = 1.0 / np.minimum(np.arange(1, 17), w)
    return c


class Stage:

    side, base, budget = None, 0, 0

    def __init__(self, k, name, prev):
        self.k, self.name, self.prev, self.ends, self.s = k, name, prev, [], {}

    def beside(self, side, base, budget):
        self.side, self.base, self.budget = side, base, budget
        return base + budget

    def share(self, n, steps):
        return self.base + self.budget * n // steps

    def side_pe(self, pe, n, steps):
        if self.side:
            self.side.emit_pe(pe, self.share(n + 1, steps))

    def side_out(self, who, eng, n, steps):
        if self.side:
            self.side.emit_out(who, eng, self.share(n, steps))

    def sem(self, name):
        if name not in self.s:
            self.s[name] = self.k.new_sem(f"{self.name}_{name}")
        return self.s[name]

    def join(self, eng):
        for p in self.prev:
            for s, v in p.ends:
                eng.wait_ge(s, v)

    def sp(self, e): pass
    def act(self, e): pass
    def dve(self, e): pass
    def pe(self, e): pass


class Kern:
    def __init__(self, nc, ctx):
        self.nc, self.ctx, self.sems = nc, ctx, []
        self.top = (nc.sbuf_base + 31) // 32 * 32

    def new_sem(self, name):
        s = self.ctx.enter_context(self.nc.semaphore(name))
        self.sems.append(s)
        return s

    def at(self, name, off, cols, dt=F32, parts=P):
        assert off + cols <= self.arena_words, (name, off, cols)
        return self.nc.alloc_sbuf_tensor_at(name, [parts, cols], dt, offset=self.arena + 4 * off)

    def keep(self, name, cols, dt=F32):
        t = self.nc.alloc_sbuf_tensor_at(name, [P, cols], dt, offset=self.top)
        self.top += 4 * ((cols + 7) // 8 * 8)
        return t

    def slot(self, u):
        return u % 2

    def const(self, c):
        return self.cst[:, c:c + P]

    def col(self, c):
        return self.pcol[:, c:c + 1]

    def pick(self, h, n):
        return self.cst[0:n, C_ID + h:C_ID + h + 1].broadcast_to([n, P])

    def ones(self, n, w):
        return self.cst[0:n, C_ONE:C_ONE + 1].broadcast_to([n, w])

    def hh(self, i):
        return self.hhi[:, i * T:(i + 1) * T]

    def hl(self, i):
        return self.hlo[:, i * T:(i + 1) * T]

    def stream_sems(self, tag, ready=0):
        self.ready = ready
        self.landed = [self.new_sem(f"{tag}_unit_landed_{i}") for i in range(2)]
        self.hi_done = self.new_sem(f"{tag}_unit_hi_done")
        self.split = self.new_sem(f"{tag}_unit_split")
        self.unit_used = self.new_sem(f"{tag}_unit_used")
        self.units = 0


def wait_split(k, pe, u0, du=0):
    if not (isinstance(du, int) and u0 + du < k.ready):
        pe.wait_ge(k.split, du + (u0 + 1 - k.ready))


def units(k, n):
    k.units += n
    return k.units - n



def load_unit(k, sp, u0, du, src, cols):
    slot = k.slot(u0)
    if isinstance(du, int) and u0 + du < k.ready:
        return
    if not (isinstance(du, int) and u0 + du < k.ready + 2):
        sp.wait_ge(k.split, du + (u0 - 1 - k.ready))
    n = src.shape[1]
    dst = k.wraw[:, slot * SLOT:slot * SLOT + n * cols].rearrange("p (k n) -> p k n", n=cols)
    sp.dma_start(dst, src).then_inc(k.landed[slot], 16)


def hi_unit(k, act, u0, du):
    slot = k.slot(u0)
    act.wait_ge(k.landed[slot], du * 8 + 16 * (u0 // 2 + 1 - k.ready // 2))
    if not (isinstance(du, int) and u0 + du < 2):
        act.wait_ge(k.unit_used, du + (u0 - 1))
    act.activation(k.whi[:, slot * SLOT:(slot + 1) * SLOT], k.wraw[:, slot * SLOT:(slot + 1) * SLOT],
                   ACT.Copy).then_inc(k.hi_done, 1)


def lo_units(k, pool, n):
    def one(slot, value):
        a = slot * SLOT
        pool.wait_ge(k.hi_done, value)
        pool.tensor_tensor(k.wlo[:, a:a + SLOT], k.wraw[:, a:a + SLOT], k.whi[:, a:a + SLOT],
                           ALU.subtract).then_inc(k.split, 1)
    with pool.Fori(0, n // 2) as i:
        one(0, i * 2 + 1)
        one(1, i * 2 + 2)
    if n % 2:
        one(0, n)


def fm_unit(k, pe, u0, kt, cols, xh, xl, outs, ready=None, done=None):
    a = k.slot(u0) * SLOT
    if ready:
        for i in range(kt):
            w = [slice(a + i * cols + c * P, a + i * cols + (c + 1) * P) for c in range(len(outs))]
            pe.wait_ge(ready.sem("hi"), i + 1)
            for c, out in enumerate(outs):
                pe.matmul(out, k.whi[:, w[c]], xh(i), start=i == 0, stop=False, skip_group_check=True)
                pe.matmul(out, k.wlo[:, w[c]], xh(i), start=False, stop=False, skip_group_check=True)
            pe.wait_ge(ready.sem("lo"), i + 1)
            for c, out in enumerate(outs):
                mm = pe.matmul(out, k.whi[:, w[c]], xl(i), start=False, stop=i == kt - 1, skip_group_check=True)
                if done and i == kt - 1 and c < len(outs) - 1:
                    mm.then_inc(done, 1)
        return mm
    for c, out in enumerate(outs):
        for i in range(kt):
            w = slice(a + i * cols + c * P, a + i * cols + (c + 1) * P)
            pe.matmul(out, k.whi[:, w], xh(i), start=i == 0, stop=False)
            pe.matmul(out, k.whi[:, w], xl(i), start=False, stop=False)
            mm = pe.matmul(out, k.wlo[:, w], xh(i), start=False, stop=i == kt - 1)
        if done and c < len(outs) - 1:
            mm.then_inc(done, 1)
    return mm


def tm_unit(k, pe, u0, kt, cols, off, width, xh, xl, out):
    a = k.slot(u0) * SLOT
    for t in range(TT):
        tok = slice(t * P, (t + 1) * P)
        for i in range(kt):
            w = slice(a + i * cols + off, a + i * cols + off + width)
            pe.matmul(out(t), xh(i)[:, tok], k.whi[:, w], start=i == 0, stop=False)
            pe.matmul(out(t), xl(i)[:, tok], k.whi[:, w], start=False, stop=False)
            mm = pe.matmul(out(t), xh(i)[:, tok], k.wlo[:, w], start=False, stop=i == kt - 1)
    return mm



class Stats(Stage):

    SLOTS = 3
    AT = 22528
    RSTD = 7

    def __init__(self, k, name, prev, tile=None, emitted=False, bank=0):
        super().__init__(k, name, prev)
        self.tile, self.emitted, self.bank = tile, emitted, bank
        self.sq = k.at(f"{name}_squares", self.AT, self.SLOTS * T)
        self.diag = self.sq[:, 0:T]
        self.ends = [(self.sem("rstd"), 1)]
        self.ahead = None
        self.urgent = False

    def slot(self, t):
        return self.sq[:, t % self.SLOTS * T:(t % self.SLOTS + 1) * T]

    def square(self, act, t):
        k = self.k
        if t == 0:
            act.activation(k.eps[:, 1:2], k.eps[:, 0:1], ACT.Sqrt)
        if self.tile:
            s, v = self.tile(t)
            act.wait_ge(s, v)
        if t >= self.SLOTS:
            act.wait_ge(self.sem("summed"), t - self.SLOTS + 1)
        act.activation(self.slot(t), k.xT[:, t * T:(t + 1) * T], ACT.Square).then_inc(self.sem("squared"), 1)

    def sum(self, pe, t):
        k = self.k
        pe.wait_ge(self.sem("squared"), t + 1)
        for i in range(TT):
            mm = pe.matmul(k.ps[:, self.bank, i:i + 1], self.slot(t)[:, i * P:(i + 1) * P], k.ones(P, 1),
                           start=t == i == 0, stop=t == KD - 1 and i == TT - 1, skip_group_check=True)
        mm.then_inc(self.sem("summed"), 1)

    def act(self, act):
        k = self.k
        if not self.emitted:
            self.join(act)
            for t in range(KD):
                self.square(act, t)
        if self.urgent:
            hi_unit(k, act, self.ahead, 0)
        act.wait_ge(self.sem("summed"), KD)
        act.activation(k.root[:, 0:TT], k.ps[:, self.bank, 0:TT], ACT.Sqrt, bias=k.eps[:, 0:1],
                       scale=1.0 / D).then_inc(self.sem("root"), 1)
        if self.ahead is not None and not self.urgent:
            hi_unit(k, act, self.ahead, 0)

    def pe(self, pe):
        k = self.k
        if not self.emitted:
            self.join(pe)
            for t in range(KD):
                self.sum(pe, t)
        self.join(pe)
        pe.wait_ge(self.sem("diagonals"), 2)
        pe.matmul(k.ps[:, self.RSTD, :], k.ones(P, P), self.diag, start=True, stop=True)\
          .then_inc(self.sem("rstd"), 1)

    def dve(self, dve):
        k = self.k
        dve.wait_ge(self.sem("root"), 1)
        dve.reciprocal(k.root[:, TT:2 * TT], k.root[:, 0:TT]).then_inc(self.sem("diagonals"), 1)
        dve.wait_ge(self.sem("diagonals"), 1)
        dve.wait_ge(self.sem("summed"), KD)
        dve.tensor_tensor(self.diag.rearrange("p (t f) -> p t f", f=P),
                          k.const(C_ID).unsqueeze(1).broadcast_to([P, TT, P]),
                          k.root[:, TT:2 * TT].unsqueeze(2).broadcast_to([P, TT, P]), ALU.mult)\
           .then_inc(self.sem("diagonals"), 1)


class Norm(Stage):

    def __init__(self, k, name, prev, wcol, final=False):
        super().__init__(k, name, prev)
        self.wcol, self.final = wcol, final
        self.h = k.xT if final else k.at(f"{name}_h", KD * T, KD * T)
        self.ready = self.sem("scaled" if final else "lo")
        self.ends = [(self.ready, KD)]

    def act(self, act):
        k = self.k
        if not self.final:
            self.join(act)
            for t in range(KD):
                act.wait_ge(self.sem("scaled"), t + 1)
                act.activation(k.hhi[:, t * T:(t + 1) * T], self.h[:, t * T:(t + 1) * T],
                               ACT.Copy).then_inc(self.sem("hi"), 1)

    def dve(self, dve):
        k = self.k
        self.join(dve)
        for t in range(KD + 1):
            if t < KD:
                dve.scalar_tensor_tensor(self.h[:, t * T:(t + 1) * T], k.xT[:, t * T:(t + 1) * T],
                                         k.col(self.wcol + t), k.ps[:, Stats.RSTD, :], ALU.mult,
                                         ALU.mult).then_inc(self.sem("scaled"), 1)
            if t and not self.final:
                dve.wait_ge(self.sem("scaled"), t)
                dve.wait_ge(self.sem("hi"), t)
                dve.tensor_tensor(k.hlo[:, (t - 1) * T:t * T], self.h[:, (t - 1) * T:t * T],
                                  k.hhi[:, (t - 1) * T:t * T], ALU.subtract).then_inc(self.sem("lo"), 1)


class Seg:

    def __init__(self, kind, n, src, cols, evac, eng="act", loop=False, off=0, width=None, tiles=UT):
        self.kind, self.n, self.src, self.cols, self.evac = kind, n, src, cols, evac
        self.eng, self.loop, self.off, self.width, self.tiles = eng, loop, off, width or cols, tiles


class Project(Stage):

    def __init__(self, k, name, prev, norm, segs):
        super().__init__(k, name, prev)
        self.norm = norm
        self.segs = segs
        self.u0 = k.units
        for s in segs:
            s.u0 = units(k, s.n)
        n = k.units - self.u0
        self.out = [self.sem("out_even"), self.sem("out_odd")]
        self.ends = [(self.out[0], (n + 1) // 2), (self.out[1], n // 2)]

    def each(self, eng, body, which=lambda s: True, peel=lambda s: False):
        for s in filter(which, self.segs):
            if s.loop:
                first = 1 if peel(s) else 0
                for j in range(2 * first):
                    body(s, j, 0)
                with eng.Fori(first, s.n // 2) as i:
                    for j in range(2):
                        body(s, j, i)
            else:
                for j in range(s.n):
                    body(s, j, 0)

    def load(self, s, j, i):
        load_unit(self.k, self.engine, s.u0 + j, i * 2, s.src(j, i), s.cols)

    def sp(self, sp):
        self.engine = sp
        if self.k.ready:
            s, self.segs = self.segs[0], self.segs[1:]
            for j in range(s.n):
                load_unit(self.k, sp, s.u0 + j % 2, j // 2 * 2, s.src(j % 2, j // 2), s.cols)
            self.each(sp, self.load)
            self.segs = [s] + self.segs
        else:
            self.each(sp, self.load, peel=lambda s: s.u0 < 2)

    def pe(self, pe):
        k = self.k

        def unit(s, j, i):
            local = s.u0 + j - self.u0
            bank = 2 * (local % 2)
            wait_split(k, pe, s.u0 + j, i * 2)
            if local >= 2 or not isinstance(i, int):
                pe.wait_ge(self.out[local % 2], i + local // 2)
            if s.kind == "fm":
                mm = fm_unit(k, pe, s.u0 + j, KD, s.cols, k.hh, k.hl,
                             [k.ps[:, bank + c, :] for c in range(s.tiles)],
                             self.norm if local == 0 and isinstance(i, int) else None)
                if s.off:
                    mm = tm_unit(k, pe, s.u0 + j, KD, s.cols, s.off, s.width, k.hh, k.hl,
                                 lambda t: k.ps[:, bank + 1, t * P:t * P + s.width])
            else:
                mm = tm_unit(k, pe, s.u0 + j, KD, s.cols, 0, s.cols, k.hh, k.hl,
                             lambda t: k.ps[:, bank + t // 2, t % 2 * UC:t % 2 * UC + s.cols])
            mm.then_inc(k.unit_used, 1)
        self.each(pe, unit, peel=lambda s: s.u0 - self.u0 < 2)

    def evac(self, eng, who):
        k = self.k

        def unit(s, j, i):
            local = s.u0 + j - self.u0
            bank = 2 * (local % 2)
            if s.eng == who:
                eng.wait_ge(k.unit_used, i * 2 + (s.u0 + j + 1))
                s.evac(eng, j, i, bank).then_inc(self.out[local % 2], 1)
            if who == "act":
                hi_unit(k, eng, s.u0 + j + 2, i * 2)
        self.each(eng, unit, lambda s: who == "act" or s.eng == who)

    def act(self, act):
        self.join(act)
        self.evac(act, "act")

    def dve(self, dve):
        self.join(dve)
        self.evac(dve, "dve")


class Job:

    def __init__(self, who, evac, c=None, tm=None, need=(), rows=P):
        self.who, self.evac, self.c, self.tm, self.need, self.rows = who, evac, c, tm, need, rows


class Jobs(Stage):

    PIECE = 6

    def __init__(self, k, name, prev):
        super().__init__(k, name, prev)
        self.units, self.jobs, self.pieces = [], [], []
        self.at = {"pe": 0, "act": 0, "dve": 0}
        self.joined = set()
        self.early = 0

    def unit(self, src, kt, cols, xh, xl, jobs):
        u = units(self.k, 1)
        self.units.append((u, src, cols))
        for job in jobs:
            job.n, job.u, job.kt, job.cols, job.xh, job.xl = len(self.jobs), u, kt, cols, xh, xl
            job.last = job is jobs[-1]
            if not job.last:
                self.early += 1
            job.early = self.early
            self.jobs.append(job)
            if job.c is not None:
                steps = [(job, None, i) for i in range(kt)]
                per = self.PIECE // 3
            else:
                steps = [(job, t, i) for t in range(job.tm[0], job.tm[1]) for i in range(kt)]
                per = self.PIECE * 2 // 3
            for a in range(0, len(steps), per):
                self.pieces.append(steps[a:a + per])
            job.end = len(self.pieces)
        return len(self.pieces)

    def ends_at(self, upto=None):
        n = sum(1 for job in self.jobs if upto is None or job.end <= upto)
        return [(self.bank(b), (n + 3 - b) // 4) for b in range(min(4, n))]

    def read(self, job):
        return self.bank(job.n % 4), job.n // 4 + 1

    def bank(self, b):
        return self.sem(f"bank{b}")

    def sp(self, sp):
        for u, src, cols in self.units:
            load_unit(self.k, sp, u, 0, src, cols)

    def start(self, who, eng):
        if who not in self.joined:
            self.joined.add(who)
            self.join(eng)

    def done(self, eng, job):
        if job.last:
            eng.wait_ge(self.k.unit_used, job.u + 1)
        else:
            eng.wait_ge(self.sem("job"), job.early)

    def emit_pe(self, pe, upto):
        k = self.k
        while self.at["pe"] < min(upto, len(self.pieces)):
            self.start("pe", pe)
            piece = self.pieces[self.at["pe"]]
            self.at["pe"] += 1
            for job, t, i in piece:
                b, a = job.n % 4, k.slot(job.u) * SLOT + i * job.cols
                t0 = 0 if t is None else job.tm[0]
                first = i == 0 and t in (None, t0)
                if first:
                    wait_split(k, pe, job.u)
                    if job.n >= 4:
                        pe.wait_ge(self.bank(b), job.n // 4)
                    for s, v in job.need:
                        pe.wait_ge(s, v)
                if t is None:
                    w = slice(a + job.c * P, a + job.c * P + job.rows)
                    out, ops = k.ps[0:job.rows, b, :], [(k.whi[:, w], job.xh(i)), (k.whi[:, w], job.xl(i)),
                                               (k.wlo[:, w], job.xh(i))]
                    end = i == job.kt - 1
                    stop = end
                else:
                    _, t1, off, width, pitch = job.tm
                    w = slice(a + off, a + off + width)
                    tok = slice(t * P, (t + 1) * P)
                    out = k.ps[:, b, (t - t0) * pitch:(t - t0) * pitch + width]
                    ops = [(job.xh(i)[:, tok], k.whi[:, w]), (job.xl(i)[:, tok], k.whi[:, w]),
                           (job.xh(i)[:, tok], k.wlo[:, w])]
                    stop = i == job.kt - 1
                    end = stop and t == t1 - 1
                for n, (lhs, rhs) in enumerate(ops):
                    mm = pe.matmul(out, lhs, rhs, start=i == 0 and n == 0, stop=stop and n == 2)
                if end:
                    mm.then_inc(k.unit_used if job.last else self.sem("job"), 1)

    def emit_out(self, who, eng, upto):
        while self.at[who] < len(self.jobs) and self.jobs[self.at[who]].end <= upto:
            job = self.jobs[self.at[who]]
            self.at[who] += 1
            if job.who == who:
                self.start(who, eng)
                self.done(eng, job)
                job.evac(eng, job.n % 4).then_inc(self.bank(job.n % 4), 1)
            if who == "act" and job.last and job.u + 2 < self.k.units:
                hi_unit(self.k, eng, job.u + 2, 0)


class Rest(Stage):

    def __init__(self, k, name, prev, jobs, upto=None):
        super().__init__(k, name, prev)
        self.jobs, self.upto = jobs, upto or len(jobs.pieces)
        self.ends = [e for p in prev for e in p.ends] + jobs.ends_at(upto)

    def pe(self, pe):
        self.jobs.emit_pe(pe, self.upto)

    def act(self, act):
        self.jobs.emit_out("act", act, self.upto)

    def dve(self, dve):
        self.jobs.emit_out("dve", dve, self.upto)


class Rope(Stage):

    def __init__(self, k, name, prev, qk, t1, t2):
        super().__init__(k, name, prev)
        self.qk, self.t1, self.t2 = qk, t1, t2
        self.ends = [(self.sem("turned"), 8)]

    def pe(self, pe):
        k = self.k
        self.join(pe)
        for t in range(8):
            if t >= 4:
                pe.wait_ge(self.sem("sin"), t - 3)
            pe.matmul(k.ps[:, 4 + t % 4, :], k.const(C_ROT), self.qk[:, t * T:(t + 1) * T],
                      start=True, stop=True).then_inc(self.sem("swapped"), 1)
            self.side_pe(pe, t, 8)

    def dve(self, dve):
        k = self.k
        self.join(dve)
        for t in range(8):
            self.side_out("dve", dve, t, 8)
            scale = -HD ** -0.5 if t < 4 else 1.0
            a, b = (x[:, t % 2 * T:(t % 2 + 1) * T] for x in (self.t1, self.t2))
            tile = self.qk[:, t * T:(t + 1) * T]
            dve.scalar_tensor_tensor(a, tile, scale, k.cos[:, :], ALU.mult, ALU.mult)\
               .then_inc(self.sem("cos"), 1)
            dve.wait_ge(self.sem("swapped"), t + 1)
            dve.scalar_tensor_tensor(b, k.ps[:, 4 + t % 4, :], scale, k.sin[:, :], ALU.mult, ALU.mult)\
               .then_inc(self.sem("sin"), 1)
            dve.wait_ge(self.sem("cos"), t + 1)
            dve.wait_ge(self.sem("sin"), t + 1)
            dve.tensor_tensor(tile, a, b, ALU.add).then_inc(self.sem("turned"), 1)

    def act(self, act):
        self.side_out("act", act, 7, 8)


class Attention(Stage):


    def __init__(self, k, name, prev, q, kk, v, mask, scr, ns, yhi, ylo):
        super().__init__(k, name, prev)
        self.q, self.kk, self.v, self.mask, self.yhi, self.ylo = q, kk, v, mask, yhi, ylo
        self.ns = k.at(f"{name}_negscores", ns, 2 * T)
        self.p = k.at(f"{name}_probs", scr, 4 * T)
        self.pt = k.at(f"{name}_probsT", scr + 4 * T, 2 * TT * T)
        self.N = HEADS * TT
        self.stat = k.stat
        self.ends = [(self.sem("lo"), HEADS)]

    WEIGHTS = (1, 1, 1, 1)
    TAIL = 2

    def share(self, n, steps):
        w = [self.WEIGHTS[i % TT] for i in range(self.N)] + [self.TAIL] * (steps - self.N)
        return self.base + self.budget * sum(w[:n]) // sum(w)

    def pe(self, pe):
        k = self.k
        self.join(pe)
        for n in range(self.N + 4):
            if n < self.N:
                h, i = divmod(n, TT)
                if n >= 2:
                    pe.wait_ge(self.sem("masked"), n - 1)
                pe.matmul(k.ps[:, 4 + n % 2, 0:(i + 1) * P], self.q(h)[:, i * P:(i + 1) * P],
                          self.kk(h)[:, 0:(i + 1) * P], start=True, stop=True)\
                  .then_inc(self.sem("scores"), 1)
            m = n - 3
            if 0 <= m < self.N:
                i = m % TT
                pe.wait_ge(self.sem("probs"), m + 1)
                if m >= 1:
                    pe.wait_ge(self.sem("copied"), m)
                for b in range(i + 1):
                    tr = pe.transpose(k.ps[:, 6, b * P:(b + 1) * P],
                                      self.p[:, m % 4 * T + b * P:m % 4 * T + (b + 1) * P], k.const(C_ID))
                tr.then_inc(self.sem("turned"), 1)
            m = n - 4
            if m >= 0 and m % TT == TT - 1:
                h = m // TT
                pe.wait_ge(self.sem("copied"), m + 1)
                if h >= 1:
                    pe.wait_ge(self.sem("lo"), h)
                r = slice(h % 2 * HD, h % 2 * HD + HD)
                for b in range(TT):
                    mm = pe.matmul(k.ps[r, 7, b * P:T], self.v(b, h),
                                   self.pt[:, (h % 2 * TT + b) * T + b * P:(h % 2 * TT + b + 1) * T],
                                   start=b == 0, stop=b == TT - 1, skip_group_check=True)
                mm.then_inc(self.sem("values"), 1)
            self.side_pe(pe, n, self.N + 4)

    def dve(self, dve):
        k = self.k
        self.join(dve)
        for n in range(self.N + 4):
            self.side_out("dve", dve, n, self.N + 4)
            if n < self.N:
                i = n % TT
                w = (i + 1) * P
                dve.wait_ge(self.sem("scores"), n + 1)
                if n >= 2:
                    dve.wait_ge(self.sem("exp"), n - 1)
                dve.tensor_tensor_reduce(self.ns[:, n % 2 * T:n % 2 * T + w], k.ps[:, 4 + n % 2, 0:w],
                                         self.mask(i), 1.0, BIG, ALU.add, ALU.min,
                                         self.stat[:, n:n + 1]).then_inc(self.sem("masked"), 1)
            m = n - 1
            if 0 <= m < self.N:
                w = (m % TT + 1) * P
                dve.wait_ge(self.sem("exp"), m + 1)
                dve.reciprocal(self.stat[:, 64 + m:65 + m], self.stat[:, 32 + m:33 + m])\
                   .then_inc(self.sem("recip"), 1)
                dve.wait_ge(self.sem("recip"), m + 1)
                pr = self.p[:, m % 4 * T:m % 4 * T + w]
                dve.tensor_scalar(pr, pr, self.stat[:, 64 + m:65 + m], None, ALU.mult)\
                   .then_inc(self.sem("probs"), 1)
            m = n - 4
            if m >= 0 and m % TT == TT - 1:
                h = m // TT
                r = slice(h % 2 * HD, h % 2 * HD + HD)
                dve.wait_ge(self.sem("hi"), h + 1)
                dve.tensor_tensor(self.ylo[r, h // 2 * T:(h // 2 + 1) * T], k.ps[r, 7, :],
                                  self.yhi[r, h // 2 * T:(h // 2 + 1) * T], ALU.subtract)\
                   .then_inc(self.sem("lo"), 1)

    def act(self, act):
        k = self.k
        self.join(act)
        for n in range(self.N + 4):
            self.side_out("act", act, n, self.N + 4)
            if n < self.N:
                w = (n % TT + 1) * P
                act.wait_ge(self.sem("masked"), n + 1)
                if n >= 4:
                    act.wait_ge(self.sem("turned"), n - 3)
                act.activation(self.p[:, n % 4 * T:n % 4 * T + w], self.ns[:, n % 2 * T:n % 2 * T + w],
                               ACT.Exp, bias=self.stat[:, n:n + 1], scale=-1.0,
                               accum_out=self.stat[:, 32 + n:33 + n]).then_inc(self.sem("exp"), 1)
            m = n - 3
            if 0 <= m < self.N:
                h, i = divmod(m, TT)
                act.wait_ge(self.sem("turned"), m + 1)
                if h >= 2 and i == 0:
                    act.wait_ge(self.sem("values"), h - 1)
                dst = self.pt[:, h % 2 * TT * T:(h % 2 + 1) * TT * T].rearrange("p (b q) -> p b q", b=TT)
                act.activation(dst[:, 0:i + 1, i * P:(i + 1) * P],
                               k.ps[:, 6, 0:(i + 1) * P].rearrange("p (b q) -> p b q", q=P),
                               ACT.Copy).then_inc(self.sem("copied"), 1)
            m = n - 4
            if m >= 0 and m % TT == TT - 1:
                h = m // TT
                r = slice(h % 2 * HD, h % 2 * HD + HD)
                act.wait_ge(self.sem("values"), h + 1)
                act.activation(self.yhi[r, h // 2 * T:(h // 2 + 1) * T], k.ps[r, 7, :],
                               ACT.Copy).then_inc(self.sem("hi"), 1)


class Conv(Stage):

    def __init__(self, k, name, prev, src, dst, tiles, wcol, bcol):
        super().__init__(k, name, prev)
        self.src, self.dst, self.tiles, self.wcol, self.bcol = src, dst, tiles, wcol, bcol
        self.ends = [(self.sem("silu"), tiles)]

    def tap(self, t, j):
        a = t * (T + CONV - 1) + j
        return self.src[:, a:a + T]

    def act(self, act):
        k = self.k
        self.join(act)
        for t in range(self.tiles):
            self.side_out("act", act, t, 2 * self.tiles)
            act.activation(self.dst[:, t * T:(t + 1) * T], self.tap(t, 0), ACT.Identity,
                           bias=k.col(self.bcol + t), scale=k.col(self.wcol + t))\
               .then_inc(self.sem("tap"), 1)
        for t in range(self.tiles):
            self.side_out("act", act, t + self.tiles, 2 * self.tiles)
            act.wait_ge(self.sem("taps"), t + 1)
            d = self.dst[:, t * T:(t + 1) * T]
            act.activation(d, d, ACT.Silu).then_inc(self.sem("silu"), 1)

    def dve(self, dve):
        k = self.k
        self.join(dve)
        for t0 in range(0, self.tiles, 4):
            for j in range(1, CONV):
                self.side_out("dve", dve, t0 // 4 * 3 + j - 1, self.tiles // 4 * 3)
                for t in range(t0, t0 + 4):
                    d = self.dst[:, t * T:(t + 1) * T]
                    if j == 1:
                        dve.wait_ge(self.sem("tap"), t + 1)
                    else:
                        dve.wait_ge(self.sem("part"), t0 // 4 * 8 + (j - 2) * 4 + t - t0 + 1)
                    ins = dve.scalar_tensor_tensor(d, self.tap(t, j), k.col(self.wcol + j * self.tiles + t),
                                                   d, ALU.mult, ALU.add)
                    ins.then_inc(self.sem("taps" if j == CONV - 1 else "part"), 1)


    def pe(self, pe):
        self.side_pe(pe, 0, 1)


class Softplus(Stage):

    def __init__(self, k, name, prev, x, out, w, pre):
        super().__init__(k, name, prev)
        self.x, self.out, self.w, self.pre = x, out, w, pre
        self.ends = [(self.sem("step"), 11)]

    def pe(self, pe):
        self.side_pe(pe, 0, 1)

    def act(self, act):
        k, w = self.k, self.w
        self.side_out("act", act, 0, 1)
        e, u, ln = (k.tmp[:, i * 64:i * 64 + w] for i in range(3))
        act.wait_ge(self.sem("step"), 2)
        act.activation(e, k.tmp[:, 192:192 + w], ACT.Exp).then_inc(self.sem("exp"), 1)
        act.wait_ge(self.sem("step"), 3)
        act.activation(ln, u, ACT.Ln).then_inc(self.sem("ln"), 1)

    def dve(self, dve):
        k, w = self.k, self.w
        e, u, ln, na, eq, num, den, x2 = (k.tmp[:, i * 64:i * 64 + w] for i in range(8))
        step = self.sem("step")
        self.side_out("dve", dve, 0, 1)
        self.join(dve)
        self.pre(dve, x2).then_inc(step, 1)
        dve.wait_ge(step, 1)
        dve.scalar_tensor_tensor(na, x2, -1.0, x2, ALU.mult, ALU.min).then_inc(step, 1)
        dve.wait_ge(self.sem("exp"), 1)
        dve.tensor_scalar(u, e, 1.0, None, ALU.add).then_inc(step, 1)
        dve.wait_ge(step, 3)
        dve.tensor_scalar(den, u, 1.0, None, ALU.subtract).then_inc(step, 1)
        dve.wait_ge(step, 4)
        dve.tensor_scalar(eq, den, 0.0, None, ALU.is_equal).then_inc(step, 1)
        dve.wait_ge(step, 5)
        dve.wait_ge(self.sem("ln"), 1)
        dve.tensor_tensor(num, ln, eq, ALU.add).then_inc(step, 1)
        dve.tensor_tensor(den, den, eq, ALU.add).then_inc(step, 1)
        dve.wait_ge(step, 7)
        dve.reciprocal(den, den).then_inc(step, 1)
        dve.wait_ge(step, 8)
        dve.tensor_tensor(num, num, den, ALU.mult).then_inc(step, 1)
        dve.wait_ge(step, 9)
        dve.tensor_tensor(num, num, e, ALU.mult).then_inc(step, 1)
        dve.wait_ge(step, 10)
        dve.scalar_tensor_tensor(self.out, x2, 0.0, num, ALU.max, ALU.add).then_inc(step, 1)


class Turn(Stage):

    def __init__(self, k, name, prev, rows, p0, n, out):
        super().__init__(k, name, prev)
        self.rows, self.p0, self.n, self.out = rows, p0, n, out
        self.ends = [(self.sem("cols"), 1)]

    def pe(self, pe):
        k, p, n = self.k, slice(self.p0, self.p0 + self.n), self.n
        self.join(pe)
        for t in range(TT):
            tr = pe.transpose(k.ps[:, 7, t * n:(t + 1) * n], self.rows[p, t * P:(t + 1) * P],
                              k.cst[p, C_ID + self.p0:C_ID + self.p0 + n])
        tr.then_inc(self.sem("turned"), 1)

    def dve(self, dve):
        self.join(dve)
        dve.wait_ge(self.sem("turned"), 1)
        self.out(dve, self.k.ps[:, 7, 0:TT * self.n]).then_inc(self.sem("cols"), 1)


class Gates(Stage):

    def __init__(self, k, name, prev, sp, g8):
        super().__init__(k, name, prev)
        self.spf, self.g8 = sp, g8
        self.ends = [(self.sem("emt"), 1)]

    def pe(self, pe):
        k = self.k
        self.join(pe)
        for t in range(TT):
            pe.transpose(k.ps[0:MH, 4, t * P:(t + 1) * P], self.spf[:, t * MH:(t + 1) * MH], k.const(C_ID))
            tr = pe.transpose(k.ps[0:MH, 5, t * P:(t + 1) * P], self.g8[:, t * 8:t * 8 + MH], k.const(C_ID))
        tr.then_inc(self.sem("rows"), 1)
        self.side_pe(pe, 0, 2)
        pe.wait_ge(self.sem("scan"), 6)
        for t in range(TT):
            pe.transpose(k.ps[:, 6, t * MH:(t + 1) * MH], k.gr[0:MH, 2 * T + t * P:2 * T + (t + 1) * P],
                         k.const(C_ID)[0:MH, 0:MH])
            tr = pe.transpose(k.ps[:, 7, t * MH:(t + 1) * MH], k.gr[0:MH, t * P:(t + 1) * P],
                              k.const(C_ID)[0:MH, 0:MH])
        tr.then_inc(self.sem("cols"), 1)
        self.side_pe(pe, 1, 2)

    def dve(self, dve):
        k = self.k
        self.side_out("dve", dve, 0, 2)
        b, ig, a, m = (k.gr[0:MH, i * T:(i + 1) * T] for i in range(4))
        s = self.sem("scan")
        self.join(dve)
        dve.wait_ge(self.sem("rows"), 1)
        dve.tensor_copy(m, k.ps[0:MH, 4, :]).then_inc(s, 1)
        dve.wait_ge(s, 1)
        dve.tensor_tensor_scan(b, k.ones(MH, T), m, 0.0, ALU.mult, ALU.subtract).then_inc(s, 1)
        dve.wait_ge(s, 2)
        dve.tensor_tensor(a, k.ps[0:MH, 5, :], b, ALU.subtract).then_inc(s, 1)
        dve.wait_ge(s, 3)
        dve.tensor_tensor_scan(m, k.ones(MH, T), a, -BIG, ALU.mult, ALU.max).then_inc(s, 1)
        dve.wait_ge(s, 4)
        dve.tensor_tensor(ig, b, m, ALU.add).then_inc(s, 1)
        dve.wait_ge(s, 5)
        dve.tensor_scalar(b, ig, -1.0, 80.0, ALU.mult, ALU.min).then_inc(s, 1)
        dve.wait_ge(self.sem("cols"), 1)
        dve.tensor_copy(k.acol[:, 0:16], k.ps[:, 6, 0:16]).then_inc(self.sem("acol"), 1)

    def act(self, act):
        k = self.k
        self.side_out("act", act, 1, 2)
        act.wait_ge(self.sem("cols"), 1)
        act.wait_ge(self.sem("acol"), 1)
        act.activation(k.acol[:, 16:32], k.ps[:, 7, 0:16], ACT.Exp).then_inc(self.sem("emt"), 1)


class Mlstm(Stage):

    H_AT = 2 * T + TT * (TT + 1) // 2 * P
    SCRATCH = H_AT + MH * T

    def __init__(self, k, name, prev, qk, v, mo, mo_ready, scr, mb, yhi, ylo, ncol):
        super().__init__(k, name, prev)
        self.qk, self.v, self.mo, self.yhi, self.ylo, self.ncol = qk, v, mo, yhi, ylo, ncol
        self.mo_ready = mo_ready
        self.e = k.at(f"{name}_decay", scr, 2 * T)
        self.sq = k.at(f"{name}_squares", scr, T)
        self.pt = k.at(f"{name}_weighted", scr + 2 * T, self.H_AT - 2 * T)
        self.hn = k.at(f"{name}_h", scr + self.H_AT, MH * T)
        self.mb = k.at(f"{name}_maxima", mb, MH * T)
        self.yt = k.at(f"{name}_y", mb, MH * T)
        self.ends = [(self.sem("lo"), MH), (self.sem("hi"), MH)]
        self.steps = MH * (TT + 1) + MH + 4

    def num(self):
        return self.k.ps[:, 6:8, 0:2 * (MD + 1)].rearrange("p b (t d) -> p b t d", d=MD + 1)

    def weights(self, s, a, b):
        off = sum(T - x * P for x in range(s)) - s * P
        return self.pt[:, off + a:off + b]

    def pe(self, pe):
        k = self.k
        self.join(pe)
        step = 0
        for h in range(MH):
            pe.matmul(k.ps[:, 4 + h, :], k.pick(h, MH), k.gr[0:MH, 3 * T:4 * T], start=True, stop=True)\
              .then_inc(self.sem("spread"), 1)
        for h in range(MH):
            if h == 0:
                pe.wait_ge(self.sem("maxima"), MH)
            for s in range(TT):
                n = h * TT + s
                if n >= 2:
                    pe.wait_ge(self.sem("weighted"), n - 1)
                pe.matmul(k.ps[:, 4 + n % 2, s * P:T], self.qk[:, (4 + h) * T + s * P:(4 + h) * T + (s + 1) * P],
                          self.qk[:, h * T + s * P:(h + 1) * T], start=True, stop=True)\
                  .then_inc(self.sem("scores"), 1)
                self.side_pe(pe, step, self.steps)
                step += 1
            pe.wait_ge(self.sem("weighted"), TT * (h + 1))
            if h >= 1:
                pe.wait_ge(self.sem("h"), h)
            for t in range(TT):
                for s in range(t + 1):
                    mm = pe.matmul(self.num()[:, t // 2, t % 2, :], self.weights(s, t * P, (t + 1) * P),
                                   self.v[:, (s * MH + h) * (MD + 1):(s * MH + h + 1) * (MD + 1)],
                                   start=s == 0, stop=s == t)
            mm.then_inc(self.sem("sums"), 1)
            if h == MH - 1:
                step += 3
            self.side_pe(pe, step, self.steps)
            step += 1
        pe.wait_ge(self.sem("normed"), 1)
        for h in range(MH):
            if h >= 2:
                pe.wait_ge(self.sem("yt"), h - 1)
            for t in range(TT):
                tr = pe.transpose(k.ps[:, 4 + h % 2, t * P:(t + 1) * P],
                                  self.hn[:, (h * TT + t) * P:(h * TT + t + 1) * P], k.const(C_ID))
            tr.then_inc(self.sem("fm"), 1)
            self.side_pe(pe, step, self.steps)
            step += 1
        self.side_pe(pe, step, self.steps)

    def dve(self, dve):
        k = self.k
        self.join(dve)
        st = k.stat
        step = self.sem("stat")
        ns = 0

        def gap(h, s):
            n = h * TT + s
            if n >= 2:
                dve.wait_ge(self.sem("weighted"), n - 1)
            t = self.e[:, n % 2 * T + s * P:(n % 2 + 1) * T]
            dve.tensor_scalar(t, self.mb[:, h * T + s * P:(h + 1) * T], k.acol[:, s * MH + h:s * MH + h + 1],
                              0.0, ALU.subtract, ALU.max).then_inc(self.sem("gap0"), 1)
            dve.wait_ge(self.sem("gap0"), n + 1)
            d = self.e[:, n % 2 * T + s * P:n % 2 * T + (s + 1) * P]
            dve.tensor_tensor(d, d, k.const(C_ST), ALU.add).then_inc(self.sem("gap"), 1)

        def weigh(h, s):
            n = h * TT + s
            if h >= 1 and s == 0:
                dve.wait_ge(self.sem("sums"), h)
            dve.wait_ge(self.sem("scores"), n + 1)
            dve.wait_ge(self.sem("decay"), n + 1)
            dve.scalar_tensor_tensor(self.weights(s, s * P, T), k.ps[:, 4 + n % 2, s * P:T],
                                     MD ** -0.5, self.e[:, n % 2 * T + s * P:(n % 2 + 1) * T],
                                     ALU.mult, ALU.mult).then_inc(self.sem("weighted"), 1)
        for h in range(MH):
            if h == 0:
                dve.wait_ge(self.sem("maxima"), MH)
            else:
                dve.wait_ge(self.sem("ssq"), h)
            gap(h, 0)
            for s in range(TT):
                self.side_out("dve", dve, h * (TT + 1) + s, self.steps)
                if s + 1 < TT:
                    gap(h, s + 1)
                weigh(h, s)
            self.side_out("dve", dve, h * (TT + 1) + TT, self.steps)
            dve.wait_ge(self.sem("sums"), h + 1)
            num = self.num()
            den = st[:, h * TT:(h + 1) * TT]
            den4 = den.rearrange("p (b t) -> p b t", b=2)
            emt = k.acol[:, 16:32].rearrange("p (b t h) -> p b t h", b=2, h=MH)[:, :, :, h]
            dve.tensor_copy(den4, num[:, :, :, MD]).then_inc(step, 1)
            dve.wait_ge(step, ns + 1)
            dve.scalar_tensor_tensor(den4, den4, -1.0, den4, ALU.mult, ALU.max).then_inc(step, 1)
            dve.wait_ge(step, ns + 2)
            dve.tensor_tensor(den4, den4, emt, ALU.max).then_inc(step, 1)
            dve.wait_ge(step, ns + 3)
            dve.reciprocal(den, den).then_inc(step, 1)
            dve.wait_ge(step, ns + 4)
            hn = self.hn[:, h * T:(h + 1) * T].rearrange("p (b t d) -> p b t d", b=2, d=MD)
            dve.tensor_tensor(hn, num[:, :, :, 0:MD], den4.unsqueeze(3).broadcast_to([P, 2, 2, MD]),
                              ALU.mult).then_inc(self.sem("h"), 1)
            dve.wait_ge(self.sem("h"), h + 1)
            dve.wait_ge(self.sem("weighted"), TT * (h + 1))
            flat = self.hn[:, h * T:(h + 1) * T]
            dve.tensor_tensor(self.sq[:, :], flat, flat, ALU.mult).then_inc(step, 1)
            ns += 5
            dve.wait_ge(step, ns)
            dve.tensor_reduce(st[:, 16 + h * TT:16 + (h + 1) * TT],
                              self.sq[:, :].rearrange("p (t d) -> p t d", d=MD), AX.X, ALU.add)\
               .then_inc(self.sem("ssq"), 1)
        self.side_out("dve", dve, MH * (TT + 1), self.steps)
        for ready, value in self.mo_ready:
            dve.wait_ge(ready, value)
        dve.tensor_scalar(self.mo[:, :], self.mo[:, :], 0.5, 0.5, ALU.mult, ALU.add)\
           .then_inc(self.sem("out_gate"), 1)
        dve.wait_ge(self.sem("root"), 1)
        dve.reciprocal(st[:, 48:64], st[:, 32:48]).then_inc(step, 1)
        dve.wait_ge(step, ns + 1)
        hn = self.hn[:, :].rearrange("p (g d) -> p g d", d=MD)
        dve.tensor_tensor(hn, hn, st[:, 48:64].unsqueeze(2).broadcast_to([P, 16, MD]), ALU.mult)\
           .then_inc(self.sem("normed"), 1)
        for h in range(MH):
            y = self.yt[:, h * T:(h + 1) * T]
            self.side_out("dve", dve, MH * (TT + 1) + 3 + h, self.steps)
            dve.wait_ge(self.sem("fm"), h + 1)
            if h == 0:
                dve.wait_ge(self.sem("out_gate"), 1)
            dve.scalar_tensor_tensor(y, k.ps[:, 4 + h % 2, :], k.col(self.ncol + h),
                                     self.mo[:, h * T:(h + 1) * T], ALU.mult, ALU.mult)\
               .then_inc(self.sem("yt"), 1)
        for h in range(MH):
            dve.wait_ge(self.sem("yt"), h + 1)
            dve.wait_ge(self.sem("hi"), h + 1)
            dve.tensor_tensor(self.ylo[:, h * T:(h + 1) * T], self.yt[:, h * T:(h + 1) * T],
                              self.yhi[:, h * T:(h + 1) * T], ALU.subtract).then_inc(self.sem("lo"), 1)

    def act(self, act):
        k = self.k
        self.join(act)
        for h in range(MH):
            act.wait_ge(self.sem("spread"), h + 1)
            act.activation(self.mb[:, h * T:(h + 1) * T], k.ps[:, 4 + h, :], ACT.Copy)\
               .then_inc(self.sem("maxima"), 1)
        for n in range(MH * TT):
            h, s = divmod(n, TT)
            self.side_out("act", act, h * (TT + 1) + s, self.steps)
            act.wait_ge(self.sem("gap"), n + 1)
            e = self.e[:, n % 2 * T + s * P:(n % 2 + 1) * T]
            act.activation(e, e, ACT.Exp, scale=-1.0).then_inc(self.sem("decay"), 1)
        self.side_out("act", act, MH * (TT + 1), self.steps)
        act.wait_ge(self.sem("ssq"), MH)
        act.activation(k.stat[:, 32:48], k.stat[:, 16:32], ACT.Sqrt, bias=k.eps[:, 0:1], scale=1.0 / MD)\
           .then_inc(self.sem("root"), 1)
        for h in range(MH):
            self.side_out("act", act, MH * (TT + 1) + 3 + h, self.steps)
            act.wait_ge(self.sem("yt"), h + 1)
            act.activation(self.yhi[:, h * T:(h + 1) * T], self.yt[:, h * T:(h + 1) * T], ACT.Copy)\
               .then_inc(self.sem("hi"), 1)


class Branches(Jobs):

    def __init__(self, k, name, prev, g, merged):
        super().__init__(k, name, prev)
        self.g, self.merged, self.gated = g, merged, 0
        self.users = [None] * 4
        self.final = {}

    def gate(self, wgate, half, bias=None, free=()):
        k = self.k
        self.gates = []
        for j in range(2):
            jobs = []
            for t in range(2 * j, 2 * j + 2):
                waits = [self.read(self.users[t])] if self.users[t] else list(free)

                def evac(act, bank, t=t, waits=waits):
                    for s, v in waits:
                        act.wait_ge(s, v)
                    more = {} if bias is None else {"bias": bias(4 * half + t)}
                    return act.activation(self.g[:, t * T:(t + 1) * T], k.ps[:, bank, :], ACT.Tanh,
                                          scale=0.5, **more)
                jobs.append(Job("act", evac, c=t % 2))
            at = self.unit(wgate(half * 512 + j * UC), KD, UC, k.hh, k.hl, jobs)
            self.gates += jobs
        return at

    def up(self, wup, kt, y, half, add, need=(), free=()):
        k = self.k
        nup = 2 if kt == KD else 1
        w = 512 // nup
        for j in range(nup):
            jobs = []
            for c in range(w // P):
                t = j * (w // P) + c
                waits = [self.read(self.gates[t])] + (list(free) if t == 0 else [])
                if add:
                    self.gated += 1

                def evac(dve, bank, t=t, n=self.gated, waits=waits):
                    g = self.g[:, t * T:(t + 1) * T]
                    m = self.merged[:, (4 * half + t) * T:(4 * half + t + 1) * T]
                    for s, v in waits:
                        dve.wait_ge(s, v)
                    ins = dve.scalar_tensor_tensor(g if add else m, g, 1.0, k.ps[:, bank, :], ALU.add, ALU.mult)
                    if not add:
                        return ins
                    ins.then_inc(self.sem("gated"), 1)
                    dve.wait_ge(self.sem("gated"), n)
                    return dve.tensor_tensor(m, m, g, ALU.add)
                jobs.append(Job("dve", evac, c=c, need=need if t == 0 else ()))
                self.users[t] = self.final[4 * half + t] = jobs[-1]
            at = self.unit(wup(half * 512 + j * w, w), kt, w, y[0], y[1], jobs)
        return at


class Split(Stage):

    def __init__(self, k, name, prev, x, hi, lo, upto, tile, part=None):
        super().__init__(k, name, prev)
        self.x, self.hi, self.lo, self.upto, self.tile = x, hi, lo, upto, tile
        self.t0 = part.upto if part else 0
        if part:
            self.s = part.s
        self.ready = self.sem("lo")
        self.ends = [(self.ready, upto)]

    def act(self, act):
        for t in range(self.t0, self.upto):
            s, v = self.tile(t)
            act.wait_ge(s, v)
            act.activation(self.hi[:, t * T:(t + 1) * T], self.x[:, t * T:(t + 1) * T], ACT.Copy)\
               .then_inc(self.sem("hi"), 1)

    def dve(self, dve):
        for t in range(self.t0, self.upto):
            s, v = self.tile(t)
            dve.wait_ge(s, v)
            dve.wait_ge(self.sem("hi"), t + 1)
            dve.tensor_tensor(self.lo[:, t * T:(t + 1) * T], self.x[:, t * T:(t + 1) * T],
                              self.hi[:, t * T:(t + 1) * T], ALU.subtract).then_inc(self.sem("lo"), 1)


class OutProj(Stage):

    BANK = 4

    def __init__(self, k, name, prev, w, x, xh, xl, read):
        super().__init__(k, name, prev)
        self.read = read
        self.w, self.x, self.xh, self.xl = w, x, xh, xl
        self.u0 = units(k, 4)
        self.ends = [(self.sem("added"), 8)]

    def tile(self, t):
        return self.sem("added"), t + 1

    def bank(self, c):
        return self.k.ps[:, (self.BANK + c) % 8, :]

    def sp(self, sp):
        for j in range(4):
            load_unit(self.k, sp, self.u0 + j, 0, self.w(j * UC, UC), UC)

    def pe(self, pe):
        k = self.k
        for j in range(4):
            wait_split(k, pe, self.u0 + j)
            if j == 2:
                for s, v in self.read:
                    pe.wait_ge(s, v)
            fm_unit(k, pe, self.u0 + j, KD, UC, self.xh, self.xl, [self.bank(2 * j + i) for i in range(2)],
                    self.x if j == 0 else None, self.sem("even")).then_inc(k.unit_used, 1)
            if j:
                self.stats.sum(pe, 2 * j - 2)
                self.stats.sum(pe, 2 * j - 1)
        self.stats.sum(pe, 6)
        self.stats.sum(pe, 7)

    def act(self, act):
        for j in range(4):
            if j < 3:
                hi_unit(self.k, act, self.u0 + j + 2, 0)
            self.stats.square(act, 2 * j)
            self.stats.square(act, 2 * j + 1)
        self.stats.ahead = self.u0 + 5

    def dve(self, dve):
        k = self.k
        for j in range(4):
            for c in range(2 * j, 2 * j + 2):
                if c % 2:
                    dve.wait_ge(k.unit_used, self.u0 + j + 1)
                else:
                    dve.wait_ge(self.sem("even"), j + 1)
                x = k.xT[:, c * T:(c + 1) * T]
                dve.scalar_tensor_tensor(x, self.bank(c), 0.5, x, ALU.mult, ALU.add)\
                   .then_inc(self.sem("added"), 1)


class Up(Stage):

    def __init__(self, k, name, prev, before, src, n, fhi, flo, scr):
        super().__init__(k, name, prev)
        self.before = before
        self.src, self.n, self.fhi, self.flo = src, n, fhi, flo
        self.r = scr[0]
        self.f = scr[1]
        self.u0 = units(k, n)
        self.ends = [(self.sem("lo"), n), (self.sem("hi"), n)]
        self.banks = [(self.sem("r"), n)]

    def sp(self, sp):
        with sp.Fori(0, self.n // 2) as i:
            for j in range(2):
                load_unit(self.k, sp, self.u0 + j, i * 2, self.src(j, i * 2), UC)

    def pe(self, pe):
        k = self.k
        after_down = isinstance(self.before, Down)

        def unit(j, du):
            wait_split(k, pe, self.u0 + j, du)
            if isinstance(du, int) and du + j < 2:
                if after_down:
                    pe.wait_ge(*self.before.tile(2 * j + 1))
            else:
                pe.wait_ge(self.sem("r"), du + (j - 1))
            fm_unit(k, pe, self.u0 + j, KD, UC, k.hh, k.hl, [k.ps[:, 2 * j + c, :] for c in range(2)],
                    self.before if not after_down and isinstance(du, int) and du + j == 0 else None)\
                .then_inc(k.unit_used, 1)
        unit(0, 0)
        unit(1, 0)
        with pe.Fori(1, self.n // 2) as i:
            unit(0, i * 2)
            unit(1, i * 2)

    def out(self, x, j, du):
        w = UT * T
        return x[:, bass.ds(du * w + j * w, w)]

    def act(self, act):
        k = self.k
        self.join(act)

        def unit(j, du):
            w = UT * T
            r, f = self.r[:, j * w:(j + 1) * w], self.f[:, j * w:(j + 1) * w]
            act.wait_ge(k.unit_used, du + (self.u0 + j + 1))
            if not (isinstance(du, int) and du + j < 2):
                act.wait_ge(self.sem("f"), du + (j - 1))
            act.activation(r, k.ps[:, 2 * j:2 * j + 2, :].rearrange("p a b -> p (a b)"), ACT.Relu)\
               .then_inc(self.sem("r"), 1)
            hi_unit(k, act, self.u0 + j + 2, du)
            act.wait_ge(self.sem("f"), du + (j + 1))
            act.activation(self.out(self.fhi, j, du), f, ACT.Copy).then_inc(self.sem("hi"), 1)
        unit(0, 0)
        unit(1, 0)
        with act.Fori(1, self.n // 2) as i:
            unit(0, i * 2)
            unit(1, i * 2)

    def dve(self, dve):
        k = self.k
        self.join(dve)

        def unit(j, du):
            w = UT * T
            r, f = self.r[:, j * w:(j + 1) * w], self.f[:, j * w:(j + 1) * w]
            dve.wait_ge(self.sem("r"), du + (j + 1))
            if not (isinstance(du, int) and du + j < 2):
                dve.wait_ge(self.sem("hi"), du + (j - 1))
            dve.tensor_tensor(f, r, r, ALU.mult).then_inc(self.sem("f"), 1)
            dve.wait_ge(self.sem("hi"), du + (j + 1))
            dve.tensor_tensor(self.out(self.flo, j, du), f, self.out(self.fhi, j, du), ALU.subtract)\
               .then_inc(self.sem("lo"), 1)
        unit(0, 0)
        unit(1, 0)
        with dve.Fori(1, self.n // 2) as i:
            unit(0, i * 2)
            unit(1, i * 2)


class Glu(Stage):

    def __init__(self, k, name, prev, norm, src, n, fhi, flo, scr):
        super().__init__(k, name, prev)
        self.norm = norm
        self.src, self.n, self.fhi, self.flo = src, n, fhi, flo
        self.r, self.f = scr[0][:, :], scr[1][:, :]
        self.u0 = units(k, 2 * n)
        self.ends = [(self.sem("lo"), n), (self.sem("hi"), n)]
        self.banks = [(self.sem("silu"), n), (self.sem("f"), n)]

    def pairs(self, eng, body):
        body(0)
        with eng.Fori(1, self.n) as i:
            body(i)

    def sp(self, sp):
        with sp.Fori(0, self.n) as i:
            for j in range(2):
                load_unit(self.k, sp, self.u0 + j, i * 2, self.src(j, i), UC)

    def pe(self, pe):
        k = self.k

        def pair(i):
            for j in range(2):
                wait_split(k, pe, self.u0 + j, i * 2)
                if not isinstance(i, int):
                    pe.wait_ge(self.sem("f" if j else "silu"), i)
                fm_unit(k, pe, self.u0 + j, KD, UC, k.hh, k.hl, [k.ps[:, 2 * j + c, :] for c in range(2)],
                        self.norm if isinstance(i, int) and j == 0 else None).then_inc(k.unit_used, 1)
        self.pairs(pe, pair)

    def tiles(self, x, i):
        return x[:, bass.ds(i * (2 * T), 2 * T)]

    def act(self, act):
        k = self.k
        self.join(act)

        def pair(i):
            act.wait_ge(k.unit_used, i * 2 + (self.u0 + 1))
            if not isinstance(i, int):
                act.wait_ge(self.sem("f"), i)
            act.activation(self.r, k.ps[:, 0:2, :].rearrange("p a b -> p (a b)"), ACT.Silu)\
               .then_inc(self.sem("silu"), 1)
            hi_unit(k, act, self.u0 + 2, i * 2)
            hi_unit(k, act, self.u0 + 3, i * 2)
            act.wait_ge(self.sem("f"), i + 1)
            act.activation(self.tiles(self.fhi, i), self.f, ACT.Copy).then_inc(self.sem("hi"), 1)
        self.pairs(act, pair)

    def dve(self, dve):
        k = self.k
        self.join(dve)

        def pair(i):
            dve.wait_ge(self.sem("silu"), i + 1)
            dve.wait_ge(k.unit_used, i * 2 + (self.u0 + 2))
            if not isinstance(i, int):
                dve.wait_ge(self.sem("hi"), i)
                dve.wait_ge(self.sem("lo"), i)
            dve.tensor_tensor(self.f, self.r, k.ps[:, 2:4, :].rearrange("p a b -> p (a b)"), ALU.mult)\
               .then_inc(self.sem("f"), 1)
            dve.wait_ge(self.sem("hi"), i + 1)
            dve.tensor_tensor(self.tiles(self.flo, i), self.f, self.tiles(self.fhi, i), ALU.subtract)\
               .then_inc(self.sem("lo"), 1)
        self.pairs(dve, pair)


class Down(Stage):

    def __init__(self, k, name, prev, up, src, n, fhi, flo, last=False, following=()):
        super().__init__(k, name, prev)
        self.up, self.stats, self.following = up, None, following
        self.src, self.n, self.fhi, self.flo, self.last = src, n, fhi, flo, last
        self.u0 = units(k, n)
        self.u1 = units(k, len(following))
        self.ends = [(self.sem("added"), 8)]

    def tile(self, t):
        return self.sem("added"), t + 1

    def sp(self, sp):
        k = self.k
        with sp.Fori(0, self.n // 2) as i:
            for j in range(2):
                load_unit(k, sp, self.u0 + j, i * 2, self.src(j, i * 2), D)
        if self.n % 2:
            load_unit(k, sp, self.u0 + self.n - 1, 0, self.src(0, self.n - 1), D)
        for n, src in enumerate(self.following):
            load_unit(k, sp, self.u1 + n, 0, src, UC)

    def pe(self, pe):
        k = self.k

        def unit(j, du, first=False, last=False):
            a = k.slot(self.u0 + j) * SLOT
            wait_split(k, pe, self.u0 + j, du)
            pe.wait_ge(self.up.sem("lo"), du + (j + 1))
            for n, c in enumerate((4, 5, 6, 7, 0, 1, 2, 3) if first else range(KD)):
                if first and n == 4:
                    for s, v in self.up.banks:
                        pe.wait_ge(s, v)
                for i in range(2):
                    w = slice(a + i * D + c * P, a + i * D + (c + 1) * P)
                    x = bass.ds(du * (2 * T) + (j * 2 + i) * T, T)
                    pe.matmul(k.ps[:, c, :], k.whi[:, w], self.fhi[:, x], start=first and i == 0,
                              stop=False, skip_group_check=True)
                    pe.matmul(k.ps[:, c, :], k.whi[:, w], self.flo[:, x], start=False, stop=False,
                              skip_group_check=True)
                    mm = pe.matmul(k.ps[:, c, :], k.wlo[:, w], self.fhi[:, x], start=False,
                                   stop=last and i == 1, skip_group_check=True)
                if last and c < KD - 1:
                    mm.then_inc(self.sem("tile"), 1)
                if n == KD - 1:
                    mm.then_inc(k.unit_used, 1)
                if last and self.stats and c >= 2:
                    self.stats.sum(pe, c - 2)
            if last and self.stats:
                self.stats.sum(pe, KD - 2)
                self.stats.sum(pe, KD - 1)
        odd = self.n % 2
        unit(0, 0, first=True)
        unit(1, 0)
        end = self.n - 1 if odd else self.n - 2
        with pe.Fori(1, end // 2) as i:
            unit(0, i * 2)
            unit(1, i * 2)
        if odd:
            unit(0, self.n - 1, last=True)
        else:
            unit(0, self.n - 2)
            unit(1, self.n - 2, last=True)

    def act(self, act):
        k = self.k
        n = self.n - 1 if self.following else self.n - 2 if self.last else self.n
        with act.Fori(0, n // 2) as i:
            for j in range(2):
                hi_unit(k, act, self.u0 + j + 2, i * 2)
        if n % 2:
            hi_unit(k, act, self.u0 + n - 1 + 2, 0)
        if self.stats:
            for t in range(KD):
                self.stats.square(act, t)
            if self.following:
                self.stats.ahead, self.stats.urgent = self.u1 + 1, True

    def dve(self, dve):
        k = self.k
        for c in range(KD):
            if c < KD - 1:
                dve.wait_ge(self.sem("tile"), c + 1)
            else:
                dve.wait_ge(k.unit_used, self.u0 + self.n)
            x = k.xT[:, c * T:(c + 1) * T]
            dve.tensor_tensor(x, x, k.ps[:, c, :], ALU.add).then_inc(self.sem("added"), 1)


class Params(Stage):

    def __init__(self, k, name, free, sets, at):
        super().__init__(k, name, [])
        self.free, self.sets = free, sets
        self.prow = [k.at(f"{name}_rows{i}", at + i * P, P) for i in range(len(sets))]
        self.ends = [(self.sem("cols"), len(sets))]

    def sp(self, sp):
        for prow, (rows, _) in zip(self.prow, self.sets):
            for src, r, n in rows:
                sp.dma_start(prow[r:r + n, :], src).then_inc(self.sem("landed"), 16)

    def pe(self, pe):
        k = self.k
        pe.wait_ge(*self.free)
        pe.wait_ge(self.sem("landed"), 16 * sum(len(rows) for rows, _ in self.sets))
        for i, prow in enumerate(self.prow):
            tr = pe.transpose(k.ps[:, 7, i * P:i * P + NPC], prow[0:NPC, :], k.const(C_ID)[0:NPC, 0:NPC])
        tr.then_inc(self.sem("turned"), 1)

    def dve(self, dve):
        dve.wait_ge(self.sem("turned"), 1)
        for i, (_, dst) in enumerate(self.sets):
            dve.tensor_copy(dst, self.k.ps[:, 7, i * P:i * P + NPC]).then_inc(self.sem("cols"), 1)


class Columns(Stage):

    def __init__(self, k, name, prev, src, half, bcasts):
        super().__init__(k, name, prev)
        self.src, self.half, self.bcasts = src, half, bcasts
        self.spread = [(self.sem("spread"), 16 * len(bcasts))]
        self.ends = [(self.sem("cols"), 2)] if src is not None else []

    def sp(self, sp):
        for dst, src in self.bcasts:
            sp.dma_start(dst, src).then_inc(self.sem("spread"), 16)

    def dve(self, dve):
        k = self.k
        if self.src is not None:
            a, n = self.half
            dve.tensor_copy(k.pcol[:, :], self.src).then_inc(self.sem("cols"), 1)
            dve.wait_ge(self.sem("cols"), 1)
            dve.tensor_scalar(k.hbias[:, 0:n], k.pcol[:, a:a + n], 0.5, None, ALU.mult)\
               .then_inc(self.sem("cols"), 1)


class Lead(Stage):

    def __init__(self, k, name, prev, stats):
        super().__init__(k, name, prev)
        self.stats = stats

    def act(self, act):
        for t in range(KD):
            self.stats.square(act, t)
        hi_unit(self.k, act, 0, 0)
        self.stats.ahead = 1

    def pe(self, pe):
        for t in range(KD):
            self.stats.sum(pe, t)


class Preload(Lead):

    def __init__(self, k, name, prev, srcs, stats):
        super().__init__(k, name, prev, stats)
        self.srcs = srcs
        units(k, 2)

    def sp(self, sp):
        for u, src in enumerate(self.srcs):
            load_unit(self.k, sp, u, 0, src, UC)


class Fill(Stage):

    def __init__(self, k, name, prev, fills, more=()):
        super().__init__(k, name, prev)
        self.fills = fills
        self.ends = [(self.sem("filled"), len(fills)), *more]

    def dve(self, dve):
        self.join(dve)
        for ap, value in self.fills:
            dve.memset(ap, value).then_inc(self.sem("filled"), 1)


class Setup(Stage):

    def __init__(self, k, name, prev, x, table):
        super().__init__(k, name, prev)
        self.x, self.table = x, table
        self.xtm = k.at("setup_x", 0, TT * D)
        self.ends = [(self.sem("fm_act"), 4), (self.sem("fm_dve"), 4)]

    def tile(self, t):
        return self.sem("fm_dve" if t % 2 else "fm_act"), t // 2 + 1

    def sp(self, sp):
        sp.dma_start(self.k.cst[:, 0:C_ROT], self.table[:, 0:C_ROT]).then_inc(self.sem("identity"), 16)
        for t in range(TT):
            sp.dma_start(self.xtm[:, t * D:(t + 1) * D], self.x[0, t * P:(t + 1) * P, :])\
              .then_inc(self.sem(f"x{t}"), 16)
        sp.dma_start(self.k.cst[:, C_ROT:C_END], self.table[:, C_ROT:C_END]).then_inc(self.sem("table"), 16)

    def pe(self, pe):
        k = self.k
        pe.wait_ge(self.sem("identity"), 16)
        for t in range(TT):
            pe.wait_ge(self.sem(f"x{t}"), 16)
            for c in range(KD):
                tr = pe.transpose(k.ps[:, c, t * P:(t + 1) * P],
                                  self.xtm[:, t * D + c * P:t * D + (c + 1) * P], k.const(C_ID))
                if t == TT - 1:
                    tr.then_inc(self.sem("turned"), 1)

    def act(self, act):
        k = self.k
        for c in range(0, KD, 2):
            act.wait_ge(self.sem("turned"), c + 1)
            act.activation(k.xT[:, c * T:(c + 1) * T], k.ps[:, c, :], ACT.Copy).then_inc(self.sem("fm_act"), 1)
        act.wait_ge(self.sem("eps"), 1)

    def dve(self, dve):
        k = self.k
        dve.memset(k.eps[:, :], EPS).then_inc(self.sem("eps"), 1)
        for c in range(1, KD, 2):
            dve.wait_ge(self.sem("turned"), c + 1)
            dve.tensor_copy(k.xT[:, c * T:(c + 1) * T], k.ps[:, c, :]).then_inc(self.sem("fm_dve"), 1)


class Angles(Stage):

    def __init__(self, k, name, prev, positions, table):
        super().__init__(k, name, prev)
        self.positions, self.table = positions, table
        self.posi = k.at("setup_positions", TT * D, T, I32)
        self.w = [k.at(f"setup_w{i}", TT * D + (i + 1) * T, T) for i in range(4)]
        self.ends = [(self.sem("step"), 16)]

    def sp(self, sp):
        sp.dma_start(self.posi[:, :], self.positions.broadcast_to([P, T])).then_inc(self.sem("pos"), 16)

    def dve(self, dve):
        k = self.k
        step = self.sem("step")
        done = 0

        def then(ins):
            nonlocal done
            done += 1
            ins.then_inc(step, 1)
            dve.wait_ge(step, done)
        dve.wait_ge(self.table, 16)
        dve.wait_ge(self.sem("pos"), 16)
        pos, ang, rs, rc = (w[:, :] for w in self.w)
        then(dve.tensor_copy(pos, self.posi[:, :]))
        then(dve.tensor_scalar(ang, pos, k.cst[:, C_INV:C_INV + 1], None, ALU.mult))
        magic = 1.5 * 2 ** 23
        two_pi = 2 * math.pi
        hi = 6.28125
        for out, turn, shift in ((rs, 0.0, 0.0), (rc, 0.25, math.pi / 2)):
            then(dve.tensor_scalar(pos, ang, 1 / two_pi, turn, ALU.mult, ALU.add))
            then(dve.tensor_scalar(pos, pos, magic, None, ALU.add))
            then(dve.tensor_scalar(pos, pos, magic, None, ALU.subtract))
            then(dve.scalar_tensor_tensor(out, pos, -hi, ang, ALU.mult, ALU.add))
            then(dve.scalar_tensor_tensor(out, pos, -(two_pi - hi), out, ALU.mult, ALU.add))
            lim = 3.1415925
            then(dve.tensor_scalar(out, out, shift, lim, ALU.add, ALU.min))
            then(dve.tensor_scalar(out, out, -lim, None, ALU.max))


class Rotary(Stage):

    def __init__(self, k, name, prev, angles):
        super().__init__(k, name, prev)
        self.rs, self.rc = angles.w[2], angles.w[3]

    def act(self, act):
        k = self.k
        self.join(act)
        act.activation(k.sin[:, :], self.rs[:, :], ACT.Sin).then_inc(self.sem("sines"), 1)
        act.activation(k.cos[:, :], self.rc[:, :], ACT.Sin).then_inc(self.sem("sines"), 1)

    def dve(self, dve):
        k = self.k
        dve.wait_ge(self.sem("sines"), 2)
        dve.tensor_scalar(k.cos[:, :], k.cos[:, :], k.cst[:, C_MSK:C_MSK + 1], k.cst[:, C_UNM:C_UNM + 1],
                          ALU.mult, ALU.add).then_inc(self.sem("cos"), 1)


class SsdPrep(Stage):

    def __init__(self, k, name, prev, c, xs, bt, cb, rows, s):
        super().__init__(k, name, prev)
        self.c, self.xs, self.bt, self.cb, self.rows, self.s = c, xs, bt, cb, rows, s
        self.ends = [(self.sem("tm_act"), 5), (self.sem("tm_dve"), 5), (self.sem("step"), 10),
                     (self.sem("exps"), 4), (self.sem("cb"), 2)]

    STEPS = 16

    def pe(self, pe):
        k = self.k
        self.join(pe)
        for c in range(10):
            if c >= 2:
                pe.wait_ge(self.sem("tm_act" if c % 2 == 0 else "tm_dve"), c // 2)
            for t in range(TT):
                tr = pe.transpose(k.ps[:, 4 + c % 2, t * P:(t + 1) * P],
                                  self.c[:, c * T + t * P:c * T + (t + 1) * P], k.const(C_ID))
            tr.then_inc(self.sem("turned"), 1)
            self.side_pe(pe, c, self.STEPS)
        for g in range(SG):
            for t in range(TT):
                a = slice((8 + g) * T + t * P, (8 + g) * T + (t + 1) * P)
                b = slice((10 + g) * T + t * P, (10 + g) * T + (t + 1) * P)
                mm = pe.matmul(k.ps[:, 6 + g, t * P:(t + 1) * P], self.c[:, a], self.c[:, b],
                               start=True, stop=True)
            mm.then_inc(self.sem("products"), 1)
        self.side_pe(pe, 10, self.STEPS)
        pe.wait_ge(self.sem("step"), 1)
        pe.wait_ge(self.sem("tm_act"), 5)
        pe.wait_ge(self.sem("tm_dve"), 5)
        for t in range(TT):
            tr = pe.transpose(k.ps[0:SH, 4, t * P:(t + 1) * P], self.s["a"][:, t * SH:(t + 1) * SH],
                              k.const(C_ID))
        tr.then_inc(self.sem("arows"), 1)
        self.side_pe(pe, 12, self.STEPS)
        pe.wait_ge(self.sem("step"), 6)
        for t in range(TT):
            tr = pe.transpose(k.ps[:, 5, t * SH:(t + 1) * SH], self.rows[0:SH, T + t * P:T + (t + 1) * P],
                              k.const(C_ID)[0:SH, 0:SH])
        tr.then_inc(self.sem("cols"), 1)
        self.side_pe(pe, 15, self.STEPS)
        pe.wait_ge(self.sem("step"), 7)
        pe.wait_ge(self.sem("cb"), 1)
        last = k.cst[:, C_ID + P - 1:C_ID + P].broadcast_to([P, P])
        pe.matmul(k.ps[:, 6, 0:TT * SH], last, self.s["loc"], start=True, stop=True)\
          .then_inc(self.sem("total"), 1)

    def tm(self, c):
        if c < 8:
            return self.xs[:, :].rearrange("p (t f) -> p t f", t=TT)[:, :, c * P:(c + 1) * P]
        return self.bt[:, :].rearrange("p (t f) -> p t f", t=TT)[:, :, (c - 8) * P:(c - 7) * P]

    def act(self, act):
        k = self.k
        self.join(act)
        act.activation(self.s["A"], self.s["a_log"], ACT.Exp).then_inc(self.sem("exps"), 1)
        for c in range(0, 10, 2):
            self.side_out("act", act, c, self.STEPS)
            act.wait_ge(self.sem("turned"), c + 1)
            act.activation(self.tm(c), k.ps[:, 4, :].rearrange("p (t f) -> p t f", t=TT), ACT.Copy)\
               .then_inc(self.sem("tm_act"), 1)
        self.side_out("act", act, 13, self.STEPS)
        act.wait_ge(self.sem("step"), 9)
        act.activation(self.s["eloc"], self.s["loc"], ACT.Exp).then_inc(self.sem("exps"), 1)
        act.activation(self.s["etot"], self.s["tot"], ACT.Exp).then_inc(self.sem("exps"), 1)
        act.activation(self.s["dec"], self.s["dec"], ACT.Exp).then_inc(self.sem("exps"), 1)

    def dve(self, dve):
        k, s = self.k, self.s
        step = self.sem("step")
        self.join(dve)
        dve.wait_ge(self.sem("exps"), 1)
        h16 = lambda x: x.rearrange("p (t h) -> p t h", h=SH)
        dve.scalar_tensor_tensor(h16(s["a"]), h16(s["dt"]), -1.0,
                                 s["A"].unsqueeze(1).broadcast_to([P, TT, SH]), ALU.mult, ALU.mult)\
           .then_inc(step, 1)
        for c in range(1, 10, 2):
            dve.wait_ge(self.sem("turned"), c + 1)
            dve.tensor_copy(self.tm(c), k.ps[:, 5, :].rearrange("p (t f) -> p t f", t=TT))\
               .then_inc(self.sem("tm_dve"), 1)
        for g in range(SG):
            dve.wait_ge(self.sem("products"), g + 1)
            dve.tensor_tensor(self.cb[:, g * T:(g + 1) * T].rearrange("p (t f) -> p t f", f=P),
                              k.ps[:, 6 + g, :].rearrange("p (t f) -> p t f", f=P),
                              k.const(C_KEEP).unsqueeze(1).broadcast_to([P, TT, P]), ALU.mult)\
               .then_inc(self.sem("cb"), 1)
        dve.wait_ge(self.sem("arows"), 1)
        dve.tensor_copy(self.rows[0:SH, 0:T], k.ps[0:SH, 4, :]).then_inc(step, 1)
        dve.wait_ge(step, 2)
        for t in range(TT):
            dve.tensor_tensor_scan(self.rows[0:SH, T + t * P:T + (t + 1) * P], k.ones(SH, P),
                                   self.rows[0:SH, t * P:(t + 1) * P], 0.0, ALU.mult, ALU.add)\
               .then_inc(step, 1)
        dve.wait_ge(self.sem("cols"), 1)
        dve.tensor_copy(s["loc"], k.ps[:, 5, 0:TT * SH]).then_inc(step, 1)
        dve.wait_ge(self.sem("total"), 1)
        dve.tensor_copy(s["tot"], k.ps[:, 6, 0:TT * SH]).then_inc(step, 1)
        dve.wait_ge(step, 8)
        dve.tensor_tensor(s["dec"], s["tot"], s["loc"], ALU.subtract).then_inc(step, 1)
        dve.wait_ge(self.sem("exps"), 4)
        dve.tensor_tensor(s["dtdec"], s["dt"], s["dec"], ALU.mult).then_inc(step, 1)


class Ssd(Stage):

    def __init__(self, k, name, prev, c, xs, bt, cb, rows, s, sz, scr):
        super().__init__(k, name, prev)
        self.c, self.xs, self.bt, self.cb, self.rows, self.s, self.sz = c, xs, bt, cb, rows, s, sz
        self.xdt = k.at(f"{name}_xdt", scr, D)
        self.xdd = k.at(f"{name}_xdecayed", scr + D, D)
        self.e = k.at(f"{name}_decay", scr + 2 * D, 2 * D)
        self.state = k.at(f"{name}_state", scr + 4 * D, D)
        self.y = k.at(f"{name}_y", scr + 5 * D, D)
        self.ends = [(self.sem("normed"), TT)]

    STEPS = 4 * TT

    def pe(self, pe):
        k = self.k
        self.join(pe)
        for t in range(TT):
            if t:
                pe.wait_ge(self.sem("within_read"), t)
                pe.wait_ge(self.sem("state"), t)
            for g in range(SG):
                for h in range(g * SPG, (g + 1) * SPG):
                    mm = pe.matmul(k.ps[:, 4 + h // 4, h % 4 * P:(h % 4 + 1) * P], k.pick(h, SH),
                                   self.rows[0:SH, T + t * P:T + (t + 1) * P], start=True, stop=True)
                mm.then_inc(self.sem("sums"), 1)
            self.side_pe(pe, 4 * t, self.STEPS)
            if t:
                pe.wait_ge(self.sem("gap"), SG * t + 1)
                for g in range(SG):
                    mm = pe.matmul(k.ps[:, 4 + g, :], self.c[:, (10 + g) * T + t * P:(10 + g) * T + (t + 1) * P],
                                   self.state[:, g * 512:(g + 1) * 512], start=True, stop=True)
                mm.then_inc(self.sem("across"), 1)
            self.side_pe(pe, 4 * t + 1, self.STEPS)
            pe.wait_ge(self.sem("gap"), SG * (t + 1))
            if t < TT - 1:
                pe.wait_ge(self.sem("xdd"), t + 1)
                for g in range(SG):
                    mm = pe.matmul(k.ps[:, 6 + g, :], self.bt[:, t * 256 + g * P:t * 256 + (g + 1) * P],
                                   self.xdd[:, g * 512:(g + 1) * 512], start=True, stop=True)
                mm.then_inc(self.sem("states"), 1)
            self.side_pe(pe, 4 * t + 2, self.STEPS)
            pe.wait_ge(self.sem("xdt"), t + 1)
            pe.wait_ge(self.sem("weighted"), SG * (t + 1))
            if t:
                pe.wait_ge(self.sem("off"), t)
            for h in range(SH):
                mm = pe.matmul(k.ps[:, 4 + h // SPG, h % SPG * SHD:(h % SPG + 1) * SHD],
                               self.e[:, h * P:(h + 1) * P], self.xdt[:, h * SHD:(h + 1) * SHD],
                               start=True, stop=True)
            mm.then_inc(self.sem("within"), 1)
            self.side_pe(pe, 4 * t + 3, self.STEPS)

    def dve(self, dve):
        k, s = self.k, self.s
        self.join(dve)
        hd = lambda x: x.rearrange("p (h d) -> p h d", d=SHD)
        bank = lambda b: k.ps[:, b:b + 2, :].rearrange("p b (h d) -> p (b h) d", d=SHD)
        per_head = lambda x, t, w: x[:, t * SH:(t + 1) * SH].unsqueeze(2).broadcast_to([P, SH, w])
        y, xdt = hd(self.y[:, :]), hd(self.xdt[:, :])
        local = self.sem("local")
        n = 0
        for t in range(TT):
            x = hd(self.xs[:, t * D:(t + 1) * D])
            if t:
                dve.wait_ge(self.sem("within"), t)
            for g in range(SG):
                dve.wait_ge(self.sem("sums"), SG * t + g + 1)
                dve.tensor_tensor(self.e[:, g * D:(g + 1) * D].rearrange("p (h t) -> p h t", t=P),
                                  k.ps[:, 4 + 2 * g:6 + 2 * g, :].rearrange("p b (h t) -> p (b h) t", t=P),
                                  s["loc"][:, t * SH + g * SPG:t * SH + (g + 1) * SPG].unsqueeze(2)
                                  .broadcast_to([P, SPG, P]), ALU.subtract).then_inc(self.sem("gap"), 1)
            for g in range(SG):
                e = self.e[:, g * D:(g + 1) * D]
                dve.wait_ge(self.sem("gap"), SG * t + g + 1)
                dve.tensor_scalar(e, e, 0.0, None, ALU.min).then_inc(self.sem("min"), 1)
            if t:
                dve.wait_ge(self.sem("states"), t)
            dve.tensor_tensor(hd(self.xdd[:, :]), x, per_head(s["dtdec"], t, SHD), ALU.mult)\
               .then_inc(self.sem("xdd"), 1)
            dve.tensor_tensor(xdt, x, per_head(s["dt"], t, SHD), ALU.mult).then_inc(self.sem("xdt"), 1)
            for g in range(SG):
                dve.wait_ge(self.sem("exp"), SG * t + g + 1)
                eg = self.e[:, g * D:(g + 1) * D].rearrange("p (h t) -> p h t", t=P)
                cb = self.cb[:, g * T + t * P:g * T + (t + 1) * P].unsqueeze(1).broadcast_to([P, SPG, P])
                dve.tensor_tensor(eg, eg, cb, ALU.mult).then_inc(self.sem("weighted"), 1)
            if t:
                dve.wait_ge(self.sem("across"), t)
                dve.wait_ge(self.sem("square"), t)
                dve.tensor_tensor(y, bank(4), per_head(s["eloc"], t, SHD), ALU.mult)\
                   .then_inc(self.sem("off"), 1)
            if t < TT - 1:
                st = hd(self.state[:, :])
                if t:
                    dve.tensor_tensor(st, st, per_head(s["etot"], t, SHD), ALU.mult)\
                       .then_inc(self.sem("aged"), 1)
                    dve.wait_ge(self.sem("aged"), t)
                dve.wait_ge(self.sem("states"), t + 1)
                if t:
                    dve.tensor_tensor(st, st, bank(6), ALU.add).then_inc(self.sem("state"), 1)
                else:
                    dve.tensor_copy(st, bank(6)).then_inc(self.sem("state"), 1)
            dve.wait_ge(self.sem("within"), t + 1)
            if t:
                dve.wait_ge(self.sem("off"), t)
                dve.tensor_tensor(y, y, bank(4), ALU.add).then_inc(self.sem("within_read"), 1)
            else:
                dve.tensor_copy(y, bank(4)).then_inc(self.sem("within_read"), 1)
            dve.tensor_tensor(xdt, x, s["D"].unsqueeze(2).broadcast_to([P, SH, SHD]), ALU.mult)\
               .then_inc(local, 1)
            n += 1
            dve.wait_ge(local, n)
            dve.wait_ge(self.sem("within_read"), t + 1)
            dve.tensor_tensor(y, y, xdt, ALU.add).then_inc(local, 1)
            n += 1
            dve.wait_ge(local, n)
            z = self.sz[:, t * D:(t + 1) * D]
            dve.tensor_tensor(z, z, self.y[:, :], ALU.mult).then_inc(self.sem("gated"), 1)
        dve.wait_ge(self.sem("root"), 1)
        dve.reciprocal(k.stat[:, 8:12], k.stat[:, 4:8]).then_inc(local, 1)
        dve.wait_ge(local, n + 1)
        for t in range(TT):
            z = self.sz[:, t * D:(t + 1) * D]
            dve.tensor_scalar(z, z, k.stat[:, 8 + t:9 + t], None, ALU.mult).then_inc(self.sem("normed"), 1)

    def act(self, act):
        k = self.k
        self.join(act)
        for t in range(TT):
            self.side_out("act", act, 4 * t, self.STEPS)
            for g in range(SG):
                e = self.e[:, g * D:(g + 1) * D]
                act.wait_ge(self.sem("min"), SG * t + g + 1)
                act.activation(e, e, ACT.Exp).then_inc(self.sem("exp"), 1)
            self.side_out("act", act, 4 * t + 3, self.STEPS)
            act.wait_ge(self.sem("gated"), t + 1)
            act.activation(self.y[:, :], self.sz[:, t * D:(t + 1) * D], ACT.Square,
                           accum_out=k.stat[:, t:t + 1]).then_inc(self.sem("square"), 1)
        act.wait_ge(self.sem("square"), TT)
        act.activation(k.stat[:, 4:8], k.stat[:, 0:4], ACT.Sqrt, bias=k.eps[:, 0:1], scale=1.0 / D)\
           .then_inc(self.sem("root"), 1)


class SsdOut(Stage):

    def __init__(self, k, name, prev, y, wcol, yhi, ylo):
        super().__init__(k, name, prev)
        self.y, self.wcol, self.yhi, self.ylo = y, wcol, yhi, ylo
        self.ends = [(self.sem("lo"), KD)]

    def pe(self, pe):
        k = self.k
        self.join(pe)
        for c in range(KD):
            if c >= 4:
                pe.wait_ge(self.sem("lo"), c - 3)
            for t in range(TT):
                tr = pe.transpose(k.ps[:, 4 + c % 4, t * P:(t + 1) * P], self.y[:, t * D + c * P:t * D + (c + 1) * P],
                                  k.const(C_ID))
            tr.then_inc(self.sem("turned"), 1)

    def act(self, act):
        k = self.k
        self.join(act)
        for c in range(KD):
            act.wait_ge(self.sem("turned"), c + 1)
            act.activation(self.yhi[:, c * T:(c + 1) * T], k.ps[:, 4 + c % 4, :], ACT.Copy,
                           scale=k.col(self.wcol + c)).then_inc(self.sem("hi"), 1)

    def dve(self, dve):
        k = self.k
        self.join(dve)
        for c in range(KD):
            dve.wait_ge(self.sem("hi"), c + 1)
            dve.scalar_tensor_tensor(self.ylo[:, c * T:(c + 1) * T], k.ps[:, 4 + c % 4, :], k.col(self.wcol + c),
                                     self.yhi[:, c * T:(c + 1) * T], ALU.mult, ALU.subtract)\
               .then_inc(self.sem("lo"), 1)


class PoolMix(Stage):

    def __init__(self, k, name, prev, u, a, b, pooled, wsrc, w, scol, yhi, ylo):
        super().__init__(k, name, prev)
        self.u, self.ab, self.pooled, self.wsrc, self.w = u, (a, b), pooled, wsrc, w
        self.scol, self.yhi, self.ylo = scol, yhi, ylo
        self.ends = [(self.sem("lo"), len(WINDOWS))]

    def pe(self, pe):
        k = self.k
        self.join(pe)
        self.side_pe(pe, 0, 5)
        for g in range(len(WINDOWS)):
            pe.wait_ge(self.sem("pooled"), g + 1)
            if g == 0:
                pe.wait_ge(self.sem("weights"), 16)
            pe.matmul(k.ps[:, 4 + g, :], self.w[:, g * P:(g + 1) * P], self.pooled[:, g * T:(g + 1) * T],
                      start=True, stop=True).then_inc(self.sem("mixed"), 1)
            self.side_pe(pe, g + 1, 5)

    def act(self, act):
        k = self.k
        self.join(act)
        act.dma_start(self.w[:, :].rearrange("p (g d) -> p g d", d=P), self.wsrc).then_inc(self.sem("weights"), 16)
        for g in range(len(WINDOWS)):
            self.side_out("act", act, g + 1, 5)
            act.wait_ge(self.sem("mixed"), g + 1)
            act.activation(self.yhi[:, g * T:(g + 1) * T], k.ps[:, 4 + g, :], ACT.Copy,
                           scale=k.col(self.scol + g)).then_inc(self.sem("hi"), 1)

    def dve(self, dve):
        k = self.k
        self.join(dve)
        step = self.sem("step")
        n, pad = 0, 16
        for g, win in enumerate(WINDOWS):
            tile = self.u[:, g * (T + pad):(g + 1) * (T + pad)]
            src, shift, side = tile, 1, 0
            self.side_out("dve", dve, g + 1, 5)
            if g:
                dve.wait_ge(self.sem("pooled"), g)
            while shift < win:
                dst = self.ab[side][:, :]
                dve.tensor_tensor(dst[:, pad:], src[:, pad:], src[:, pad - shift:T + pad - shift], ALU.add)\
                   .then_inc(step, 1)
                n += 1
                dve.wait_ge(step, n)
                src, shift, side = dst, 2 * shift, 1 - side
            out = self.pooled[:, g * T:(g + 1) * T]
            dve.scalar_tensor_tensor(out, src[:, pad:], 1.0 / win, tile[:, pad:], ALU.mult, ALU.subtract)\
               .then_inc(step, 1)
            head = self.ab[side][:, pad:2 * pad]
            dve.tensor_tensor(head, src[:, pad:2 * pad], k.cst[:, C_CNT + 16 * g:C_CNT + 16 * (g + 1)],
                              ALU.mult).then_inc(step, 1)
            n += 2
            dve.wait_ge(step, n)
            dve.tensor_tensor(out[:, 0:16], head, tile[:, pad:2 * pad], ALU.subtract)\
               .then_inc(self.sem("pooled"), 1)
        for g in range(len(WINDOWS)):
            dve.wait_ge(self.sem("hi"), g + 1)
            dve.scalar_tensor_tensor(self.ylo[:, g * T:(g + 1) * T], k.ps[:, 4 + g, :],
                                     k.col(self.scol + g), self.yhi[:, g * T:(g + 1) * T],
                                     ALU.mult, ALU.subtract).then_inc(self.sem("lo"), 1)


class Dup(Stage):

    def __init__(self, k, name, prev, pairs):
        super().__init__(k, name, prev)
        self.pairs = pairs
        self.ends = [(self.sem("copied"), 16 * len(pairs))]

    def act(self, act):
        self.join(act)
        for dst, src in self.pairs:
            act.dma_start(dst, src).then_inc(self.sem("copied"), 16)


class Select(Stage):

    def __init__(self, k, name, prev, qi, ki, wi, r, sc, m8):
        super().__init__(k, name, prev)
        self.qi, self.ki, self.wi, self.r, self.sc, self.m8 = qi, ki, wi, r, sc, m8
        self.ends = [(self.sem("mask"), TT - 1)]

    DOTS = (TT - 1) * IH
    STEPS = DOTS + TOPK // 8

    def pe(self, pe):
        k = self.k
        self.join(pe)
        for n in range((TT - 1) * IH):
            i, h = n // IH + 1, n % IH
            if n >= 2:
                pe.wait_ge(self.sem("relu"), n - 1)
            r = slice(h % 2 * HD, (h % 2 + 1) * HD)
            pe.matmul(k.ps[:, 4 + n % 2, 0:(i + 1) * P], self.qi[r, h // 2 * T + i * P:h // 2 * T + (i + 1) * P],
                      self.ki[r, 0:(i + 1) * P], start=True, stop=True).then_inc(self.sem("dots"), 1)
            self.side_pe(pe, n, self.STEPS)
        self.side_pe(pe, self.STEPS - 1, self.STEPS)

    def act(self, act):
        k = self.k
        self.join(act)
        for n in range((TT - 1) * IH):
            w = (n // IH + 2) * P
            self.side_out("act", act, n, self.STEPS)
            act.wait_ge(self.sem("dots"), n + 1)
            if n >= 2:
                act.wait_ge(self.sem("score"), n - 1)
            act.activation(self.r[:, n % 2 * T:n % 2 * T + w], k.ps[:, 4 + n % 2, 0:w], ACT.Relu)\
               .then_inc(self.sem("relu"), 1)
        self.side_out("act", act, self.STEPS, self.STEPS)

    def score(self, i):
        return self.sc[:, (i - 1) * T:(i - 1) * T + (i + 1) * P]

    def dve(self, dve):
        k = self.k
        self.join(dve)
        for n in range((TT - 1) * IH):
            i, h = n // IH + 1, n % IH
            w = (i + 1) * P
            self.side_out("dve", dve, n, self.STEPS)
            sc, r = self.score(i), self.r[:, n % 2 * T:n % 2 * T + w]
            wi = self.wi[:, i * IH + h:i * IH + h + 1]
            dve.wait_ge(self.sem("relu"), n + 1)
            if h:
                dve.wait_ge(self.sem("score"), n)
                dve.scalar_tensor_tensor(sc, r, wi, sc, ALU.mult, ALU.add).then_inc(self.sem("score"), 1)
            else:
                dve.tensor_scalar(sc, r, wi, None, ALU.mult).then_inc(self.sem("score"), 1)
        dve.wait_ge(self.sem("score"), (TT - 1) * IH)
        for i in range(1, TT):
            d = self.score(i)[:, i * P:(i + 1) * P]
            dve.tensor_tensor(d, d, k.const(C_QK), ALU.subtract).then_inc(self.sem("causal"), 1)
        dve.wait_ge(self.sem("causal"), TT - 1)

        def largest(i):
            dve.max(self.m8[:, 8 * i:8 * i + 8], self.score(i)).then_inc(self.sem("largest"), 1)

        def take(i, value):
            dve.wait_ge(self.sem("largest"), value)
            dve.match_replace(self.score(i), self.m8[:, 8 * i:8 * i + 8], self.score(i), TAKEN)\
               .then_inc(self.sem("taken"), 1)
        for i in range(1, TT):
            largest(i)
        for i in range(1, TT):
            take(i, i)
        for r in range(1, TOPK // 8):
            self.side_out("dve", dve, self.DOTS + r, self.STEPS)
            for i in range(1, TT):
                dve.wait_ge(self.sem("taken"), (TT - 1) * (r - 1) + i)
                largest(i)
            for i in range(1, TT):
                take(i, (TT - 1) * r + i)
        dve.wait_ge(self.sem("taken"), (TT - 1) * (TOPK // 8))
        for i in range(1, TT):
            dve.tensor_scalar(self.score(i), self.score(i), TAKEN / 1.5, BIG, ALU.is_gt, ALU.mult)\
               .then_inc(self.sem("mask"), 1)


class Store(Stage):

    def __init__(self, k, name, prev, norm, out):
        super().__init__(k, name, prev)
        self.norm, self.out = norm, out
        self.y = k.at("store_y", 0, TT * D)

    def pe(self, pe):
        k = self.k
        for c in range(KD):
            pe.wait_ge(self.norm.ready, c + 1)
            for t in range(TT if c < 4 else TT - 1):
                self.turn(pe, t, c)
        for c in range(4, KD):
            self.turn(pe, TT - 1, c)

    def turn(self, pe, t, c):
        k = self.k
        tr = pe.transpose(k.ps[:, 2 * t + c // 4, c % 4 * P:(c % 4 + 1) * P],
                          k.xT[:, c * T + t * P:c * T + (t + 1) * P], k.const(C_ID))
        if c % 4 == 3:
            tr.then_inc(self.sem("turned"), 1)

    def half(self, t, b):
        return self.y[:, t * D + b * 512:t * D + (b + 1) * 512]

    def act(self, act):
        self.join(act)
        for t in range(TT):
            act.wait_ge(self.sem("turned"), t + 1)
            act.activation(self.half(t, 0), self.k.ps[:, 2 * t, :], ACT.Copy).then_inc(self.sem("low"), 1)

    def dve(self, dve):
        self.join(dve)
        for t in range(TT):
            dve.wait_ge(self.sem("turned"), TT + t + 1)
            dve.tensor_copy(self.half(t, 1), self.k.ps[:, 2 * t + 1, :]).then_inc(self.sem("high"), 1)

    def sp(self, sp):
        for t in range(TT):
            sp.wait_ge(self.sem("low"), t + 1)
            sp.wait_ge(self.sem("high"), t + 1)
            sp.dma_start(self.out[0, t * P:(t + 1) * P, :], self.y[:, t * D:(t + 1) * D])\
              .then_inc(self.sem("stored"), 16)
        sp.wait_ge(self.sem("stored"), 16 * TT)



def weight(w, l, r0, rows, c0, cols):
    v = w[bass.ds(l, 1), r0:r0 + rows, bass.ds(c0, cols)] if isinstance(r0, int) else \
        w[bass.ds(l, 1), bass.ds(r0, rows), bass.ds(c0, cols)]
    return v.rearrange("l (k p) n -> p (l k) n", p=P)


def rows_of(w, l, a, n):
    return w[bass.ds(l, 1), a:a + n * P].rearrange("l (a p) -> (l a) p", p=P)


def emit(k, stages, hand_on=True):
    nc = k.nc
    with nc.Block(no_gpsimd_drain=True) as block:
        @block.sync
        def _(sp):
            for s in stages:
                s.sp(sp)
            if hand_on:
                sp.wait_ge(k.split, k.units - k.ready)

        @block.scalar
        def _(act):
            for s in stages:
                s.act(act)

        @block.vector
        def _(dve):
            for s in stages:
                s.dve(dve)

        @block.tensor
        def _(pe):
            for s in stages:
                s.pe(pe)

        @block.gpsimd
        def _(pool):
            lo_units(k, pool, k.units - k.ready)


BESIDE1 = {"rope": 11, "att": 38, "conv": 15, "forget": 5, "gates": 7, "mlstm": 42}
BESIDE2 = {"conv": 18, "dt": 5, "prep": 9, "ssd": 38, "select": 50, "att": 24, "pool": 12}


NPC = 104
NMIX, CW, CB, MN, NMLP, B1, B2 = 0, 8, 40, 48, 52, 60, 88
S_FIN1, S_N1, S_CW, S_CB, S_SN, S_PS, S_N2, S_FIN2 = 0, 8, 16, 64, 76, 84, 88, 96


def first_steps(k, A, table):
    setup = Setup(k, "setup", [], A["x"], table)
    angles = Angles(k, "angles", [], A["positions"], setup.sem("table"))
    stats = Stats(k, "stats_first", [], setup.tile, emitted=True)
    preload = Preload(k, "preload", [], [weight(A["w_in"], 0, 0, D, AQ + j * UC, UC) for j in range(2)], stats)
    sets = []
    for l in range(DEPTH + 1):
        if l < DEPTH:
            rows = [(rows_of(A["norm_mix_w"], l, 0, 8), NMIX, 8),
                    (A["conv_w"][l].rearrange("j (a p) -> (j a) p", p=P), CW, 32),
                    (rows_of(A["conv_b"], l, 0, 8), CB, 8), (rows_of(A["mlstm_norm_w"], l, 0, 4), MN, 4),
                    (rows_of(A["norm_mlp_w"], l, 0, 8), NMLP, 8), (rows_of(A["b_in"], l, 0, 28), B1, 28),
                    (rows_of(A["b_in"], l, GA, 16), B2, 16)]
        else:
            rows = [(A["final_norm_w"].rearrange("(a p) -> a p", p=P), S_FIN1, 8),
                    (rows_of(A["norm1_w_2"], 0, 0, 8), S_N1, 8),
                    (A["conv_w_2"][0].rearrange("j (a p) -> (j a) p", p=P), S_CW, 48),
                    (rows_of(A["conv_b_2"], 0, 0, 12), S_CB, 12), (rows_of(A["ssd_norm_w_2"], 0, 0, 8), S_SN, 8),
                    (rows_of(A["pool_scale_2"], 0, 0, 4), S_PS, 4), (rows_of(A["norm2_w_2"], 0, 0, 8), S_N2, 8),
                    (A["final_norm_w_2"].rearrange("(a p) -> a p", p=P), S_FIN2, 8)]
        sets.append((rows, k.pall[:, l * NPC:(l + 1) * NPC]))
    params = Params(k, "all_params", setup.tile(7), sets, TT * D + 5 * T)
    stats.prev = [params]
    return [setup, angles, preload, params, stats, Rotary(k, "rotary", [angles], angles)]


def first_layer(k, l, A):
    k.stream_sems("first", 2)
    st = []

    def add(cls, name, *a, prev=None, **kw):
        st.append(cls(k, name, st[-1:] if prev is None else prev, *a, **kw))
        return st[-1]
    o_qk, o_v = 0, 4096
    o_mv = o_v + 2048
    o_mo = o_mv + TT * MH * (MD + 1)
    o_cv = o_mo + 2048
    o_ya = up8(o_cv + 8 * (T + CONV - 1))
    o_scr = o_ya + 4096
    o_vb = o_scr + 6144
    qk = k.at("qk", o_qk, 8 * T)
    v = k.at("v", o_v, TT * 512)
    mv = k.at("mv", o_mv, TT * MH * (MD + 1))
    mo = k.at("mo", o_mo, 4 * T)
    cv = k.at("conv_in", o_cv, 8 * (T + CONV - 1))
    mqk = k.at("conv_out", o_qk, 8 * T)
    vb = k.at("token_bias", o_vb, 1032)
    k.tmp = k.at("softplus_tmp", o_scr, 512)
    k.gr = k.at("gate_rows", o_scr + Mlstm.H_AT, 4 * T)
    ya = [k.at(f"ya_{p}", o_ya + i * 2048, 2048, F32R) for i, p in enumerate(("hi", "lo"))]
    yb = [k.at(f"yb_{p}", o_qk + i * 2048, 2048, F32R) for i, p in enumerate(("hi", "lo"))]
    params = add(Columns, "params", k.pall[:, bass.ds(l * NPC, NPC)], (B1 + 24, 20),
                 [(vb[:, a:a + n], A["b_in"][bass.ds(l, 1), c:c + n].broadcast_to([P, n]))
                  for a, c, n in ((0, AV, 512), (512, MV, 512), (1024, MI, 8))])
    norm = add(Norm, "norm_mix", NMIX)
    cv3 = cv[:, :].rearrange("p (t w) -> p t w", w=T + CONV - 1)
    fill = add(Fill, "fill", [(mv[:, :], 1.0), (cv3[:, :, 0:CONV - 1], 0.0)], params.spread)
    w_in = A["w_in"]

    def src(c0):
        return lambda j, i: weight(w_in, l, 0, D, i * (2 * UC) + (c0 + j * UC), UC)

    def fm_out(dst, w, pad, bcol, func):
        def evac(act, j, i, bank):
            for c in range(UT):
                ins = act.activation(dst[:, bass.ds(i * (4 * w) + (2 * j + c) * w + pad, T)], k.ps[:, bank + c, :],
                                     func, bias=k.pcol[:, bass.ds(i * 4 + bcol + 2 * j + c, 1)])
            return ins
        return evac

    def v_out(dve, j, i, bank):
        return dve.tensor_tensor(
            v[:, :].rearrange("p (t f) -> p t f", t=TT)[:, :, j * UC:(j + 1) * UC],
            k.ps[:, bank:bank + 2, :].rearrange("p b (t f) -> p (b t) f", t=2),
            vb[:, j * UC:(j + 1) * UC].unsqueeze(1).broadcast_to([P, TT, UC]), ALU.add)
    proj = add(Project, "proj", norm, [
        Seg("fm", 4, src(AQ), UC, fm_out(qk, T, 0, B1, ACT.Identity), loop=True),
        Seg("tm", 2, src(AV), UC, v_out, eng="dve")], prev=[fill])

    g, merged = k.at("gate", o_scr + Mlstm.SCRATCH, 4 * T), k.at("merged", o_cv, 8 * T)
    side = add(Branches, "side", g, merged)

    def plain(c0, cols, jobs):
        return side.unit(weight(w_in, l, 0, D, c0, cols), KD, cols, k.hh, k.hl, jobs)

    def conv_in(t):
        a = t * (T + CONV - 1) + CONV - 1
        return Job("act", lambda act, bank: act.activation(
            cv[:, a:a + T], k.ps[:, bank, :], ACT.Identity, bias=k.col(B1 + 12 + t)), c=t % UT)

    def values(j, half):
        def evac(dve, bank):
            dst = mv[:, :].rearrange("p (t h d) -> p t h d", h=MH, d=MD + 1)[:, 2 * half:2 * half + 2,
                                                                             2 * j:2 * j + 2, 0:MD]
            bias = vb[:, 512 + j * UC:512 + (j + 1) * UC].rearrange("p (h d) -> p h d", d=MD)
            src = k.ps[:, bank, :].rearrange("p (t h d) -> p t h d", t=2, h=2)
            for t in range(2):
                ins = dve.tensor_tensor(dst[:, t], src[:, t], bias, ALU.add)
            return ins
        return Job("dve", evac, tm=(2 * half, 2 * half + 2, 0, UC, UC))

    def out_gate(t):
        return Job("act", lambda act, bank: act.activation(
            mo[:, t * T:(t + 1) * T], k.ps[:, bank, :], ACT.Tanh, scale=0.5, bias=k.hbias[:, t:t + 1]), c=t % UT)
    g8 = k.small[:, 0:32]

    grows = k.at("input_forget_rows", o_mo + 3 * T, T)

    def gate_out(dve, cols):
        return dve.tensor_tensor(
            g8.rearrange("p (t f) -> p t f", f=8), cols.rearrange("p (t f) -> p t f", f=8),
            vb[:, 1024:1032].unsqueeze(1).broadcast_to([P, TT, 8]), ALU.add)
    for j in range(4):
        plain(MQ + j * UC, UC, [conv_in(2 * j), conv_in(2 * j + 1)])
    gates_at = plain(MI, 8, [Job("act", lambda act, bank: act.activation(
        grows[0:8, :], k.ps[0:8, bank, :], ACT.Copy), c=0, rows=8)])
    for j in range(2):
        values_at = plain(MV + j * UC, UC, [values(j, 0), values(j, 1)])
    for j in range(2):
        plain(MO + j * UC, UC, [out_gate(2 * j), out_gate(2 * j + 1)])
    mo_ready = side.ends_at()

    t1, t2 = k.at("rope_cos", o_scr, 2 * T), k.at("rope_sin", o_scr + 2 * T, 2 * T)
    at = 0
    rope = add(Rope, "rope", qk, t1, t2, prev=[proj])
    at = rope.beside(side, at, BESIDE1["rope"])

    def head(x, t0):
        return lambda h: x[h % 2 * HD:(h % 2 + 1) * HD, (t0 + h // 2) * T:(t0 + h // 2 + 1) * T]
    att = add(Attention, "att", head(qk, 0), head(qk, 4), lambda b, h: v[:, b * 512 + h * HD:b * 512 + (h + 1) * HD],
              lambda i: k.cst[:, C_PAT + (TT - 1 - i) * P:C_PAT + TT * P], o_scr, o_mo, *ya)
    at = att.beside(side, at, BESIDE1["att"])

    def tiles(x):
        return lambda i: x[:, i * T:(i + 1) * T]

    add(Rest, "to_conv", side, gates_at)
    add(Turn, "turn_gates", grows, 0, 8, gate_out)
    conv = add(Conv, "conv", cv, mqk, 8, CW, CB)
    at = conv.beside(side, max(at, gates_at), BESIDE1["conv"])
    spf = k.small[:, 32:48]
    forget = add(Softplus, "forget", None, spf, 16, lambda dve, x2: dve.tensor_scalar(
        x2.rearrange("p (t f) -> p t f", f=MH), g8.rearrange("p (t f) -> p t f", f=8)[:, :, MH:2 * MH],
        -1.0, None, ALU.mult))
    at = forget.beside(side, at, BESIDE1["forget"])
    gates = add(Gates, "gates", spf, g8)
    at = gates.beside(side, at, BESIDE1["gates"])
    rest = add(Rest, "to_mlstm", side, values_at)
    mlstm = add(Mlstm, "mlstm", mqk, mv, mo, mo_ready, o_scr, o_v, *yb, MN)
    at = mlstm.beside(side, at, BESIDE1["mlstm"])

    for n, (b0, gcol, w, y, need) in enumerate(((4, GA, "w_proj_att", ya, att), (12, GB, "w_proj_mlstm", yb, mlstm))):
        for half in range(2):
            side.gate(lambda c, gcol=gcol: weight(w_in, l, 0, D, gcol + c, UC), half,
                      bias=lambda t, b0=b0: k.hbias[:, b0 + t:b0 + t + 1], free=att.ends)
            side.up(lambda c, cols, w=w: weight(A[w], l, 0, 512, c, cols), 4, (tiles(y[0]), tiles(y[1])), half,
                    n > 0, need=need.ends if half == 0 else (), free=conv.ends)
    mix = [k.at(f"mixed_{p}", at, 4096, F32R) for at, p in ((o_ya, "hi"), (o_v, "lo"))]
    add(Rest, "branches", side, side.final[3].end)
    part = add(Split, "split_mixed", merged, *mix, 4, lambda t: side.read(side.final[t]))
    add(Rest, "last_turn", side)
    split = add(Split, "split_mixed2", merged, *mix, 8, lambda t: side.read(side.final[t]), part)
    proj = add(OutProj, "out", lambda c, n: weight(A["w_out"], l, 0, D, c, n), split, tiles(mix[0]), tiles(mix[1]),
               side.ends_at())
    proj.stats = add(Stats, "stats_mlp", proj.tile, emitted=True, bank=proj.BANK)
    norm = add(Norm, "norm_mlp", NMLP)
    f = [k.at(f"ff_{p}", i * 8192, 8192, F32R) for i, p in enumerate(("hi", "lo"))]
    scr = [k.at(f"ff_{p}", 16384 + i * 2048, 2048) for i, p in enumerate(("relu", "square"))]
    before = norm
    assert k.units + 4 * 8 + 1 & 1 == 0
    following = [weight(w_in, l * -1 + (DEPTH - 1), 0, D, AQ + j * UC, UC) for j in (1, 0)]
    for half in range(2):
        up = add(Up, f"up{half}", before, lambda j, i, half=half: weight(
            A["w_ff1"], l, 0, D, i * UC + (half * DFF // 2 + j * UC), UC), 8, *f, scr)
        before = add(Down, f"down{half}", up, lambda j, i, half=half: weight(
            A["w_ff2"], l, i * 256 + (half * DFF // 2 + j * 256), 256, 0, D), 8, *f, last=half == 1, following=following if half == 1 else ())
    before.stats = add(Stats, "stats_next", before.tile, emitted=True)
    return st


def second_layer(k, A, out):
    k.stream_sems("second")
    st = []
    l = 0

    def add(cls, name, *a, prev=None, **kw):
        st.append(cls(k, "s_" + name, st[-1:] if prev is None else prev, *a, **kw))
        return st[-1]
    W = T + CONV - 1
    o_sz = up8(12 * W)
    o_c = o_sz + 4096
    o_scr = o_c + 12 * T
    o_small = o_scr + 6 * D + 1024
    o_rows = o_small + 1088
    xbc = k.at("s_conv_in", 0, 12 * W)
    xs, bt = k.at("s_x_tm", 0, 4096), k.at("s_b_tm", 4096, 1024)
    sz = k.at("s_silu_z", o_sz, 4096)
    c = k.at("s_conv_out", o_c, 12 * T)
    cb = k.at("s_cb", o_scr + 6 * D, 1024)
    k.tmp = k.at("s_softplus_tmp", o_scr, 512)
    rows = k.at("s_rows", o_rows, 2 * T)
    sm = k.at("s_small", o_small, 1088)
    s, at = {}, 0
    for n, w in (("dt_raw", 64), ("dt", 64), ("a", 64), ("loc", 64), ("tot", 64), ("eloc", 64), ("etot", 64),
                 ("dec", 64), ("dtdec", 64)):
        s[n] = sm[:, at:at + w]
        at += w
    per_head = k.stat[:, 32:96]
    for i, n in enumerate(("a_log", "A", "D", "dt_bias")):
        s[n] = per_head[:, i * SH:(i + 1) * SH]
    params = add(Columns, "params", None, None, [
        (s[n], A[x][0:1, :].broadcast_to([P, SH]))
        for n, x in (("dt_bias", "dt_bias_2"), ("a_log", "a_log_2"), ("D", "d_skip_2"))])
    norm = add(Norm, "norm_first", S_FIN1, final=True)
    stats = Stats(k, "s_stats1", [norm], lambda t, norm=norm: (norm.ready, t + 1), emitted=True)
    add(Lead, "lead", stats)
    st.append(stats)
    norm = add(Norm, "norm1", S_N1)
    xbc3 = xbc[:, :].rearrange("p (t w) -> p t w", w=W)
    fill = add(Fill, "fill", [(xbc3[:, :, 0:CONV - 1], 0.0)], params.spread)
    w_in = A["w_in_2"]

    def src(c0):
        return lambda j, i: weight(w_in, l, 0, D, i * (2 * UC) + (c0 + j * UC), UC)

    def pair(bank):
        return k.ps[:, bank:bank + 2, :]

    def fm_out(dst, w, pad, scale=1.0):
        def evac(act, j, i, bank):
            return act.activation(
                dst[:, bass.ds(i * (4 * w) + 2 * j * w, 2 * w)].rearrange("p (c w) -> p c w", c=2)[:, :, pad:pad + T],
                pair(bank), ACT.Copy, scale=scale)
        return evac

    proj = add(Project, "proj_ssd", norm, [Seg("fm", 6, src(XBC2), UC, fm_out(xbc, W, CONV - 1), loop=True)],
               prev=[fill])

    q = k.at("s_q", o_c, 4 * T)
    kd = [k.at(f"s_k{i}", o_c + (4 + i) * T, T) for i in range(2)]
    qi = k.at("s_qi", o_c + 6 * T, 2 * T)
    v, ki = k.at("s_v", 10 * T, TT * P), k.at("s_ki", 11 * T, T)
    ys = [k.at(f"ys_{p}", o_scr + i * 4096, 4096, F32R) for i, p in enumerate(("hi", "lo"))]
    g, merged = k.at("s_gate", o_c + 8 * T, 4 * T), k.at("s_merged", 0, 8 * T)
    r, sc = k.at("s_relu", o_sz, 2 * T), k.at("s_scores", o_sz + 5 * T, 3 * T)
    yahi, yalo = k.at("s_ya_hi", o_sz, 4 * T, F32R), k.at("s_ya_lo", o_c, 4 * T, F32R)
    pad = 16
    u = k.at("s_u", o_scr + 14 * T, 4 * (T + pad))
    yp = [k.at(f"s_yp_{p}", o_scr + i * 2048, 2048, F32R) for i, p in enumerate(("hi", "lo"))]
    pooled, pw = k.at("s_pooled", o_scr + 8 * T, 4 * T), k.at("s_pool_w", o_scr + 12 * T, 4 * P)
    ab = [k.at(f"s_window{i}", o_sz + 5 * T + i * (T + pad), T + pad) for i in range(2)]
    wi, m8 = k.small[:, 0:16], k.small[:, 16:48]

    side = add(Branches, "side", g, merged)

    def plain(c0, cols, jobs):
        return side.unit(weight(w_in, l, 0, D, c0, cols), KD, cols, k.hh, k.hl, jobs)

    def silu_z(j, half):
        return Job("act", lambda act, bank: act.activation(
            sz[:, :].rearrange("p (t f) -> p t f", t=TT)[:, 2 * half:2 * half + 2, j * UC:(j + 1) * UC],
            k.ps[:, bank, :].rearrange("p (t f) -> p t f", t=2), ACT.Silu), tm=(2 * half, 2 * half + 2, 0, UC, UC))

    def copy(dst, c, scale=1.0):
        return Job("act", lambda act, bank: act.activation(dst, k.ps[:, bank, :], ACT.Copy, scale=scale), c=c)

    def k_out(act, bank):
        act.activation(kd[0][0:HD, :], k.ps[0:HD, bank, :], ACT.Copy)
        return act.activation(kd[1][HD:P, :], k.ps[HD:P, bank, :], ACT.Copy)

    def keys_out(act, bank):
        act.activation(kd[0][HD:HD + IH, :], k.ps[HD:HD + IH, bank, :], ACT.Copy, scale=IH ** -0.5 * HD ** -0.5)
        return act.activation(ki[0:HD, :], k.ps[0:HD, bank, :], ACT.Copy)

    def dt_out(dve, cols):
        return dve.tensor_tensor(
            s["dt_raw"].rearrange("p (t f) -> p t f", f=SH), cols.rearrange("p (t f) -> p t f", f=SH),
            s["dt_bias"].unsqueeze(1).broadcast_to([P, TT, SH]), ALU.add)
    dt_rows = k.at("s_dt_rows", o_scr + T, T)
    dt_at = plain(DT2, SH, [Job("act", lambda act, bank: act.activation(
        dt_rows[0:SH, :], k.ps[0:SH, bank, :], ACT.Copy), c=0, rows=SH)])
    for j in range(4):
        z_at = plain(Z2 + j * UC, UC, [silu_z(j, 0), silu_z(j, 1)])
    for j in range(2):
        plain(Q2 + j * UC, UC, [copy(q[:, t * T:(t + 1) * T], t % 2, -HD ** -0.5) for t in (2 * j, 2 * j + 1)])
    plain(K2, UC, [Job("act", k_out, c=0), Job("act", lambda act, bank: act.activation(
        v[:, :], k.ps[:, bank, :], ACT.Copy), tm=(0, TT, P, P, P))])
    plain(QI2, UC, [copy(qi[:, t * T:(t + 1) * T], t) for t in range(2)])
    keys_at = plain(KI2, P, [Job("act", keys_out, c=0)])

    conv = add(Conv, "conv", xbc, c, 12, S_CW, S_CB, prev=side.prev)
    at = conv.beside(side, 0, BESIDE2["conv"])
    add(Rest, "to_dt", side, dt_at)
    add(Turn, "turn_dt", dt_rows, 0, SH, dt_out)
    dt = add(Softplus, "dt", None, s["dt"], 64, lambda dve, x2: dve.tensor_copy(x2, s["dt_raw"]))
    at = dt.beside(side, at, BESIDE2["dt"])
    prep = add(SsdPrep, "prep", c, xs, bt, cb, rows, s)
    at = prep.beside(side, at, BESIDE2["prep"])
    assert at <= z_at
    add(Rest, "to_ssd", side, z_at)
    ssd = add(Ssd, "ssd", c, xs, bt, cb, rows, s, sz, o_scr)
    at = ssd.beside(side, z_at, BESIDE2["ssd"])
    assert at <= keys_at
    rest = add(Rest, "to_select", side, keys_at)
    turn = add(Turn, "turn_wi", kd[0], HD, IH, lambda dve, cols: dve.tensor_copy(wi, cols))
    dup = add(Dup, "dup", [(kd[0][HD:P, :], kd[0][0:HD, :]), (kd[1][0:HD, :], kd[1][HD:P, :]),
                           (ki[HD:P, :], ki[0:HD, :])])
    ssd_out = add(SsdOut, "ssd_out", sz, S_SN, *ys, prev=[turn])

    def tiles(x):
        return lambda i: x[:, i * T:(i + 1) * T]

    def branch(b, w, kt, y, need):
        for half in range(2):
            gate(b, half)
            at = up(b, w, kt, y, half, need)
        return at

    def gate(b, half):
        side.gate(lambda c: weight(w_in, l, 0, D, G2 + b * D + c, UC), half, free=ssd_out.ends)

    def up(b, w, kt, y, half, need):
        return side.up(lambda c, n: weight(A[w], l, 0, kt * P, c, n), kt, (tiles(y[0]), tiles(y[1])), half, b > 0,
                       need=need.ends if half == 0 else (), free=ssd_out.ends)
    ssd_at = branch(0, "w_up_ssd_2", KD, ys, ssd_out)
    u3 = u[:, :].rearrange("p (t w) -> p t w", w=T + pad)
    for j in range(2):
        u_at = plain(U2 + j * UC, UC, [copy(u3[:, t, pad:], t % 2) for t in (2 * j, 2 * j + 1)])

    sel = add(Select, "select", qi, ki, wi, r, sc, m8, prev=[dup, ssd_out])
    at = keys_at
    at = sel.beside(side, at, BESIDE2["select"])
    assert at <= ssd_at
    add(Rest, "to_att", side, ssd_at)
    add(Fill, "fill_u", [(u3[:, :, 0:pad], 0.0)])
    att = add(Attention, "att", lambda h: q[h % 2 * HD:(h % 2 + 1) * HD, h // 2 * T:(h // 2 + 1) * T],
              lambda h: kd[h // 4][h % 2 * HD:(h % 2 + 1) * HD, :],
              lambda b, h: v[:, b * P + h // 4 * HD:b * P + (h // 4 + 1) * HD],
              lambda i: sel.score(i) if i else k.const(C_QK), o_scr, o_scr + 12 * T, yahi, yalo)
    at = att.beside(side, ssd_at, BESIDE2["att"])
    branch(1, "w_up_attn_2", 4, (yahi, yalo), att)
    add(Rest, "to_pool", side, u_at)
    add(Fill, "fill_windows", [(ab[0][:, 0:pad], 0.0), (ab[1][:, 0:pad], 0.0)])
    pool = add(PoolMix, "pool", u, *ab, pooled, A["pool_w_2"][0].rearrange("g c d -> c g d"), pw, S_PS, *yp)
    at = pool.beside(side, max(at, u_at), BESIDE2["pool"])
    branch(2, "w_up_pool_2", 4, yp, pool)
    mix = [k.at(f"s_mixed_{p}", 4096 + i * 4096, 4096, F32R) for i, p in enumerate(("hi", "lo"))]
    add(Rest, "branches", side, side.final[3].end)
    part = add(Split, "split_mixed", merged, *mix, 4, lambda t: side.read(side.final[t]))
    add(Rest, "last_turn", side)
    split = add(Split, "split_mixed2", merged, *mix, 8, lambda t: side.read(side.final[t]), part)
    proj = add(OutProj, "out", lambda c, n: weight(A["w_out_2"], l, 0, D, c, n), split, tiles(mix[0]), tiles(mix[1]),
               side.ends_at())
    proj.stats = add(Stats, "stats2", proj.tile, emitted=True, bank=proj.BANK)
    norm = add(Norm, "norm2", S_N2)
    f = [k.at(f"s_ff_{p}", i * 11264, 11264, F32R) for i, p in enumerate(("hi", "lo"))]
    scr = [k.at(f"s_ff_{p}", 22528 + i * 1024, 1024) for i, p in enumerate(("silu", "product"))]
    up = add(Glu, "up", norm, lambda j, i: weight(A["w_ffn_in_2"], l, 0, D, i * UC + j * FF2, UC), FF2 // UC, *f, scr)
    down = add(Down, "down", up, lambda j, i: weight(A["w_ffn_out_2"], l, i * 256 + j * 256, 256, 0, D), 11, *f,
               last=True)
    down.stats = add(Stats, "stats_last", down.tile, emitted=True)
    norm = add(Norm, "norm_last", S_FIN2, final=True)
    add(Store, "store", norm, out)
    return st


def program(nc, A, table, out):
    with ExitStack() as ctx:
        k = Kern(nc, ctx)
        k.xT = k.keep("xT", KD * T)
        k.hhi, k.hlo = k.keep("h_hi", KD * T, F32R), k.keep("h_lo", KD * T, F32R)
        k.wraw = k.keep("w_raw", 2 * SLOT)
        k.whi, k.wlo = k.keep("w_hi", 2 * SLOT, F32R), k.keep("w_lo", 2 * SLOT, F32R)
        k.cst = k.keep("constants", C_END)
        k.cos, k.sin = k.keep("cos", T), k.keep("sin", T)
        k.pall = k.keep("all_param_cols", (DEPTH + 1) * NPC)
        k.pcol = k.keep("param_cols", NPC)
        k.stat = k.keep("stat", 96)
        k.acol = k.keep("gate_cols", 32)
        k.hbias = k.keep("half_bias", 24)
        k.small = k.keep("small", 48)
        k.eps = k.keep("eps", 8)
        k.root = k.keep("root", 8)
        k.arena = k.top
        k.arena_words = (nc.sbuf_usable_end() - k.arena) // 4 if callable(nc.sbuf_usable_end) else (nc.sbuf_usable_end - k.arena) // 4
        k.ps = ctx.enter_context(nc.psum_tensor("ps", [P, 8, 512], F32))
        k.stream_sems("setup")
        emit(k, first_steps(k, A, table))
        with ExitStack() as k.ctx:
            k.sems = []
            with nc.Fori(0, DEPTH) as l:
                emit(k, first_layer(k, l, A))
                ids = [s.num for s in k.sems]
                assert max(ids) - min(ids) + 1 == len(ids)
                nc.sync.sem_clear(range(min(ids), max(ids) + 1))
                nc.all_engine_barrier()
        with ExitStack() as k.ctx:
            k.pcol = k.pall[:, DEPTH * NPC:(DEPTH + 1) * NPC]
            emit(k, second_layer(k, A, out), hand_on=False)


_INS = ['x', 'positions', 'norm_mix_w', 'w_in', 'b_in', 'conv_w', 'conv_b', 'mlstm_norm_w', 'w_proj_att',
        'w_proj_mlstm', 'w_out', 'norm_mlp_w', 'w_ff1', 'w_ff2', 'final_norm_w', 'norm1_w_2', 'w_in_2',
        'conv_w_2', 'conv_b_2', 'dt_bias_2', 'a_log_2', 'd_skip_2', 'ssd_norm_w_2', 'pool_w_2',
        'pool_scale_2', 'w_up_ssd_2', 'w_up_attn_2', 'w_up_pool_2', 'w_out_2', 'norm2_w_2',
        'w_ffn_in_2', 'w_ffn_out_2', 'final_norm_w_2']


def kernel(**inputs):
    import concourse.bacc as _bacc
    from concourse.bass_utils import run_bass_kernel_spmd as _run

    nc = _bacc.Bacc("TRN2", target_bir_lowering=False, num_devices=1)
    arrays, args = {}, {}
    for name in _INS:
        a = np.ascontiguousarray(inputs[name])
        arrays[f"in_{name}"] = a
        args[name] = nc.dram_tensor(f"in_{name}", a.shape, mybir.dt.from_np(a.dtype), kind="ExternalInput").ap()
    arrays["constants_table"] = constants()
    table = nc.dram_tensor("constants_table", (P, C_END), F32, kind="ExternalInput").ap()
    out = nc.dram_tensor("out_x", (1, T, D), F32, kind="ExternalOutput").ap()
    program(nc, args, table, out)
    r = _run(nc, [arrays], core_ids=[0])
    return r.results[0]["out_x"]
```
